# Optimizing a Trainium2 kernel written in Bass

```python
import jax, jax.numpy as jnp
from jax import lax
import numpy as np

D_MODEL = 1024
BATCH = 1
SEQ = 512
DEPTH = 2

CHUNK = 64
N_META = 16
BLOCK = 128
HEAD_DIM = 64
ROPE_THETA = 10000.0
RMS_EPS = 1e-6
NEG_INF = -1e30
SWA_HEADS = 8
SWA_KV_HEADS = 2
SWA_GROUP = SWA_HEADS // SWA_KV_HEADS
SWA_WINDOW = 128
SWA_WINDOW_CHUNKS = SWA_WINDOW // CHUNK
FOX_HEADS = 8
N_BRANCHES = 2
Q_A = SWA_HEADS * HEAD_DIM
KV_A = SWA_KV_HEADS * HEAD_DIM
QKV_B = FOX_HEADS * HEAD_DIM
SPLIT_SIZES = (Q_A, KV_A, KV_A, QKV_B, QKV_B, QKV_B, FOX_HEADS, N_BRANCHES * D_MODEL)
N_IN = Q_A + 2 * KV_A + 3 * QKV_B + FOX_HEADS + N_BRANCHES * D_MODEL
N_GROUPS = 4
EXPERTS_PER_GROUP = 8
N_EXPERTS = N_GROUPS * EXPERTS_PER_GROUP
TOP_K = 2
EXPERT_FF = 512
MOE_BLOCK = 128

kernel_name = 'hybrid_swa_sink_fox_hmoe_stream'

def rms_norm(x, g):
    xf = x.astype(jnp.float32)
    y = xf * lax.rsqrt(jnp.mean(xf * xf, axis=-1, keepdims=True) + RMS_EPS)
    return (y * g.astype(jnp.float32)).astype(x.dtype)

def chunk_id(pos):
    return (pos + CHUNK - N_META) // CHUNK

def rope(x, pos):
    half = HEAD_DIM // 2
    inv_freq = jnp.power(ROPE_THETA, -jnp.arange(0, HEAD_DIM, 2, dtype=jnp.float32) / HEAD_DIM)
    ang = pos.astype(jnp.float32)[:, None] * inv_freq[None, :]
    cos = jnp.cos(ang)[None, :, None, :]
    sin = jnp.sin(ang)[None, :, None, :]
    xf = x.astype(jnp.float32)
    x1, x2 = xf[..., :half], xf[..., half:]
    return jnp.concatenate([x1 * cos - x2 * sin, x2 * cos + x1 * sin], axis=-1).astype(x.dtype)

def sliding_window_sink_attention(q, k, v, sinks):
    B, Lp = q.shape[0], q.shape[1]
    nb = Lp // BLOCK
    qb = q.reshape(B, nb, BLOCK, SWA_KV_HEADS, SWA_GROUP, HEAD_DIM)

    def band(t):
        tp = jnp.pad(t, ((0, 0), (BLOCK, BLOCK), (0, 0), (0, 0)))
        tp = tp.reshape(B, nb + 2, BLOCK, SWA_KV_HEADS, HEAD_DIM)
        return jnp.concatenate([tp[:, j:j + nb] for j in range(3)], axis=2)

    kb, vb = band(k), band(v)
    s = jnp.einsum('bnqhgd,bnkhd->bnhgqk', qb, kb).astype(jnp.float32) * (HEAD_DIM ** -0.5)
    q_pos = jnp.arange(Lp).reshape(nb, BLOCK)
    k_pos = (jnp.arange(nb)[:, None] - 1) * BLOCK + jnp.arange(3 * BLOCK)[None, :]
    qc = chunk_id(q_pos)[:, :, None]
    kc = chunk_id(k_pos)[:, None, :]
    valid_k = ((k_pos >= 0) & (k_pos < Lp))[:, None, :]
    allowed = valid_k & (kc <= qc) & (kc > qc - SWA_WINDOW_CHUNKS)
    s = jnp.where(allowed[None, :, None, None], s, NEG_INF)
    sink = sinks.astype(jnp.float32).reshape(1, 1, SWA_KV_HEADS, SWA_GROUP, 1, 1)
    m = jnp.maximum(jnp.max(s, axis=-1, keepdims=True), sink)
    p = jnp.exp(s - m)
    w = p / (jnp.sum(p, axis=-1, keepdims=True) + jnp.exp(sink - m))
    o = jnp.einsum('bnhgqk,bnkhd->bnqhgd', w.astype(v.dtype), vb)
    return o.reshape(B, Lp, SWA_HEADS * HEAD_DIM)

def forgetting_attention(q, k, v, log_f):
    B, Lp = q.shape[0], q.shape[1]
    nb = Lp // BLOCK
    c = jnp.cumsum(log_f, axis=1)
    c_keys = c.transpose(0, 2, 1)
    k_pos = jnp.arange(Lp)
    qb = q.reshape(B, nb, BLOCK, FOX_HEADS, HEAD_DIM).transpose(1, 0, 2, 3, 4)
    cb = c.reshape(B, nb, BLOCK, FOX_HEADS).transpose(1, 0, 3, 2)
    pb = k_pos.reshape(nb, BLOCK)
    scale = HEAD_DIM ** -0.5

    def one_block(args):
        qi, ci, pi = args
        s = jnp.einsum('bqhd,bkhd->bhqk', qi, k).astype(jnp.float32) * scale
        s = s + ci[..., :, None] - c_keys[:, :, None, :]
        s = jnp.where((k_pos[None, :] <= pi[:, None])[None, None], s, NEG_INF)
        p = jax.nn.softmax(s, axis=-1)
        return jnp.einsum('bhqk,bkhd->bqhd', p.astype(v.dtype), v)

    o = lax.map(one_block, (qb, cb, pb))
    return o.transpose(1, 0, 2, 3, 4).reshape(B, Lp, FOX_HEADS * HEAD_DIM)

def token_mix(h, pos, w_in, qk_gain, sinks, b_forget, b_merge, w_o_swa, w_o_fox, w_out):
    B, Lp, D = h.shape
    proj = h @ w_in
    cuts = [int(c) for c in np.cumsum(SPLIT_SIZES)[:-1]]
    q_a, k_a, v_a, q_b, k_b, v_b, f_b, gates = jnp.split(proj, cuts, axis=-1)
    q_a = rope(rms_norm(q_a.reshape(B, Lp, SWA_HEADS, HEAD_DIM), qk_gain[0]), pos)
    k_a = rope(rms_norm(k_a.reshape(B, Lp, SWA_KV_HEADS, HEAD_DIM), qk_gain[1]), pos)
    v_a = v_a.reshape(B, Lp, SWA_KV_HEADS, HEAD_DIM)
    o_a = sliding_window_sink_attention(q_a, k_a, v_a, sinks)
    q_b = rms_norm(q_b.reshape(B, Lp, FOX_HEADS, HEAD_DIM), qk_gain[2])
    k_b = rms_norm(k_b.reshape(B, Lp, FOX_HEADS, HEAD_DIM), qk_gain[3])
    v_b = v_b.reshape(B, Lp, FOX_HEADS, HEAD_DIM)
    log_f = jax.nn.log_sigmoid(f_b.astype(jnp.float32) + b_forget.astype(jnp.float32))
    o_b = forgetting_attention(q_b, k_b, v_b, log_f)
    g = jax.nn.sigmoid((gates + b_merge).astype(jnp.float32)).astype(h.dtype).reshape(B, Lp, N_BRANCHES, D)
    merged = g[:, :, 0] * (o_a @ w_o_swa) + g[:, :, 1] * (o_b @ w_o_fox)
    return merged @ w_out

def hierarchical_moe(t, w_rg, b_rg, w_re, b_re, w_gate, w_up, w_down):
    T, D = t.shape
    g_logits = (t @ w_rg).astype(jnp.float32) + b_rg.astype(jnp.float32)
    group = jnp.argmax(g_logits, axis=-1)
    p_group = jnp.take_along_axis(jax.nn.softmax(g_logits, axis=-1), group[:, None], axis=1)
    e_logits = ((t @ w_re).astype(jnp.float32) + b_re.astype(jnp.float32)).reshape(T, N_GROUPS, EXPERTS_PER_GROUP)
    e_in_group = jnp.take_along_axis(e_logits, group[:, None, None], axis=1)[:, 0]
    top_val, top_idx = lax.top_k(e_in_group, TOP_K)
    gate = p_group * jax.nn.softmax(top_val, axis=-1)
    expert = group[:, None] * EXPERTS_PER_GROUP + top_idx

    A = T * TOP_K
    e_flat = expert.reshape(-1)
    g_flat = gate.reshape(-1)
    tok = jnp.repeat(jnp.arange(T), TOP_K)
    order = jnp.argsort(e_flat)
    e_s, tok_s, g_s = e_flat[order], tok[order], g_flat[order]
    counts = jnp.bincount(e_flat, length=N_EXPERTS)
    starts = jnp.cumsum(counts) - counts
    padded = (counts + MOE_BLOCK - 1) // MOE_BLOCK * MOE_BLOCK
    pad_ends = jnp.cumsum(padded)
    pad_starts = pad_ends - padded
    dest = pad_starts[e_s] + jnp.arange(A) - starts[e_s]
    n_blocks = -(-A // MOE_BLOCK) + N_EXPERTS
    n_rows = n_blocks * MOE_BLOCK
    rows = jnp.zeros((n_rows, D), t.dtype).at[dest].set(t[tok_s])
    blk_expert = jnp.minimum(jnp.searchsorted(pad_ends, jnp.arange(n_blocks) * MOE_BLOCK, side='right'), N_EXPERTS - 1)

    def expert_block(args):
        xb, e = args
        return (jax.nn.silu(xb @ w_gate[e]) * (xb @ w_up[e])) @ w_down[e]

    out = lax.map(expert_block, (rows.reshape(n_blocks, MOE_BLOCK, D), blk_expert)).reshape(n_rows, D)
    return jax.ops.segment_sum(out[dest] * g_s[:, None].astype(t.dtype), tok_s, num_segments=T)

def setup_inputs(seed: int = 0) -> dict:
    key = jax.random.key(seed)
    ks = jax.random.split(key, 20)
    f32 = jnp.float32
    D = D_MODEL
    nrm = lambda k, shape, scale: jax.random.normal(k, shape, f32) * scale
    return {
        'x': nrm(ks[0], (BATCH, SEQ, D), 1.0),
        'meta_tokens': nrm(ks[1], (N_META, D), 1.0),
        'norm1_g': 1.0 + nrm(ks[2], (DEPTH, D), 0.02),
        'w_in': nrm(ks[3], (DEPTH, D, N_IN), D ** -0.5),
        'qk_gain': 1.0 + nrm(ks[4], (DEPTH, 4, HEAD_DIM), 0.02),
        'attn_sinks': nrm(ks[5], (DEPTH, SWA_HEADS), 0.5),
        'b_forget': jnp.linspace(1.0, 6.0, FOX_HEADS, dtype=f32)[None, :] + nrm(ks[6], (DEPTH, FOX_HEADS), 0.1),
        'b_merge': nrm(ks[7], (DEPTH, N_BRANCHES * D), 0.02),
        'w_o_swa': nrm(ks[8], (DEPTH, Q_A, D), Q_A ** -0.5),
        'w_o_fox': nrm(ks[9], (DEPTH, QKV_B, D), QKV_B ** -0.5),
        'w_out': nrm(ks[10], (DEPTH, D, D), D ** -0.5),
        'norm2_g': 1.0 + nrm(ks[11], (DEPTH, D), 0.02),
        'w_router_group': nrm(ks[12], (DEPTH, D, N_GROUPS), D ** -0.5),
        'b_router_group': nrm(ks[13], (DEPTH, N_GROUPS), 0.01),
        'w_router_expert': nrm(ks[14], (DEPTH, D, N_EXPERTS), D ** -0.5),
        'b_router_expert': nrm(ks[15], (DEPTH, N_EXPERTS), 0.01),
        'w_exp_gate': nrm(ks[16], (DEPTH, N_EXPERTS, D, EXPERT_FF), D ** -0.5),
        'w_exp_up': nrm(ks[17], (DEPTH, N_EXPERTS, D, EXPERT_FF), D ** -0.5),
        'w_exp_down': nrm(ks[18], (DEPTH, N_EXPERTS, EXPERT_FF, D), EXPERT_FF ** -0.5),
    }

def reference(x, meta_tokens, norm1_g, w_in, qk_gain, attn_sinks, b_forget, b_merge, w_o_swa, w_o_fox, w_out,
              norm2_g, w_router_group, b_router_group, w_router_expert, b_router_expert,
              w_exp_gate, w_exp_up, w_exp_down):
    B, S, D = x.shape
    L = S + N_META
    Lp = -(-L // BLOCK) * BLOCK
    meta = jnp.broadcast_to(meta_tokens[None].astype(x.dtype), (B, N_META, D))
    h = jnp.concatenate([meta, x, jnp.zeros((B, Lp - L, D), x.dtype)], axis=1)
    pos = jnp.arange(Lp)
    for l in range(DEPTH):
        h = h + token_mix(rms_norm(h, norm1_g[l]), pos, w_in[l], qk_gain[l], attn_sinks[l], b_forget[l],
                          b_merge[l], w_o_swa[l], w_o_fox[l], w_out[l])
        t = rms_norm(h, norm2_g[l]).reshape(B * Lp, D)
        h = h + hierarchical_moe(t, w_router_group[l], b_router_group[l], w_router_expert[l], b_router_expert[l],
                                 w_exp_gate[l], w_exp_up[l], w_exp_down[l]).reshape(B, Lp, D)
    return h[:, N_META:N_META + S]


_drawn_inputs = setup_inputs


def setup_inputs(seed=0):
    import zlib

    import numpy as np

    out = dict(_drawn_inputs(seed))
    spreads = {}
    factors = {'qk_gain': 2.881,
     'attn_sinks': 64.0,
     'b_merge': 4.521,
     'b_router_group': 3.441,
     'b_router_expert': 3.485}
    for name, (base, spread) in spreads.items():
        noise = np.random.default_rng([zlib.crc32(name.encode()), seed]).standard_normal(out[name].shape)
        drawn = base * np.exp(spread * noise) if base else spread * noise
        out[name] = __import__('jax').numpy.asarray(drawn.astype(out[name].dtype))
    for name, factor in factors.items():
        out[name] = (out[name] * factor).astype(out[name].dtype)
    return out
```

```python
from contextlib import ExitStack

import concourse.bass as bass
import numpy as np
from concourse import mybir

F32 = mybir.dt.float32
BF16 = mybir.dt.bfloat16
I32 = mybir.dt.int32
U32 = mybir.dt.uint32
ALU = mybir.AluOpType
ACT = mybir.ActivationFunctionType
AX = mybir.AxisListType.X

P = 128
D = 1024
SEQ = 512
META = 16
POS = SEQ + META
DEPTH = 2
HD = 64
HEADS = 8
KV = 2
CHUNK = 64
NT = SEQ // P
TILES = NT + 1
KC = D // P
EPS = 1e-6
NEG = -1e30
LOWEST = -3.0e38
THETA = 10000.0

W_KV = HEADS * HD
W_QB = W_KV + 2 * KV * HD
W_KB = W_QB + 512
W_VB = W_KB + 512
W_F = W_VB + 512
W_G = W_F + HEADS

GROUPS = 4
PER = 8
EXPERTS = GROUPS * PER
FF = 512
FC = FF // P
PAIRS = EXPERTS // 2
CAP = 64
ROUNDS = -(-POS // CAP)
TAB = ROUNDS * P * PAIRS
NOWHERE = 1 << 20
YROWS = 2 * TILES * P

ROWS = [P] * NT + [META]
COL = [META + P * i for i in range(NT)] + [0]

CONST = {}


def constants():
    cols = []

    def put(name, a):
        a = np.asarray(a, np.float32)
        full = np.zeros((P, a.shape[1]), np.float32)
        full[:a.shape[0]] = a
        at = sum(c.shape[1] for c in cols)
        CONST[name] = (at, a.shape[1])
        cols.append(full)

    k = np.arange(P)
    put("ident", np.eye(P))
    put("upto", k[:, None] <= k[None, :])
    put("before", k[:, None] < k[None, :])
    put("ones", np.ones((P, P)))
    put("causal", np.where(k[None, :] > k[:, None], NEG, 0.0))
    key = np.arange(CHUNK + P)
    masked = np.where(k[:, None] < CHUNK, key[None, :] >= 2 * CHUNK, key[None, :] < CHUNK)
    put("window", np.where(masked, NEG, 0.0))
    inv = np.power(np.float32(THETA), -np.arange(0, HD, 2, dtype=np.float32) / np.float32(HD)).astype(np.float32)
    cos, sin = np.zeros((P, TILES, HD), np.float32), np.zeros((P, TILES, HD), np.float32)
    for i in range(TILES):
        ang = (COL[i] + k).astype(np.float32)[:, None] * inv[None, :]
        cos[:, i] = np.concatenate([np.cos(ang), np.cos(ang)], 1)
        sin[:, i] = np.concatenate([-np.sin(ang), np.sin(ang)], 1)
    put("cos", cos.reshape(P, -1))
    put("sin", sin.reshape(P, -1))
    put("down", np.tile(PER - np.arange(PER), (P, 1)))
    e = np.arange(EXPERTS)
    put("ebase", np.tile((e % 2) * CAP * PAIRS + e // 2, (P, 1)))
    put("row", np.arange(TILES)[None, :] * P + k[:, None])
    return np.concatenate(cols, 1)


NCONST = constants().shape[1]


def attention_plan():
    units = [(j, br, h) for j in [NT] + list(range(NT)) for br in (0, 1) for h in range(HEADS)]
    steps, turns, pvs = [], [], 0
    for v in range(len(units) + 5):
        st = {"score": v if v < len(units) else None, "turn": [], "pv": [], "norm": None, "oturn": None}
        if 0 <= v - 1 < len(units):
            j, br, h = units[v - 1]
            if br == 0:
                if j == NT:
                    sets = [[(P - META, META, NT)]]
                elif j == 0:
                    sets = [[(P, P, 0)], [(P - META, META, NT)]]
                else:
                    sets = [[(0, P, j - 1), (P, P, j)]]
            elif j == NT:
                sets = [[(0, META, NT)]]
            else:
                sets = [[(COL[i], P, i) for i in range(j + 1)], [(0, META, NT)]]
            for n, s in enumerate(sets):
                st["turn"].append(len(turns))
                turns.append({"unit": v - 1, "blocks": s, "first": n == 0, "last": n == len(sets) - 1, "o": None})
        if 0 <= v - 2 < len(units):
            st["pv"] = [n for n, t in enumerate(turns) if t["unit"] == v - 2]
        if 0 <= v - 3 < len(units) and units[v - 3][2] == HEADS - 1:
            st["norm"] = v - 3
        if 0 <= v - 4 < len(units) and units[v - 4][2] == HEADS - 1:
            st["oturn"] = len(turns)
            turns.append({"unit": None, "blocks": None, "o": v - 4})
        steps.append(st)
    for st in steps:
        for n in st["pv"]:
            pvs += 1
            turns[n]["pv_count"] = pvs
    return units, steps, turns


def trunk_kernel(nc, x, meta_tokens, norm1_g, w_in, qk_gain, attn_sinks, b_forget, b_merge, w_o_swa, w_o_fox, w_out,
                 norm2_g, w_router_group, b_router_group, w_router_expert, b_router_expert,
                 w_exp_gate, w_exp_up, w_exp_down, const, out):
    ctx = ExitStack()
    with ctx:
        def sb(name, shape, dt=F32):
            return ctx.enter_context(nc.sbuf_tensor(name, shape, dt))

        def sem(name):
            s = ctx.enter_context(nc.semaphore(name))
            sems.append(s)
            return s

        sems = []
        t_dram = nc.dram_tensor("t_rows", (POS, D), F32, kind="Internal").ap()
        y_dram = nc.dram_tensor("y_rows", (YROWS, D), F32, kind="Internal").ap()
        tab_dram = nc.dram_tensor("slot_table", (TAB, 4), U32, kind="Internal").ap()

        cst = sb("cst", [P, NCONST])

        def C(name):
            at, n = CONST[name]
            return cst[:, at:at + n]

        ident, upto, ones = C("ident"), C("upto"), C("ones")
        cosv = C("cos").rearrange("p (t d) -> p t d", d=HD)
        sinv = C("sin").rearrange("p (t d) -> p t d", d=HD)
        identb = sb("identb", [P, P], BF16)
        causalb = sb("causalb", [P, P], BF16)
        windowb = sb("windowb", [P, CHUNK + P], BF16)
        beforeb = sb("beforeb", [P, P], BF16)
        onesb = sb("onesb", [P, P], BF16)
        SLOT = 4096
        wslot = [sb(f"wslot{s}", [P, SLOT]) for s in range(6)]
        h = sb("h", [P, TILES, D])
        xT = sb("xT", [P, KC, POS])
        gainb = sb("gainb", [P, D])
        wr = sb("wr", [P, KC, GROUPS + EXPERTS])
        rbias = sb("rbias", [P, GROUPS + EXPERTS])
        hgain = sb("hgain", [P, 4, HD])
        sinks = sb("sinks", [P, HEADS])
        fbias = sb("fbias", [P, HEADS])
        gbias_rows = sb("gbias_rows", [2 * KC, P])
        gbias = sb("gbias", [P, 2 * KC])
        halfneg = sb("halfneg", [P, HEADS])
        small = sb("small", [P, 160])
        qaT = sb("qaT", [P, 4, POS])
        qbT = sb("qbT", [P, 4, POS])
        arena = sb("arena", [P, 4 * POS + TILES * 512])
        kbT = arena[:, 0:4 * POS].rearrange("p (c n) -> p c n", c=4)
        vb = arena[:, 4 * POS:4 * POS + TILES * 512].rearrange("p (t n) -> p t n", t=TILES)
        mrgT = arena[:, 0:KC * POS].rearrange("p (c n) -> p c n", c=KC)
        kaT = sb("kaT", [P, KV, POS])
        va = sb("va", [P, TILES, KV * HD])
        work = sb("work", [P, 3104])
        tabs = sb("tabs", [P, PAIRS + 1, 4], U32)
        cnt = sb("cnt", [1, 2], I32)
        idx_g = sb("idx_g", [P, 1], U32)
        idx_s = sb("idx_s", [P, 1], U32)
        gcol = sb("gcol", [P, 1])

        qaf, qbf = (t[:, :, :].rearrange("p c n -> p (c n)") for t in (qaT, qbT))
        xn = qaf[:, 0:2 * D].rearrange("p (b n) -> p b n", b=2)
        xsq = qbf[:, 0:D]
        sq, qn1, qn2, rot = (work[:, 512 * k:512 * (k + 1)] for k in range(4))
        qnb = work[:, 2048:3072].rearrange("p (b n) -> p b n", b=2)
        PA = work[:, 0:512].rearrange("p (b n) -> p b n", b=2)
        PF = work[:, 512:512 + 2 * POS].rearrange("p (b n) -> p b n", b=2)
        PT = work[:, 1568:2592].rearrange("p (b n) -> p b n", b=2)
        osb = work[:, 2592:3104]
        sig = work[:, 0:4 * 264].rearrange("p (k n) -> p k n", k=4)
        rbuf = qbf[:, D:2 * D + 64]
        xg = arena[:, 0:D]
        xgT = arena[:, D:2 * D].rearrange("p (c n) -> p c n", c=KC)
        sg = arena[:, 2048:2560]
        hh = arena[:, 2560:3072]
        hT = arena[:, 3072:3584].rearrange("p (c n) -> p c n", c=FC)
        ysb = arena[:, 3584:4608]

        ss, rstd = small[:, 0:8], small[:, 8:16]
        hss, hr = small[:, 16:24], small[:, 24:32]
        stat = sb("stat", [P, 3, 80])
        mx, nm, rs = stat[:, 0, :], stat[:, 1, :], stat[:, 2, :]
        esk, den, rden = small[:, 32:40], small[:, 40:48], small[:, 48:56]
        frg = sb("frg", [P, 4, TILES, HEADS])
        cso = sb("cso", [P, TILES, HEADS])
        ncTt = sb("ncTt", [HEADS, POS])

        ps = ctx.enter_context(nc.psum_tensor("ps", [P, 8, 512], F32))

        s_in = sem("s_in")
        s_cst = sem("s_cst")
        s_tab0 = sem("s_tab0")
        loaded = [sem(f"loaded{s}") for s in range(6)]
        w_qkv = [sem(f"w_qkv{k}") for k in range(5)]
        w_f = sem("w_f")
        w_gates = [[sem(f"w_gates{k}_{br}") for br in range(2)] for k in range(4)]
        w_oa, w_ob = sem("w_oa"), sem("w_ob")
        w_o = [sem(f"w_o{k}") for k in range(2)]
        freed = [sem(f"freed{s}") for s in range(6)]
        s_par = sem("s_par")
        s_g1 = sem("s_g1")
        s_g2 = sem("s_g2")
        s_ss = sem("s_ss")
        s_rstd = sem("s_rstd")
        s_xn = sem("s_xn")
        s_tp = sem("s_tp")
        s_xT = sem("s_xT")
        s_tst = [sem(f"s_tst{b}") for b in range(2)]
        s_gb = sem("s_gb")
        s_gbe = sem("s_gbe")
        s_prj = sem("s_prj")
        s_prjfree = sem("s_prjfree")
        s_sq = sem("s_sq")
        s_hss = sem("s_hss")
        s_hr = sem("s_hr")
        s_qn = sem("s_qn")
        s_qT = sem("s_qT")
        s_qTe = sem("s_qTe")
        s_fz = sem("s_fz")
        s_fe = sem("s_fe")
        s_lf = sem("s_lf")
        s_c = sem("s_c")
        s_ce = sem("s_ce")
        s_S = sem("s_S")
        s_nm = sem("s_nm")
        s_P = sem("s_P")
        s_T = sem("s_T")
        s_Te = [sem(f"s_Te{b}") for b in range(2)]
        s_PV = sem("s_PV")
        s_skin = sem("s_skin")
        s_esk = sem("s_esk")
        s_on = sem("s_on")
        s_gy = sem("s_gy")
        s_sig = sem("s_sig")
        s_mrg = sem("s_mrg")
        s_wo = sem("s_wo")
        s_res = sem("s_res")
        s_lg = sem("s_lg")
        s_M = sem("s_M")
        s_rank = sem("s_rank")
        s_exl = sem("s_exl")
        s_exd = sem("s_exd")
        s_ent = sem("s_ent")
        s_scat = sem("s_scat")
        s_tabl = sem("s_tabl")
        e_blank = sem("e_blank")
        e_st = sem("e_st")
        e_idx = sem("e_idx")
        e_gath = sem("e_gath")
        e_xgT = sem("e_xgT")
        e_xT = sem("e_xT")
        e_sg = sem("e_sg")
        e_h = sem("e_h")
        e_hT = sem("e_hT")
        e_hTe = sem("e_hTe")
        e_y = sem("e_y")
        e_scat = sem("e_scat")
        y_in = [sem(f"y_in{i}") for i in range(TILES)]
        y_add = sem("y_add")
        s_blank = sem("s_blank")
        s_out = sem("s_out")
        d_own = sem("d_own")
        p_own = sem("p_own")
        a_own = sem("a_own")
        lo, hi = min(s.num for s in sems), max(s.num for s in sems)
        assert hi - lo + 1 == len(sems)

        blank = wslot[5][:, 0:TAB * 4 // P].bitcast(U32)

        def clear_all():
            nc.all_engine_barrier()
            with nc.Block() as block:
                @block.gpsimd
                def _(pool):
                    pool.dma_reset(range(lo, hi + 1))
                    pool.sem_clear(range(lo, hi + 1))
            nc.all_engine_barrier()

        class Own:

            def __init__(self, eng, s):
                self.eng, self.s, self.n = eng, s, 0

            def link(self, ins):
                self.n += 1
                ins.then_inc(self.s, 1)
                self.eng.wait_ge(self.s, self.n)

        with nc.Block() as block:
            @block.sync
            def _(sp):
                sp.dma_start(cst[:, :], const).then_inc(s_in, 16)
                for i in range(NT):
                    sp.dma_start(h[:, i, :], x[0, i * P:(i + 1) * P, :]).then_inc(s_in, 16)
                sp.dma_start(h[0:META, NT, :], meta_tokens).then_inc(s_in, 16)
                sp.wait_ge(s_in, 16 * (TILES + 1))
                sp.wait_ge(s_tab0, 1)
                sp.dma_start(tab_dram.rearrange("(p r) c -> p (r c)", p=P), blank).then_inc(s_blank, 16)
                sp.wait_ge(s_blank, 16)

            @block.gpsimd
            def _(pool):
                pool.memset(blank, NOWHERE).then_inc(s_tab0, 1)
                pool.memset(halfneg[:, :], -0.5)
                pool.memset(tabs[:, :, :], NOWHERE)

            @block.vector
            def _(dve):
                dve.wait_ge(s_in, 16 * (TILES + 1))
                for dst, name in ((identb, "ident"), (causalb, "causal"), (windowb, "window"), (beforeb, "before"),
                                  (onesb, "ones")):
                    dve.tensor_copy(dst[:, :], C(name))
        clear_all()

        units, steps, turns = attention_plan()
        last_turn = {t["unit"]: n for n, t in enumerate(turns) if t["unit"] is not None}
        oturn_of = {t["o"] // HEADS: n for n, t in enumerate(turns) if t["o"] is not None}

        def block_of(v):
            return v // HEADS

        def pv_upto(v):
            return turns[last_turn[v]]["pv_count"]

        psf = ps[:, :, :].rearrange("p b n -> p (b n)")

        def keys_of(v):
            j, br, _ = units[v]
            if j == NT:
                return META
            return (COL[j] + P if br else (CHUNK if j else META) + P)

        def score_in(v):
            j, br, _ = units[v]
            at = 512 * (2 + 2 * (v % 2)) + (512 - META if br else 0)
            return psf[0:ROWS[j], at:at + keys_of(v)]

        def prob(v):
            return (PF if units[v][1] else PA)[:, v % 2, :]

        def prob_out(v):
            j, br, _ = units[v]
            n = keys_of(v)
            at = 0 if br else (P - META if j == NT else 2 * P - n)
            return prob(v)[0:ROWS[j], at:at + n]

        def evacuate(eng, copy, n):
            t, b = turns[n], n % 2
            src = ps[:, b, :].rearrange("p (c n) -> p c n", c=4)
            if t["o"] is not None:
                j, br, _ = units[t["o"]]
                return copy((qaT, qbT)[br][:, :, COL[j]:COL[j] + ROWS[j]], src[:, :, 0:ROWS[j]])
            r, nk, nb = ROWS[units[t["unit"]][0]], t["blocks"][0][1], len(t["blocks"])
            before = [m for m in range(n % 2, n, 2) if turns[m]["o"] is None]
            if before:
                eng.wait_ge(s_PV, turns[before[-1]]["pv_count"])
            return copy(PT[0:nk, b, :].rearrange("p (c n) -> p c n", c=4)[:, 0:nb, 0:r], src[0:nk, 0:nb, 0:r])

        def sig2(w, br):
            return sig[:, 2 * (w % 2) + br, :]

        CHUNKS = 5

        r_n = [0]

        def r(shape, dt=F32):
            n = int(np.prod(shape))
            at = r_n[0]
            r_n[0] += n
            assert r_n[0] <= 2 * D - D + 64
            v = rbuf[:, at:at + n]
            if dt != F32:
                v = v.bitcast(dt)
            names = "abc"[:len(shape)]
            if len(shape) == 1:
                return v
            return v.rearrange("p (" + " ".join(names) + ") -> p " + " ".join(names),
                               **{k: n_ for k, n_ in zip(names[1:], shape[1:])})

        r_lg = r((TILES, GROUPS + EXPERTS))
        r_gm, r_f, r_sum, r_pg, r_v1, r_v2, r_d, r_den = (r((TILES,)) for _ in range(8))
        r_dg, r_eq, r_og = (r((TILES, GROUPS)) for _ in range(3))
        r_sel = r((TILES, EXPERTS))
        r_ein, r_e2, r_w = (r((TILES, PER)) for _ in range(3))
        r_o = [r((TILES, PER)) for _ in range(2)]
        r_g = [r((TILES,)) for _ in range(2)]
        r_rank, r_at, r_hf, r_slot = (r((TILES,)) for _ in range(4))
        r_ri = r((TILES,), I32)
        r_cm, r_ci = r((2,)), r((2,), I32)
        ent = sb("ent", [P, 2, TILES, 4], U32)
        slot_at = sb("slot_at", [P, 2, TILES], U32)
        Mb = sb("Mb", [P, TILES, EXPERTS], BF16)

        work_M = work[:, 1056:1056 + 2 * TILES * EXPERTS].rearrange("p (a t n) -> p a t n", a=2, t=TILES)
        work_R = work[:, 1376:1376 + 2 * TILES * EXPERTS].rearrange("p (a t n) -> p a t n", a=2, t=TILES)

        def layer(l):
            def L(a):
                return a[bass.ds(l, 1)]

            ORDER = ((w_exp_gate, 0, 3), (w_exp_gate, 1, 0), (w_exp_up, 0, 4), (w_exp_up, 1, 1),
                     (w_exp_down, 0, 5), (w_exp_down, 1, 2))

            def load_expert(sp, w, e, s):
                src = w[bass.ds(l, 1), e]
                if w is w_exp_down:
                    sp.dma_start(wslot[s][:, :].rearrange("p (c n) -> p c n", c=FC),
                                 src.rearrange("a b (c p) n -> p (a b c) n", p=P)).then_inc(loaded[s], 16)
                else:
                    sp.dma_start(wslot[s][:, :], src.rearrange("a b (p c) n -> p (a b c n)", p=P)).then_inc(loaded[s], 16)

            def experts_sync(sp):
                with sp.Fori(1, PAIRS) as i:
                    for w, par, s in ORDER:
                        sp.wait_ge(freed[s], i)
                        load_expert(sp, w, bass.ds(2 * i + par, 1), s)

            def experts_pool(pool):
                token_bound = pool.to_reg(POS - 1)
                row_bound = pool.to_reg(YROWS - 1)

                def stage(idx, col, k):
                    pool.tensor_copy(idx[:, :], tabs[:, col, k:k + 1]).then_inc(e_idx, 1)
                    pool.wait_ge(e_idx, 1)
                    pool.sem_clear(e_idx)

                def gather(col):
                    stage(idx_g, col, 0)
                    pool.indirect_dma_start(out=xg, out_offset=None, in_=t_dram,
                                            in_offset=bass.IndirectOffsetOnAxis(ap=idx_g[:, 0:1], axis=0),
                                            bounds_check=token_bound, oob_is_err=False).then_inc(e_gath, 16)

                pool.memset(xg, 0.0).then_inc(e_blank, 1)
                pool.wait_ge(e_blank, 1)
                gather(slice(0, 1))
                with pool.Fori(0, PAIRS) as i:
                    pool.wait_ge(e_gath, 16 * (i + 1))
                    pool.wait_ge(e_xgT, i + 1)
                    gather(bass.ds(i + 1, 1))
                    pool.tensor_copy(gcol[:, :], tabs[:, bass.ds(i, 1), 2:3].bitcast(F32)).then_inc(e_st, 1)
                    pool.wait_ge(e_y, 2 * (i + 1))
                    stage(idx_s, bass.ds(i, 1), 1)
                    pool.indirect_dma_start(out=y_dram, out_offset=bass.IndirectOffsetOnAxis(ap=idx_s[:, 0:1], axis=0),
                                            in_=ysb, in_offset=None, bounds_check=row_bound,
                                            oob_is_err=False).then_inc(e_scat, 16)
                    pool.wait_ge(e_scat, 16 * (i + 1))
                pool.wait_ge(e_gath, 16 * (PAIRS + 1))

            def experts_tensor(pe):
                def turn_tokens():
                    for c in range(KC):
                        last = pe.transpose(ps[:, 6 + c // 4, (c % 4) * P:(c % 4 + 1) * P], xg[:, c::KC], ident)
                    last.then_inc(e_xgT, 1)

                pe.wait_ge(e_gath, 16)
                turn_tokens()
                with pe.Fori(0, PAIRS) as i:
                    pe.wait_ge(e_xT, 2 * (i + 1))
                    for bank, pair in ((0, (3, 0)), (1, (4, 1))):
                        wa, wb = (wslot[s][:, :].rearrange("p (c n) -> p c n", c=KC) for s in pair)
                        for s in pair:
                            pe.wait_ge(loaded[s], 16 * (i + 1))
                        for c in range(KC):
                            for par, w in ((0, wa), (1, wb)):
                                last = pe.matmul(ps[CAP * par:CAP * (par + 1), bank, :],
                                                 xgT[:, c, CAP * par:CAP * (par + 1)], w[:, c, :],
                                                 start=(c == 0), stop=(c == KC - 1))
                                if c == KC - 1:
                                    last.then_inc(freed[pair[par]], 1)
                    pe.wait_ge(e_gath, 16 * (i + 2))
                    turn_tokens()
                    pe.wait_ge(e_h, i + 1)
                    for c in range(FC):
                        last = pe.transpose(ps[:, 4, c * P:(c + 1) * P], hh[:, c * P:(c + 1) * P], ident)
                    last.then_inc(e_hT, 1)
                    pe.wait_ge(e_hTe, i + 1)
                    pe.wait_ge(e_st, i + 1)
                    for s in (5, 2):
                        pe.wait_ge(loaded[s], 16 * (i + 1))
                    for half in range(2):
                        for c in range(FC):
                            for par, s in ((0, 5), (1, 2)):
                                w = wslot[s][:, :].rearrange("p (c n) -> p c n", c=FC)
                                last = pe.matmul(ps[CAP * par:CAP * (par + 1), 2 + half, :],
                                                 hT[:, c, CAP * par:CAP * (par + 1)],
                                                 w[:, c, half * 512:(half + 1) * 512],
                                                 start=(c == 0), stop=(c == FC - 1))
                                if half == 1 and c == FC - 1:
                                    last.then_inc(freed[s], 1)

            def experts_scalar(act):
                def tokens_out(i):
                    act.wait_ge(e_xgT, i)
                    for k in range(2):
                        act.copy(xgT[:, 4 * k:4 * k + 4, :].rearrange("p c n -> p (c n)"), ps[:, 6 + k, :]).then_inc(e_xT, 1)

                tokens_out(1)
                with act.Fori(0, PAIRS) as i:
                    act.wait_ge(freed[0], i + 1)
                    act.activation(sg, ps[:, 0, :], ACT.Silu).then_inc(e_sg, 1)
                    act.wait_ge(freed[1], i + 1)
                    tokens_out(i + 2)

            def experts_vector(dve):
                with dve.Fori(0, PAIRS) as i:
                    dve.wait_ge(e_sg, i + 1)
                    dve.wait_ge(freed[1], i + 1)
                    dve.tensor_tensor(hh, sg, ps[:, 1, :], ALU.mult).then_inc(e_h, 1)
                    dve.wait_ge(e_hT, i + 1)
                    dve.tensor_copy(hT.rearrange("p c n -> p (c n)"), ps[:, 4, :]).then_inc(e_hTe, 1)
                    dve.wait_ge(freed[2], i + 1)
                    dve.wait_ge(e_st, i + 1)
                    for half in range(2):
                        dve.tensor_scalar(ysb[:, half * 512:(half + 1) * 512], ps[:, 2 + half, :], gcol[:, 0:1], None,
                                          ALU.mult).then_inc(e_y, 1)

            def load_table(pool, rows):
                pool.dma_start(tabs[:, 0:PAIRS, :].rearrange("p m c -> p (m c)"), rows).then_inc(s_tabl, 16)
                pool.wait_ge(s_tabl, 16)

            with nc.Block() as block:
                @block.sync
                def _(sp):
                    w3 = w_in[bass.ds(l, 1)].rearrange("a (p c) n -> p (a c) n", p=P)
                    wo_a = L(w_o_swa).rearrange("a (c p) n -> p (a c) n", p=P)
                    wo_b = L(w_o_fox).rearrange("a (c p) n -> p (a c) n", p=P)
                    wo = L(w_out).rearrange("a (c p) n -> p (a c) n", p=P)

                    def view(s, c):
                        return wslot[s][:, :].rearrange("p (c n) -> p c n", c=c)

                    sp.dma_start(gainb[:, :], L(norm1_g).broadcast_to((P, D))).then_inc(s_g1, 16)
                    kvf = wslot[0][:, 0:KC * 264].rearrange("p (c n) -> p c n", c=KC)
                    sp.dma_start(kvf[:, :, 0:256], w3[:, :, W_KV:W_QB]).then_inc(w_qkv[0], 16)
                    sp.dma_start(kvf[:, :, 256:264], w3[:, :, W_F:W_G]).then_inc(w_f, 16)
                    for c, at in ((1, 0), (2, W_QB), (3, W_KB), (4, W_VB)):
                        sp.dma_start(view(c, KC), w3[:, :, at:at + 512]).then_inc(w_qkv[c], 16)
                    sp.dma_start(view(5, 4), wo_a).then_inc(w_oa, 16)
                    sp.wait_ge(s_xn, TILES)
                    sp.dma_start(gainb[:, :], L(norm2_g).broadcast_to((P, D))).then_inc(s_g2, 16)
                    sp.wait_ge(s_prj, TILES)
                    sp.dma_start(view(0, 4), wo_b).then_inc(w_ob, 16)
                    for n in range(4):
                        s = n + 1
                        sp.wait_ge(s_prj, TILES * (s + 1))
                        for br in range(2):
                            dst = wslot[s][:, :].rearrange("p (c b n) -> p c b n", c=KC, b=2)
                            at = W_G + br * D + n * 256
                            sp.dma_start(dst[:, :, br, :], w3[:, :, at:at + 256]).then_inc(w_gates[n][br], 16)
                    for n in range(2):
                        sp.wait_ge(s_gy, 16 * (n + 1) - 2)
                        sp.dma_start(view(n + 1, 4), wo[:, 4 * n:4 * n + 4, :]).then_inc(w_o[n], 16)
                    free = {3: (s_gy, 16 * 3 - 2), 4: (s_gy, 16 * 4 - 2), 5: (s_gy, 64), 0: (s_gy, 64),
                            1: (s_wo, 2 * TILES), 2: (s_wo, 2 * TILES)}
                    for s in (3, 4, 5, 0, 1, 2):
                        w, par, _ = next(o for o in ORDER if o[2] == s)
                        sp.wait_ge(*free[s])
                        load_expert(sp, w, slice(par, par + 1), s)
                    for k in range(TILES):
                        sp.wait_ge(s_xn, TILES + k + 1)
                        sp.dma_start(t_dram[P * k:P * k + ROWS[k], :], xn[0:ROWS[k], k % 2, :]).then_inc(s_tst[k % 2], 16)
                    experts_sync(sp)

                @block.gpsimd
                def _(pool):
                    own = Own(pool, p_own)
                    with nc.allow_non_contiguous_dma("small parameters"):
                        pool.dma_start(hgain[:, :, :].rearrange("p k n -> p (k n)"),
                                       L(qk_gain).rearrange("a k n -> a (k n)").broadcast_to((P, 4 * HD))).then_inc(s_par, 16)
                        pool.dma_start(sinks[:, :], L(attn_sinks).broadcast_to((P, HEADS))).then_inc(s_par, 16)
                        pool.dma_start(fbias[:, :], L(b_forget).broadcast_to((P, HEADS))).then_inc(s_par, 16)
                        pool.dma_start(gbias_rows[:, :], L(b_merge).rearrange("a (k p) -> (a k) p", p=P)).then_inc(s_par, 16)
                        pool.dma_start(rbias[:, 0:GROUPS], L(b_router_group).broadcast_to((P, GROUPS))).then_inc(s_par, 16)
                        pool.dma_start(rbias[:, GROUPS:], L(b_router_expert).broadcast_to((P, EXPERTS))).then_inc(s_par, 16)
                        pool.dma_start(wr[:, :, 0:GROUPS],
                                       L(w_router_group).rearrange("a (p c) n -> p (a c) n", p=P)).then_inc(s_par, 16)
                        pool.dma_start(wr[:, :, GROUPS:],
                                       L(w_router_expert).rearrange("a (p c) n -> p (a c) n", p=P)).then_inc(s_par, 16)

                    def rsqrt_of_mean(dst, src, n):
                        own.link(pool.tensor_scalar(dst, src, 1.0 / n, EPS, ALU.mult, ALU.add))
                        return pool.tensor_tensor(dst, dst, halfneg[0:dst.shape[0], 0:dst.shape[1]], ALU.pow)

                    def norms(q):
                        for k in range(TILES):
                            r = ROWS[k]
                            pool.wait_ge(s_ss, TILES * q + k + 1)
                            rsqrt_of_mean(rstd[0:r, k:k + 1], ss[0:r, k:k + 1], D).then_inc(s_rstd, 1)

                    norms(0)
                    for u in range(4 * TILES):
                        c, i = divmod(u, TILES)
                        n = KV if c == 0 else HEADS
                        pool.wait_ge(s_hss, u + 1)
                        rsqrt_of_mean(hr[0:ROWS[i], 0:n], hss[0:ROWS[i], 0:n], HD).then_inc(s_hr, 1)
                    norms(1)
                    pool.wait_ge(s_ent, 1)
                    for a in range(2):
                        for i in range(TILES):
                            r = ROWS[i]
                            pool.indirect_dma_start(
                                out=tab_dram, out_offset=bass.IndirectOffsetOnAxis(ap=slot_at[0:r, a, i:i + 1], axis=0),
                                in_=ent[0:r, a, i, :], in_offset=None, bounds_check=TAB - 1,
                                oob_is_err=False).then_inc(s_scat, 16)
                    pool.wait_ge(s_scat, 16 * 2 * TILES)
                    load_table(pool, tab_dram[0:P * PAIRS].rearrange("(p m) c -> p (m c)", p=P))
                    for b in range(2):
                        pool.wait_ge(s_tst[b], 16 * (3 - b))
                    experts_pool(pool)

                @block.scalar
                def _(act):
                    def turned_out(q):
                        for k in range(TILES):
                            r = ROWS[k]
                            for half in range(2):
                                act.wait_ge(s_tp, 2 * (TILES * q + k) + half + 1)
                                src = ps[:, 2 * q + half, :].rearrange("p (c n) -> p c n", c=4)[:, :, 0:r]
                                act.copy(xT[:, 4 * half:4 * half + 4, COL[k]:COL[k] + r], src).then_inc(s_xT, 1)

                    turned_out(0)

                    def head_out(u):
                        c, i = divmod(u, TILES)
                        r = ROWS[i]
                        dst = (kaT, qaT, qbT, kbT)[c]
                        n = KV if c == 0 else 4
                        act.wait_ge(s_qT, u + 1)
                        src = ps[:, u % 2, :].rearrange("p (c n) -> p c n", c=4)[:, 0:n, 0:r]
                        act.copy(dst[:, 0:n, COL[i]:COL[i] + r], src).then_inc(s_qTe, 1)

                    for u in range(4 * TILES):
                        c, i = divmod(u, TILES)
                        r, n = ROWS[i], (P if c == 0 else 512)
                        act.wait_ge(s_prj, u + 1)
                        if u >= 1:
                            act.wait_ge(s_hss, u)
                        act.activation(sq[0:r, 0:n], ps[0:r, 2 + u % 3, 0:n], ACT.Square).then_inc(s_sq, 1)
                        if u == TILES:
                            act.wait_ge(s_fz, 1)
                            act.activation(frg[:, 2], frg[:, 1], ACT.Exp, scale=-1.0).then_inc(s_fe, 1)
                            act.wait_ge(s_fe, 1)
                            act.activation(frg[:, 3], frg[:, 2], ACT.Ln, bias=1.0).then_inc(s_fe, 1)
                        if u >= 2:
                            head_out(u - 2)
                    head_out(4 * TILES - 2)
                    head_out(4 * TILES - 1)
                    act.wait_ge(s_gb, 1)
                    act.copy(gbias[:, :], ps[:, 7, 0:2 * KC]).then_inc(s_gbe, 1)

                    def turn_out(n):
                        t = turns[n]
                        b = n % 2
                        act.wait_ge(s_T, n + 1)
                        evacuate(act, act.copy, n).then_inc(s_Te[b], 1)

                    for v, st in enumerate(steps):
                        if st["score"] is not None:
                            j, br, hd = units[v]
                            r = ROWS[j]
                            act.wait_ge(s_nm, v + 1)
                            if hd >= 2:
                                act.wait_ge(s_T, last_turn[v - 2] + 1)
                            elif v >= 16:
                                act.wait_ge(s_T, last_turn[v - 16 + 6] + 1)
                            act.activation(prob_out(v), score_in(v), ACT.Exp, bias=nm[0:r, v:v + 1],
                                           accum_out=rs[0:r, v:v + 1]).then_inc(s_P, 1)
                        if st["norm"] is not None and units[st["norm"]][1] == 0:
                            n = block_of(st["norm"]) // 2
                            j = units[st["norm"]][0]
                            act.wait_ge(s_skin, n + 1)
                            act.activation(esk[0:ROWS[j], :], den[0:ROWS[j], :], ACT.Exp).then_inc(s_esk, 1)
                        for n in st["turn"] + ([st["oturn"]] if st["oturn"] is not None else []):
                            if n % 2:
                                turn_out(n)

                    for w in range(2 * KC):
                        n = w // 2
                        act.wait_ge(s_gy, 4 * w + 2)
                        if w >= 2:
                            act.wait_ge(s_mrg, w - 1)
                        for br in range(2):
                            act.activation(sig2(w, br), ps[:, 4 * (w % 2) + br, 0:264], ACT.Sigmoid,
                                           bias=gbias[:, br * KC + n:br * KC + n + 1]).then_inc(s_sig, 1)
                    turned_out(1)
                    act.wait_ge(s_exl, 1)
                    act.activation(r_dg, r_dg, ACT.Exp).then_inc(s_exd, 1)
                    act.wait_ge(s_exl, 2)
                    act.activation(r_d, r_d, ACT.Exp).then_inc(s_exd, 1)
                    experts_scalar(act)

                @block.tensor
                def _(pe):
                    def turn_norm(q, k):
                        r = ROWS[k]
                        pe.wait_ge(s_xn, TILES * q + k + 1)
                        for half in range(2):
                            n = 2 * k + half
                            if n >= 2:
                                pe.wait_ge(s_xT, 2 * TILES * q + n - 1)
                            for c in range(4):
                                last = pe.transpose(ps[:, 2 * q + half, c * P:c * P + r],
                                                    xn[0:r, k % 2, 4 * half + c::KC], ident[0:r, 0:r])
                            last.then_inc(s_tp, 1)

                    for k in range(TILES):
                        turn_norm(0, k)

                    def turn_heads(u):
                        c, i = divmod(u, TILES)
                        r = ROWS[i]
                        pe.wait_ge(s_qn, u + 1)
                        if u >= 2:
                            pe.wait_ge(s_qTe, u - 1)
                        for k in range(KV if c == 0 else 4):
                            last = pe.transpose(ps[:, u % 2, k * P:k * P + r], qnb[0:r, u % 2, k * P:(k + 1) * P],
                                                ident[0:r, 0:r])
                        last.then_inc(s_qT, 1)

                    for c in range(CHUNKS):
                        n = 264 if c == 0 else 512
                        s = c
                        w = wslot[s][:, 0:KC * n].rearrange("p (c n) -> p c n", c=KC)
                        pe.wait_ge(w_qkv[c], 16)
                        if c == 0:
                            pe.wait_ge(w_f, 16)
                        for i in range(TILES):
                            u = c * TILES + i
                            r = ROWS[i]
                            pe.wait_ge(s_xT, 2 * TILES if c else 2 * (i + 1))
                            if u >= 3:
                                pe.wait_ge(s_prjfree, u - 2)
                            for k in range(KC):
                                last = pe.matmul(ps[0:r, 2 + u % 3, 0:n], xT[:, k, COL[i]:COL[i] + r], w[:, k, :],
                                                 start=(k == 0), stop=(k == KC - 1))
                            last.then_inc(s_prj, 1)
                            if u >= 2 and u - 2 < 4 * TILES:
                                turn_heads(u - 2)
                    pe.wait_ge(s_lf, 1)
                    lf = frg[:, 0]
                    cps = ps[:, 5, 0:TILES * HEADS].rearrange("p (t n) -> p t n", t=TILES)
                    pe.matmul(cps[0:META, NT, :], upto[0:META, 0:META], lf[0:META, NT, :], start=True, stop=True)
                    for j in range(NT):
                        pe.matmul(cps[:, j, :], ones[0:META, :], lf[0:META, NT, :], start=True, stop=False)
                        for i in range(j):
                            pe.matmul(cps[:, j, :], ones, lf[:, i, :], start=False, stop=False)
                        last = pe.matmul(cps[:, j, :], upto, lf[:, j, :], start=False, stop=True)
                    last.then_inc(s_c, 1)
                    pe.wait_ge(s_par, 16 * 8)
                    pe.transpose(ps[:, 7, 0:2 * KC], gbias_rows[:, :], ident[0:2 * KC, 0:2 * KC]).then_inc(s_gb, 1)
                    pe.wait_ge(s_ce, 1)
                    for j in range(NT):
                        pe.transpose(ps[0:HEADS, 6, j * P:(j + 1) * P], cso[:, j, :], ident)
                    pe.transpose(ps[0:HEADS, 5, 64:64 + META], cso[0:META, NT, :], ident[0:META, 0:META]).then_inc(s_c, 1)
                    pe.wait_ge(s_ce, 2)
                    pe.wait_ge(s_qTe, 4 * TILES)
                    pe.wait_ge(s_prjfree, CHUNKS * TILES)
                    pe.wait_ge(s_gbe, 1)

                    def score(v):
                        j, br, hd = units[v]
                        r = ROWS[j]
                        if v >= 2:
                            pe.wait_ge(s_P, v - 1)
                        part = slice(HD * (hd % 2), HD * (hd % 2) + HD)
                        b = 2 + 2 * (v % 2)
                        if br == 0:
                            q = qaT[part, hd // 2, COL[j]:COL[j] + r]
                            g = hd // (HEADS // KV)
                            if j == NT:
                                return pe.matmul(ps[0:r, b, 0:META], q, kaT[part, g, 0:META], start=True, stop=True)
                            lo_ = COL[j] - CHUNK if j else 0
                            n = COL[j] + P - lo_
                            pe.matmul(ps[:, b, 0:n], q, kaT[part, g, lo_:lo_ + n], start=True, stop=False)
                            return pe.matmul(ps[:, b, 0:n], identb[:, :], windowb[:, CHUNK + P - n:], start=False, stop=True)
                        q = qbT[part, hd // 2, COL[j]:COL[j] + r]
                        k = kbT[part, hd // 2, :]
                        pk = ident[0:HEADS, hd:hd + 1].broadcast_to((HEADS, r))
                        own_ = META if j == NT else P
                        pe.matmul(ps[0:r, b, 512 - META:512], q, k[:, 0:META], start=True, stop=False)
                        last = pe.matmul(ps[0:r, b, 512 - META:512], pk, ncTt[:, 0:META], start=False, stop=(j != NT))
                        if j == NT:
                            return pe.matmul(ps[0:r, b, 512 - META:512], identb[0:META, 0:META], causalb[0:META, 0:META],
                                             start=False, stop=True)
                        n = (j + 1) * P
                        pe.matmul(ps[:, b + 1, 0:n], q, k[:, META:META + n], start=True, stop=False)
                        pe.matmul(ps[:, b + 1, n - P:n], identb[:, :], causalb[:, :], start=False, stop=False,
                                  skip_group_check=True)
                        return pe.matmul(ps[:, b + 1, 0:n], pk, ncTt[:, META:META + n], start=False, stop=True)

                    def turn(n):
                        t = turns[n]
                        b = n % 2
                        if n >= 2:
                            pe.wait_ge(s_Te[b], n // 2)
                        if t["o"] is not None:
                            r = ROWS[units[t["o"]][0]]
                            pe.wait_ge(s_on, block_of(t["o"]) + 1)
                            for c in range(4):
                                last = pe.transpose(ps[:, b, c * P:c * P + r], osb[0:r, c * P:(c + 1) * P], ident[0:r, 0:r])
                            last.then_inc(s_T, 1)
                            return
                        v = t["unit"]
                        r = ROWS[units[v][0]]
                        pe.wait_ge(s_P, v + 1)
                        src = prob(v)
                        for k, (at, n_k, _) in enumerate(t["blocks"]):
                            last = pe.transpose(ps[0:n_k, b, k * P:k * P + r], src[0:r, at:at + n_k], ident[0:r, 0:r])
                        last.then_inc(s_T, 1)

                    def times_v(n):
                        t = turns[n]
                        b = n % 2
                        j, br, hd = units[t["unit"]]
                        r = ROWS[j]
                        pe.wait_ge(s_Te[b], n // 2 + 1)
                        if hd == 0 and t["first"] and block_of(t["unit"]) >= 2:
                            pe.wait_ge(s_on, block_of(t["unit"]) - 1)
                        for k, (_, n_k, tile) in enumerate(t["blocks"]):
                            vv = va[0:n_k, tile, HD * (hd // 4):HD * (hd // 4) + HD] if br == 0 else \
                                vb[0:n_k, tile, HD * hd:HD * (hd + 1)]
                            last = pe.matmul(ps[0:r, 6 + br, HD * hd:HD * (hd + 1)], PT[0:n_k, b, k * P:k * P + r], vv,
                                             start=(t["first"] and k == 0),
                                             stop=(t["last"] and k == len(t["blocks"]) - 1))
                        last.then_inc(s_PV, 1)

                    for v, st in enumerate(steps):
                        if st["score"] is not None:
                            score(v).then_inc(s_S, 1)
                        for n in st["turn"]:
                            turn(n)
                        for n in st["pv"]:
                            times_v(n)
                        if st["oturn"] is not None:
                            turn(st["oturn"])

                    for b in range(2):
                        pe.wait_ge(s_Te[b], (len(turns) + 1 - b) // 2)
                    pe.wait_ge(w_oa, 16)
                    pe.wait_ge(w_ob, 16)
                    woA = wslot[5][:, :].rearrange("p (c n) -> p c n", c=4)
                    woB = wslot[0][:, :].rearrange("p (c n) -> p c n", c=4)
                    for w in range(2 * KC):
                        n, half = divmod(w, 2)
                        s = 1 + n // 2
                        cols = slice(264 * half, 264 * (half + 1))
                        bank = 4 * (w % 2)
                        if n % 2 == 0 and half == 0:
                            for br in range(2):
                                pe.wait_ge(w_gates[s - 1][br], 16)
                        if w >= 2:
                            pe.wait_ge(s_mrg, w - 1)
                        wg = wslot[s][:, :].rearrange("p (c b n) -> p c b n", c=KC, b=2)
                        for br in range(2):
                            for k in range(KC):
                                last = pe.matmul(ps[:, bank + br, 0:264], wg[:, k, br, P * (n % 2):P * (n % 2) + P],
                                                 xT[:, k, cols], start=(k == 0), stop=(k == KC - 1))
                            last.then_inc(s_gy, 1)
                        for br, (wo_, oT) in enumerate(((woA, qaT), (woB, qbT))):
                            for k in range(4):
                                last = pe.matmul(ps[:, bank + 2 + br, 0:264], wo_[:, k, n * P:(n + 1) * P],
                                                 oT[:, k, cols], start=(k == 0), stop=(k == 3))
                            last.then_inc(s_gy, 1)
                    pe.wait_ge(s_mrg, 2 * KC)
                    for n in range(2):
                        pe.wait_ge(w_o[n], 16)
                    for i in range(TILES):
                        r = ROWS[i]
                        for half in range(2):
                            xu = 2 * i + half
                            if xu >= 2:
                                pe.wait_ge(s_res, xu - 1)
                            for k in range(KC):
                                w = wslot[1 + k // 4][:, :].rearrange("p (c n) -> p c n", c=4)
                                last = pe.matmul(ps[0:r, half, :], mrgT[:, k, COL[i]:COL[i] + r],
                                                 w[:, k % 4, 512 * half:512 * (half + 1)], start=(k == 0),
                                                 stop=(k == KC - 1))
                            last.then_inc(s_wo, 1)
                    for k in range(TILES):
                        r = ROWS[k]
                        turn_norm(1, k)
                        pe.wait_ge(s_xT, 2 * (TILES + k + 1))
                        for c in range(KC):
                            last = pe.matmul(ps[0:r, 4, 36 * k:36 * (k + 1)], xT[:, c, COL[k]:COL[k] + r], wr[:, c, :],
                                             start=(c == 0), stop=(c == KC - 1))
                        last.then_inc(s_lg, 1)
                    pe.wait_ge(s_M, 1)
                    for i in range(TILES):
                        r = ROWS[i]
                        for k in range(i):
                            pe.matmul(ps[0:r, 5, 32 * i:32 * (i + 1)], onesb[:, 0:r], Mb[:, k, :], start=(k == 0), stop=False)
                        pe.matmul(ps[0:r, 5, 32 * i:32 * (i + 1)], beforeb[0:r, 0:r], Mb[0:r, i, :], start=(i == 0), stop=True)
                    for i in range(TILES):
                        r = ROWS[i]
                        last = pe.matmul(ps[:, 5, 160:192], onesb[0:r, :], Mb[0:r, i, :], start=(i == 0), stop=(i == NT))
                    last.then_inc(s_rank, 1)
                    experts_tensor(pe)

                @block.vector
                def _(dve):
                    own = Own(dve, d_own)
                    link = own.link
                    dve.wait_ge(s_g1, 16)

                    def norms(q):
                        g = gainb
                        for k in range(TILES):
                            r = ROWS[k]
                            if q:
                                dve.wait_ge(s_res, 2 * (k + 1))
                            ins = dve.tensor_tensor_reduce(out=xsq[0:r, :], in0=h[0:r, k, :], in1=h[0:r, k, :], scale=1.0,
                                                           scalar=0.0, op0=ALU.mult, op1=ALU.add, accum_out=ss[0:r, k:k + 1])
                            ins.then_inc(s_ss, 1)
                            dve.wait_ge(s_ss, TILES * q + k + 1)
                        if q:
                            dve.wait_ge(s_g2, 16)
                        for k in range(TILES):
                            r = ROWS[k]
                            dve.wait_ge(s_rstd, TILES * q + k + 1)
                            if k >= 2:
                                dve.wait_ge(s_tp, 2 * (TILES * q + k - 1))
                                if q:
                                    dve.wait_ge(s_tst[k % 2], 16 * (k // 2))
                            dve.scalar_tensor_tensor(out=xn[0:r, k % 2, :], in0=h[0:r, k, :], scalar=rstd[0:r, k:k + 1],
                                                     in1=g[0:r, :], op0=ALU.mult, op1=ALU.mult).then_inc(s_xn, 1)

                    norms(0)
                    dve.wait_ge(s_par, 16 * 8)
                    for k in (0, 2):
                        link(dve.tensor_scalar(hgain[:, k, :], hgain[:, k, :], HD ** -0.5, None, ALU.mult))
                    link(dve.memset(frg[:, :, :, :], 0.0))
                    for u in range(CHUNKS * TILES):
                        c, i = divmod(u, TILES)
                        r = ROWS[i]
                        bank = ps[0:r, 2 + u % 3, :]
                        if c == CHUNKS - 1:
                            dve.wait_ge(s_prj, u + 1)
                            dve.tensor_copy(vb[0:r, i, :], bank).then_inc(s_prjfree, 1)
                            continue
                        nh = KV if c == 0 else HEADS
                        n = nh * HD
                        dve.wait_ge(s_sq, u + 1)
                        dve.tensor_reduce(hss[0:r, 0:nh], sq[0:r, 0:n].rearrange("p (h d) -> p h d", d=HD), AX,
                                          ALU.add).then_inc(s_hss, 1)
                        if c == 0:
                            dve.tensor_copy(va[0:r, i, :], bank[:, P:2 * P])
                            link(dve.tensor_copy(frg[0:r, 0, i, :], bank[:, 2 * P:2 * P + HEADS]))
                        dve.wait_ge(s_hr, u + 1)
                        y1 = qn1[0:r, 0:n].rearrange("p (h d) -> p h d", d=HD)
                        y2 = qn2[0:r, 0:n].rearrange("p (h d) -> p h d", d=HD)
                        dve.tensor_tensor(y1, bank[:, 0:n].rearrange("p (h d) -> p h d", d=HD),
                                          hr[0:r, 0:nh].unsqueeze(2).broadcast_to((r, nh, HD)), ALU.mult).then_inc(s_prjfree, 1)
                        dve.wait_ge(s_prjfree, u + 1)
                        if u >= 2:
                            dve.wait_ge(s_qT, u - 1)
                        gk = (1, 0, 2, 3)[c]
                        gb = hgain[0:r, gk, :].unsqueeze(1).broadcast_to((r, nh, HD))
                        dst = qnb[0:r, u % 2, :]
                        if c >= 2:
                            dve.tensor_tensor(dst.rearrange("p (h d) -> p h d", d=HD), y1, gb, ALU.mult).then_inc(s_qn, 1)
                            continue
                        link(dve.tensor_tensor(y2, y1, gb, ALU.mult))
                        link(dve.tensor_tensor(y1, y2, cosv[0:r, i, :].unsqueeze(1).broadcast_to((r, nh, HD)), ALU.mult))
                        sc = rot[0:r, 0:n].rearrange("p (h d) -> p h d", d=HD)
                        for a, b in ((0, 32), (32, 0)):
                            ins = dve.tensor_tensor(sc[:, :, a:a + 32], y2[:, :, b:b + 32],
                                                    sinv[0:r, i, a:a + 32].unsqueeze(1).broadcast_to((r, nh, 32)), ALU.mult)
                            link(ins)
                        if c == 0:
                            d4 = dst[:, 0:256].rearrange("p (h t d) -> p h t d", t=2, d=HD)
                            dve.tensor_tensor(d4, y1.unsqueeze(2).broadcast_to((r, nh, 2, HD)),
                                              sc.unsqueeze(2).broadcast_to((r, nh, 2, HD)), ALU.add).then_inc(s_qn, 1)
                        else:
                            dve.tensor_tensor(dst.rearrange("p (h d) -> p h d", d=HD), y1, sc, ALU.add).then_inc(s_qn, 1)
                        if u == TILES - 1:
                            z, az = frg[:, 0], frg[:, 1]
                            link(dve.tensor_tensor(z, z, fbias[:, :].unsqueeze(1).broadcast_to((P, TILES, HEADS)), ALU.add))
                            link(dve.tensor_scalar(az, z, -1.0, None, ALU.mult))
                            dve.tensor_tensor(az, z, az, ALU.max).then_inc(s_fz, 1)
                            dve.wait_ge(s_fz, 1)
                            link(dve.tensor_scalar(z, z, 0.0, None, ALU.min))
                        if u == TILES:
                            dve.wait_ge(s_fe, 2)
                            dve.tensor_tensor(frg[:, 0], frg[:, 0], frg[:, 3], ALU.subtract).then_inc(s_lf, 1)
                    dve.wait_ge(s_c, 1)
                    cps = ps[:, 5, 0:TILES * HEADS].rearrange("p (t n) -> p t n", t=TILES)
                    dve.tensor_copy(cso[:, 0:NT, :], cps[:, 0:NT, :])
                    dve.tensor_copy(cso[0:META, NT, :], cps[0:META, NT, :]).then_inc(s_ce, 1)
                    dve.wait_ge(s_c, 2)
                    dve.tensor_scalar(ncTt[:, META:POS], ps[0:HEADS, 6, :], -1.0, None, ALU.mult)
                    dve.tensor_scalar(ncTt[:, 0:META], ps[0:HEADS, 5, 64:64 + META], -1.0, None, ALU.mult).then_inc(s_ce, 1)
                    dve.wait_ge(s_qT, 4 * TILES)
                    link(dve.memset(PA[:, :, 0:CHUNK], 0.0))

                    for v, st in enumerate(steps):
                        if st["score"] is not None:
                            j, br, hd = units[v]
                            r = ROWS[j]
                            dve.wait_ge(s_S, v + 1)
                            link(dve.tensor_reduce(mx[0:r, v:v + 1], score_in(v), AX, ALU.max))
                            floor = sinks[0:r, hd:hd + 1] if br == 0 else LOWEST
                            dve.tensor_scalar(nm[0:r, v:v + 1], mx[0:r, v:v + 1], floor, -1.0, ALU.max,
                                              ALU.mult).then_inc(s_nm, 1)
                        for n in st["turn"] + ([st["oturn"]] if st["oturn"] is not None else []):
                            if n % 2 == 0:
                                dve.wait_ge(s_T, n + 1)
                                evacuate(dve, dve.tensor_copy, n).then_inc(s_Te[0], 1)
                        if st["norm"] is not None:
                            u = st["norm"]
                            j, br, _ = units[u]
                            r = ROWS[j]
                            v0 = u - HEADS + 1
                            blk = block_of(u)
                            dve.wait_ge(s_nm, u + 1)
                            dve.wait_ge(s_PV, pv_upto(u))
                            if br == 0:
                                dve.tensor_tensor(den[0:r, :], sinks[0:r, :], nm[0:r, v0:v0 + HEADS], ALU.add).then_inc(s_skin, 1)
                                dve.wait_ge(s_esk, blk // 2 + 1)
                                link(dve.tensor_tensor(den[0:r, :], esk[0:r, :], rs[0:r, v0:v0 + HEADS], ALU.add))
                                link(dve.reciprocal(rden[0:r, :], den[0:r, :]))
                            else:
                                link(dve.reciprocal(rden[0:r, :], rs[0:r, v0:v0 + HEADS]))
                            if blk >= 1:
                                dve.wait_ge(s_T, oturn_of[blk - 1] + 1)
                            dve.tensor_tensor(osb[0:r, :].rearrange("p (h d) -> p h d", d=HD),
                                              ps[0:r, 6 + br, :].rearrange("p (h d) -> p h d", d=HD),
                                              rden[0:r, :].unsqueeze(2).broadcast_to((r, HEADS, HD)),
                                              ALU.mult).then_inc(s_on, 1)

                    for w in range(2 * KC):
                        n, half = divmod(w, 2)
                        bank = 4 * (w % 2)
                        dve.wait_ge(s_gy, 4 * w + 4)
                        dve.wait_ge(s_sig, 2 * w + 2)
                        for br in range(2):
                            ins = dve.tensor_tensor(sig2(w, br), sig2(w, br), ps[:, bank + 2 + br, 0:264], ALU.mult)
                            link(ins)
                        dve.tensor_tensor(mrgT[:, n, 264 * half:264 * (half + 1)], sig2(w, 0), sig2(w, 1),
                                          ALU.add).then_inc(s_mrg, 1)
                    for i in range(TILES):
                        r = ROWS[i]
                        for half in range(2):
                            xu = 2 * i + half
                            hv = h[0:r, i, 512 * half:512 * (half + 1)]
                            dve.wait_ge(s_wo, xu + 1)
                            dve.tensor_tensor(hv, hv, ps[0:r, half, :], ALU.add).then_inc(s_res, 1)
                    norms(1)
                    def b3(a, n):
                        return a.unsqueeze(2).broadcast_to((P, TILES, n))

                    def first_max(src, top, eq, onehot, n):
                        down = C("down")[:, 0:n].unsqueeze(1).broadcast_to((P, TILES, n))
                        link(dve.tensor_reduce(top, src, AX, ALU.max))
                        link(dve.tensor_tensor(eq, src, b3(top, n), ALU.is_equal))
                        link(dve.tensor_tensor(eq, eq, down, ALU.mult))
                        link(dve.tensor_reduce(r_f, eq, AX, ALU.max))
                        link(dve.tensor_tensor(onehot, eq, b3(r_f, n), ALU.is_equal))

                    link(dve.memset(r_lg, 0.0))
                    dve.wait_ge(s_lg, TILES)
                    lgp = ps[:, 4, 0:36 * TILES].rearrange("p (t n) -> p t n", t=TILES)
                    link(dve.tensor_tensor(r_lg[:, 0:NT, :], lgp[:, 0:NT, :],
                                           rbias[:, :].unsqueeze(1).broadcast_to((P, NT, 36)), ALU.add))
                    link(dve.tensor_tensor(r_lg[0:META, NT, :], lgp[0:META, NT, :], rbias[0:META, :], ALU.add))
                    first_max(r_lg[:, :, 0:GROUPS], r_gm, r_eq, r_og, GROUPS)
                    dve.tensor_tensor(r_dg, r_lg[:, :, 0:GROUPS], b3(r_gm, GROUPS), ALU.subtract).then_inc(s_exl, 1)
                    og4 = r_og.unsqueeze(3).broadcast_to((P, TILES, GROUPS, PER))
                    sel4 = r_sel.rearrange("p t (g e) -> p t g e", g=GROUPS)
                    link(dve.tensor_tensor(sel4, r_lg[:, :, GROUPS:].rearrange("p t (g e) -> p t g e", g=GROUPS), og4,
                                           ALU.mult))
                    link(dve.tensor_reduce(r_ein, r_sel.rearrange("p t (g e) -> p t e g", g=GROUPS), AX, ALU.add))
                    first_max(r_ein, r_v1, r_w, r_o[0], PER)
                    link(dve.scalar_tensor_tensor(out=r_e2, in0=r_o[0], scalar=LOWEST, in1=r_ein, op0=ALU.mult, op1=ALU.add))
                    first_max(r_e2, r_v2, r_w, r_o[1], PER)
                    dve.tensor_tensor(r_d, r_v2, r_v1, ALU.subtract).then_inc(s_exl, 1)
                    for a in range(2):
                        link(dve.tensor_tensor(work_M[:, a].rearrange("p t (g e) -> p t g e", g=GROUPS), og4,
                                               r_o[a].unsqueeze(2).broadcast_to((P, TILES, GROUPS, PER)), ALU.mult))
                    dve.tensor_tensor(Mb[:, :, :], work_M[:, 0], work_M[:, 1], ALU.add).then_inc(s_M, 1)
                    dve.wait_ge(s_exd, 2)
                    link(dve.tensor_reduce(r_sum, r_dg, AX, ALU.add))
                    link(dve.reciprocal(r_pg, r_sum))
                    link(dve.tensor_scalar(r_den, r_d, 1.0, None, ALU.add))
                    link(dve.reciprocal(r_den, r_den))
                    link(dve.tensor_tensor(r_g[0], r_den, r_pg, ALU.mult))
                    link(dve.tensor_tensor(r_g[1], r_g[0], r_d, ALU.mult))
                    link(dve.memset(work_R[:, 0], 0.0))
                    dve.wait_ge(s_rank, 1)
                    rkp = ps[:, 5, 0:32 * TILES].rearrange("p (t n) -> p t n", t=TILES)
                    dve.tensor_copy(work_R[:, 0, 0:NT, :], rkp[:, 0:NT, :])
                    link(dve.tensor_copy(work_R[0:META, 0, NT, :], rkp[0:META, NT, :]))
                    ebase = C("ebase").unsqueeze(1).broadcast_to((P, TILES, EXPERTS))
                    for a in range(2):
                        link(dve.tensor_tensor(work_R[:, 1], work_M[:, a], work_R[:, 0], ALU.mult))
                        link(dve.tensor_reduce(r_rank, work_R[:, 1], AX, ALU.add))
                        link(dve.tensor_tensor(work_R[:, 1], work_M[:, a], ebase, ALU.mult))
                        link(dve.tensor_reduce(r_at, work_R[:, 1], AX, ALU.add))
                        link(dve.tensor_copy(r_ri, r_rank))
                        link(dve.tensor_scalar(r_ri, r_ri, 6, None, ALU.arith_shift_right))
                        link(dve.tensor_copy(r_hf, r_ri))
                        link(dve.scalar_tensor_tensor(out=r_slot, in0=r_rank, scalar=float(PAIRS), in1=r_at, op0=ALU.mult,
                                                      op1=ALU.add))
                        link(dve.scalar_tensor_tensor(out=slot_at[:, a, :], in0=r_hf, scalar=float(CAP * PAIRS), in1=r_slot,
                                                      op0=ALU.mult, op1=ALU.add))
                        link(dve.tensor_copy(ent[:, a, :, 0], C("row")))
                        link(dve.tensor_scalar(ent[:, a, :, 1], C("row"), float(a * TILES * P), None, ALU.add))
                        link(dve.tensor_copy(ent[:, a, :, 2].bitcast(F32), r_g[a]))
                        link(dve.tensor_copy(ent[:, a, :, 3], C("row")))
                    link(dve.tensor_reduce(r_cm[0:1, 0:1], ps[0:1, 5, 160:192], AX, ALU.max))
                    link(dve.tensor_scalar(r_ci[0:1, 0:1], r_cm[0:1, 0:1], CAP - 1.0, None, ALU.add))
                    dve.tensor_scalar(cnt[0:1, 0:1], r_ci[0:1, 0:1], 6, None, ALU.arith_shift_right).then_inc(s_ent, 1)
                    experts_vector(dve)

            clear_all()

            rounds = nc.values_load(cnt[0:1, 0:1], min_val=1, max_val=ROUNDS)
            with nc.If(rounds > 1):
                with nc.Fori(1, rounds) as rnd:
                    with nc.Block() as block:
                        @block.sync
                        def _(sp):
                            for w, par, s in ORDER:
                                load_expert(sp, w, slice(par, par + 1), s)
                            experts_sync(sp)

                        @block.gpsimd
                        def _(pool):
                            load_table(pool, tab_dram.rearrange("(r p m) c -> r p (m c)", p=P, m=PAIRS)[
                                bass.ds(rnd, 1)].rearrange("r p n -> (r p) n"))
                            experts_pool(pool)

                        @block.scalar
                        def _(act):
                            experts_scalar(act)

                        @block.tensor
                        def _(pe):
                            experts_tensor(pe)

                        @block.vector
                        def _(dve):
                            experts_vector(dve)
                    clear_all()

            with nc.Block() as block:
                @block.sync
                def _(sp):
                    for i in range(TILES):
                        for a in range(2):
                            at = (a * TILES + i) * P
                            sp.dma_start(wslot[i][0:ROWS[i], a * D:(a + 1) * D], y_dram[at:at + ROWS[i], :]).then_inc(y_in[i], 16)
                    sp.wait_ge(s_tab0, 1)
                    sp.dma_start(tab_dram.rearrange("(p r) c -> p (r c)", p=P), blank).then_inc(s_blank, 16)
                    sp.wait_ge(s_blank, 16)

                @block.gpsimd
                def _(pool):
                    pool.memset(blank, NOWHERE).then_inc(s_tab0, 1)

                @block.vector
                def _(dve):
                    for i in range(TILES):
                        r_ = ROWS[i]
                        dve.wait_ge(y_in[i], 32)
                        for a in range(2):
                            dve.tensor_tensor(h[0:r_, i, :], h[0:r_, i, :], wslot[i][0:r_, a * D:(a + 1) * D],
                                              ALU.add).then_inc(y_add, 1)
                            dve.wait_ge(y_add, 2 * i + a + 1)
            clear_all()

        with nc.Fori(0, DEPTH) as l:
            layer(l)

        with nc.Block() as block:
            @block.sync
            def _(sp):
                for i in range(NT):
                    sp.dma_start(out[0, i * P:(i + 1) * P, :], h[:, i, :]).then_inc(s_out, 16)
                sp.wait_ge(s_out, 16 * NT)


INPUTS = ["x", "meta_tokens", "norm1_g", "w_in", "qk_gain", "attn_sinks", "b_forget", "b_merge", "w_o_swa", "w_o_fox",
          "w_out", "norm2_g", "w_router_group", "b_router_group", "w_router_expert", "b_router_expert", "w_exp_gate",
          "w_exp_up", "w_exp_down"]


def kernel(**inputs):
    import concourse.bacc as bacc
    from concourse.bass_utils import run_bass_kernel_spmd

    nc = bacc.Bacc("TRN2", target_bir_lowering=False, num_devices=1)
    arrays = {f"in_{name}": np.ascontiguousarray(inputs[name]) for name in INPUTS}
    arrays["in_constants"] = constants()
    args = [nc.dram_tensor(name, a.shape, F32, kind="ExternalInput").ap() for name, a in arrays.items()]
    out = nc.dram_tensor("out_0", (1, SEQ, D), F32, kind="ExternalOutput").ap()
    trunk_kernel(nc, *args, out)
    result = run_bass_kernel_spmd(nc, [arrays], core_ids=[0])
    return result.results[0]["out_0"]
```

```python
from contextlib import ExitStack

import concourse.bass as bass
import numpy as np
from concourse import mybir

F32 = mybir.dt.float32
BF16 = mybir.dt.bfloat16
I32 = mybir.dt.int32
U32 = mybir.dt.uint32
ALU = mybir.AluOpType
ACT = mybir.ActivationFunctionType
AX = mybir.AxisListType.X

P = 128
D = 1024
SEQ = 512
META = 16
POS = SEQ + META
DEPTH = 2
HD = 64
HEADS = 8
KV = 2
CHUNK = 64
NT = SEQ // P
TILES = NT + 1
KC = D // P
EPS = 1e-6
NEG = -1e30
LOWEST = -3.0e38
THETA = 10000.0

W_KV = HEADS * HD
W_QB = W_KV + 2 * KV * HD
W_KB = W_QB + 512
W_VB = W_KB + 512
W_F = W_VB + 512
W_G = W_F + HEADS

GROUPS = 4
PER = 8
EXPERTS = GROUPS * PER
FF = 512
FC = FF // P
PAIRS = EXPERTS // 2
CAP = 64
ROUNDS = -(-POS // CAP)
TAB = ROUNDS * P * PAIRS
NOWHERE = 1 << 20
YROWS = 2 * TILES * P

ROWS = [P] * NT + [META]
COL = [META + P * i for i in range(NT)] + [0]

EARLY = 24
FILL = (2, 2, 2, 1, 1)
HALF = POS // 2

CONST = {}


def constants():
    cols = []

    def put(name, a):
        a = np.asarray(a, np.float32)
        full = np.zeros((P, a.shape[1]), np.float32)
        full[:a.shape[0]] = a
        at = sum(c.shape[1] for c in cols)
        CONST[name] = (at, a.shape[1])
        cols.append(full)

    k = np.arange(P)
    put("ident", np.eye(P))
    put("upto", k[:, None] <= k[None, :])
    put("before", k[:, None] < k[None, :])
    put("ones", np.ones((P, P)))
    put("causal", np.where(k[None, :] > k[:, None], NEG, 0.0))
    key = np.arange(CHUNK + P)
    masked = np.where(k[:, None] < CHUNK, key[None, :] >= 2 * CHUNK, key[None, :] < CHUNK)
    put("window", np.where(masked, NEG, 0.0))
    inv = np.power(np.float32(THETA), -np.arange(0, HD, 2, dtype=np.float32) / np.float32(HD)).astype(np.float32)
    cos, sin = np.zeros((P, TILES, HD), np.float32), np.zeros((P, TILES, HD), np.float32)
    for i in range(TILES):
        ang = (COL[i] + k).astype(np.float32)[:, None] * inv[None, :]
        cos[:, i] = np.concatenate([np.cos(ang), np.cos(ang)], 1)
        sin[:, i] = np.concatenate([-np.sin(ang), np.sin(ang)], 1)
    put("cos", cos.reshape(P, -1))
    put("sin", sin.reshape(P, -1))
    put("down", np.tile(PER - np.arange(PER), (P, 1)))
    e = np.arange(EXPERTS)
    put("ebase", np.tile((e % 2) * CAP * PAIRS + e // 2, (P, 1)))
    put("pick", np.arange(3 * HEADS)[:, None] % HEADS == np.arange(HEADS)[None, :])
    put("row", np.arange(TILES)[None, :] * P + k[:, None])
    return np.concatenate(cols, 1)


NCONST = constants().shape[1]


def attention_plan():
    units = [(j, br, h) for j in [NT] + list(range(NT)) for br in (0, 1) for h in range(HEADS)]
    steps, turns, pvs = [], [], 0
    for v in range(len(units) + 6):
        st = {"score": v if v < len(units) else None, "turn": [], "pv": [], "norm": None, "oturn": None}
        if 0 <= v - 2 < len(units):
            j, br, h = units[v - 2]
            if br == 0:
                if j == NT:
                    sets = [[(P - META, META, NT)]]
                elif j == 0:
                    sets = [[(P, P, 0)], [(P - META, META, NT)]]
                else:
                    sets = [[(0, P, j - 1), (P, P, j)]]
            elif j == NT:
                sets = [[(0, META, NT)]]
            else:
                sets = [[(COL[i], P, i) for i in range(j + 1)], [(0, META, NT)]]
            for n, s in enumerate(sets):
                st["turn"].append(len(turns))
                turns.append({"unit": v - 2, "blocks": s, "first": n == 0, "last": n == len(sets) - 1, "o": None})
        if 0 <= v - 3 < len(units):
            st["pv"] = [n for n, t in enumerate(turns) if t["unit"] == v - 3]
        if 0 <= v - 4 < len(units) and units[v - 4][2] == HEADS - 1:
            st["norm"] = v - 4
        if 0 <= v - 5 < len(units) and units[v - 5][2] == HEADS - 1:
            st["oturn"] = len(turns)
            turns.append({"unit": None, "blocks": None, "o": v - 5})
        steps.append(st)
    for st in steps:
        st["fill"], st["fill_out"] = [[], []], None
    for g in range(EARLY):
        place, k = 2 * len(units) * g // EARLY, 0
        for m in FILL:
            steps[place // 2]["fill"][place % 2] = [(g, k + a) for a in range(m)]
            k += m
            place += 1
        steps[(place - 1) // 2]["fill_out"] = g
    for st in steps:
        for n in st["pv"]:
            pvs += 1
            turns[n]["pv_count"] = pvs
    return units, steps, turns


def trunk_kernel(nc, x, meta_tokens, norm1_g, w_in, qk_gain, attn_sinks, b_forget, b_merge, w_o_swa, w_o_fox, w_out,
                 norm2_g, w_router_group, b_router_group, w_router_expert, b_router_expert,
                 w_exp_gate, w_exp_up, w_exp_down, const, out):
    ctx = ExitStack()
    with ctx:
        def sb(name, shape, dt=F32):
            return ctx.enter_context(nc.sbuf_tensor(name, shape, dt))

        def sem(name):
            s = ctx.enter_context(nc.semaphore(name))
            sems.append(s)
            return s

        sems = []
        t_dram = nc.dram_tensor("t_rows", (POS, D), F32, kind="Internal").ap()
        y_dram = nc.dram_tensor("y_rows", (YROWS, D), F32, kind="Internal").ap()
        tab_dram = nc.dram_tensor("slot_table", (TAB, 4), U32, kind="Internal").ap()

        cst = sb("cst", [P, NCONST])

        def C(name):
            at, n = CONST[name]
            return cst[:, at:at + n]

        ident, upto, ones = C("ident"), C("upto"), C("ones")
        cosv = C("cos").rearrange("p (t d) -> p t d", d=HD)
        sinv = C("sin").rearrange("p (t d) -> p t d", d=HD)
        identb = sb("identb", [P, P], BF16)
        causalb = sb("causalb", [P, P], BF16)
        windowb = sb("windowb", [P, CHUNK + P], BF16)
        beforeb = sb("beforeb", [P, P], BF16)
        onesb = sb("onesb", [P, P], BF16)
        SLOT = 4096
        wslot = [sb(f"wslot{s}", [P, SLOT]) for s in range(6)]
        h = sb("h", [P, TILES, D])
        xT = sb("xT", [P, KC, POS])
        gainb = sb("gainb", [P, D])
        wr = sb("wr", [P, KC, GROUPS + EXPERTS])
        rbias = sb("rbias", [P, GROUPS + EXPERTS])
        hgain = sb("hgain", [P, 4, HD])
        sinks = sb("sinks", [P, HEADS])
        fbias = sb("fbias", [P, HEADS])
        gbias_rows = sb("gbias_rows", [2 * KC, P])
        gbias = sb("gbias", [P, 2 * KC])
        halfneg = sb("halfneg", [P, HEADS])
        small = sb("small", [P, 160])
        qaT = sb("qaT", [P, 4, POS])
        qbT = sb("qbT", [P, 4, POS])
        arena = sb("arena", [P, 4 * POS + TILES * 512])
        kbT = arena[:, 0:4 * POS].rearrange("p (c n) -> p c n", c=4)
        vb = arena[:, 4 * POS:4 * POS + TILES * 512].rearrange("p (t n) -> p t n", t=TILES)
        vbf = arena[:, 4 * POS:4 * POS + TILES * 512]
        mrgT = arena[:, 0:KC * POS].rearrange("p (c n) -> p c n", c=KC)
        kaT = sb("kaT", [P, KV, POS])
        va = sb("va", [P, TILES, KV * HD])
        work = sb("work", [P, 3104])
        tabs = sb("tabs", [P, PAIRS + 1, 4], U32)
        cnt = sb("cnt", [1, 2], I32)
        idx_g = sb("idx_g", [P, 1], U32)
        idx_s = sb("idx_s", [P, 1], U32)
        gcol = sb("gcol", [P, 1])

        qaf, qbf = (t[:, :, :].rearrange("p c n -> p (c n)") for t in (qaT, qbT))
        kaf = kaT[:, :, :].rearrange("p c n -> p (c n)")
        xn = [qaf[:, 0:D], qaf[:, D:2 * D], kaf[:, 0:D], work[:, 0:D], work[:, 1700:1700 + D]]
        xsq = qbf[:, 0:D]
        sq, qn1, qn2, rot = (work[:, 512 * k:512 * (k + 1)] for k in range(4))
        qnb = work[:, 2048:3072].rearrange("p (b n) -> p b n", b=2)
        PA = work[:, 0:512].rearrange("p (b n) -> p b n", b=2)
        PF = work[:, 512:512 + 2 * POS].rearrange("p (b n) -> p b n", b=2)
        PT = work[:, 1568:2592].rearrange("p (b n) -> p b n", b=2)
        osb = work[:, 2592:3104]
        sig = work[:, 0:4 * HALF].rearrange("p (k n) -> p k n", k=4)
        rbuf = qbf[:, D:2 * D + 64]
        xg = arena[:, 0:D]
        xgT = arena[:, D:2 * D].rearrange("p (c n) -> p c n", c=KC)
        sg = arena[:, 2048:2560]
        hh = arena[:, 2560:3072]
        hT = arena[:, 3072:3584].rearrange("p (c n) -> p c n", c=FC)
        ysb = arena[:, 3584:4608]

        ss, rstd = small[:, 0:8], small[:, 8:16]
        hss, hr = small[:, 16:24], small[:, 24:32]
        stat = sb("stat", [P, 3, 80])
        mx, nm, rs = stat[:, 0, :], stat[:, 1, :], stat[:, 2, :]
        esk, den, rden = small[:, 32:40], small[:, 40:48], small[:, 48:56]
        frg = sb("frg", [P, 4, TILES, HEADS])
        cso = sb("cso", [P, TILES, HEADS])
        cres = sb("cres", [P, TILES, HEADS])
        cpart = sb("cpart", [P, TILES, 3, HEADS])
        cpartb = sb("cpartb", [P, TILES, HEADS], BF16)
        nc3 = sb("nc3", [3 * HEADS, POS], BF16)
        pickb = sb("pickb", [3 * HEADS, HEADS], BF16)

        ps = ctx.enter_context(nc.psum_tensor("ps", [P, 8, 512], F32))

        s_in = sem("s_in")
        s_cst = sem("s_cst")
        s_tab0 = sem("s_tab0")
        loaded = [sem(f"loaded{s}") for s in range(6)]
        w_qkv = [sem(f"w_qkv{k}") for k in range(5)]
        w_f = sem("w_f")
        w_gates = [[sem(f"w_gates{k}_{br}") for br in range(2)] for k in range(4)]
        w_oa, w_ob = sem("w_oa"), sem("w_ob")
        w_o = [sem(f"w_o{k}") for k in range(2)]
        freed = [sem(f"freed{s}") for s in range(6)]
        s_par = sem("s_par")
        s_g1 = sem("s_g1")
        s_g2 = sem("s_g2")
        s_ss = sem("s_ss")
        s_rstd = sem("s_rstd")
        s_xn = sem("s_xn")
        s_tp = sem("s_tp")
        s_xT = sem("s_xT")
        s_tst = sem("s_tst")
        s_h = sem("s_h")
        s_gb = sem("s_gb")
        s_gbe = sem("s_gbe")
        s_prj = sem("s_prj")
        s_prjfree = sem("s_prjfree")
        s_sq = sem("s_sq")
        s_hss = sem("s_hss")
        s_hr = sem("s_hr")
        s_qn = sem("s_qn")
        s_qT = sem("s_qT")
        s_qTe = sem("s_qTe")
        s_fz = sem("s_fz")
        s_fe = sem("s_fe")
        s_lf = sem("s_lf")
        s_c = sem("s_c")
        s_ce = sem("s_ce")
        s_S = sem("s_S")
        s_nm = sem("s_nm")
        s_P = sem("s_P")
        s_T = sem("s_T")
        s_Te = [sem(f"s_Te{b}") for b in range(2)]
        s_PV = sem("s_PV")
        s_skin = sem("s_skin")
        s_esk = sem("s_esk")
        s_on = sem("s_on")
        s_z = sem("s_z")
        s_zo = [sem(f"s_zo{k}") for k in range(2)]
        s_gate = sem("s_gate")
        s_y = sem("s_y")
        s_sig = sem("s_sig")
        s_mrg = sem("s_mrg")
        s_wo = sem("s_wo")
        s_res = sem("s_res")
        s_lg = sem("s_lg")
        s_M = sem("s_M")
        s_rank = sem("s_rank")
        s_exl = sem("s_exl")
        s_exd = sem("s_exd")
        s_ent = sem("s_ent")
        s_scat = sem("s_scat")
        s_tabl = sem("s_tabl")
        e_blank = sem("e_blank")
        e_st = sem("e_st")
        e_idx = sem("e_idx")
        e_gath = sem("e_gath")
        e_xgT = sem("e_xgT")
        e_xT = sem("e_xT")
        e_sg = sem("e_sg")
        e_h = sem("e_h")
        e_hT = sem("e_hT")
        e_hTe = sem("e_hTe")
        e_y = sem("e_y")
        e_scat = sem("e_scat")
        y_in = [sem(f"y_in{i}") for i in range(TILES)]
        y_add = sem("y_add")
        s_blank = sem("s_blank")
        s_out = sem("s_out")
        d_own = sem("d_own")
        p_own = sem("p_own")
        a_own = sem("a_own")
        lo, hi = min(s.num for s in sems), max(s.num for s in sems)
        assert hi - lo + 1 == len(sems)

        blank = vbf[:, 0:TAB * 4 // P].bitcast(U32)

        def y_tile(i, a):
            if i == NT:
                return arena[0:META, a * D:(a + 1) * D]
            return wslot[4 + i // 2][:, (2 * (i % 2) + a) * D:(2 * (i % 2) + a + 1) * D]

        def clear_all():
            nc.all_engine_barrier()
            with nc.Block() as block:
                @block.gpsimd
                def _(pool):
                    pool.dma_reset(range(lo, hi + 1))
                    pool.sem_clear(range(lo, hi + 1))
            nc.all_engine_barrier()

        class Own:

            def __init__(self, eng, s):
                self.eng, self.s, self.n = eng, s, 0

            def link(self, ins):
                self.n += 1
                ins.then_inc(self.s, 1)
                self.eng.wait_ge(self.s, self.n)

        with nc.Block() as block:
            @block.sync
            def _(sp):
                sp.dma_start(cst[:, :], const).then_inc(s_in, 16)
                for i in range(NT):
                    sp.dma_start(h[:, i, :], x[0, i * P:(i + 1) * P, :]).then_inc(s_in, 16)
                sp.dma_start(h[0:META, NT, :], meta_tokens).then_inc(s_in, 16)
                sp.wait_ge(s_in, 16 * (TILES + 1))

            @block.gpsimd
            def _(pool):
                pool.memset(halfneg[:, :], -0.5)
                pool.memset(tabs[:, :, :], NOWHERE)

            @block.vector
            def _(dve):
                dve.wait_ge(s_in, 16 * (TILES + 1))
                for dst, name in ((identb, "ident"), (causalb, "causal"), (windowb, "window"), (beforeb, "before"),
                                  (onesb, "ones")):
                    dve.tensor_copy(dst[:, :], C(name))
                dve.tensor_copy(pickb[:, :], C("pick")[0:3 * HEADS, :])
        clear_all()

        units, steps, turns = attention_plan()
        last_turn = {t["unit"]: n for n, t in enumerate(turns) if t["unit"] is not None}
        oturn_of = {t["o"] // HEADS: n for n, t in enumerate(turns) if t["o"] is not None}

        def block_of(v):
            return v // HEADS

        def pv_upto(v):
            return turns[last_turn[v]]["pv_count"]

        psf = ps[:, :, :].rearrange("p b n -> p (b n)")

        def keys_of(v):
            j, br, _ = units[v]
            if j == NT:
                return META
            return (COL[j] + P if br else (CHUNK if j else META) + P)

        def score_in(v):
            j, br, _ = units[v]
            at = 512 * (2 + 2 * (v % 2)) + (512 - META if br else 0)
            return psf[0:ROWS[j], at:at + keys_of(v)]

        def prob(v):
            return (PF if units[v][1] else PA)[:, v % 2, :]

        def prob_out(v):
            j, br, _ = units[v]
            n = keys_of(v)
            at = 0 if br else (P - META if j == NT else 2 * P - n)
            return prob(v)[0:ROWS[j], at:at + n]

        def evacuate(eng, copy, n):
            t, b = turns[n], n % 2
            src = ps[:, b, :].rearrange("p (c n) -> p c n", c=4)
            if t["o"] is not None:
                j, br, _ = units[t["o"]]
                return copy((qaT, qbT)[br][:, :, COL[j]:COL[j] + ROWS[j]], src[:, :, 0:ROWS[j]])
            r, nk, nb = ROWS[units[t["unit"]][0]], t["blocks"][0][1], len(t["blocks"])
            before = [m for m in range(n % 2, n, 2) if turns[m]["o"] is None]
            if before:
                eng.wait_ge(s_PV, turns[before[-1]]["pv_count"])
            return copy(PT[0:nk, b, :].rearrange("p (c n) -> p c n", c=4)[:, 0:nb, 0:r], src[0:nk, 0:nb, 0:r])

        def sig2(w, br):
            return sig[:, 2 * (w % 2) + br, :]

        def z_at(g):
            s, k = divmod(g, wslot[0].shape[1] // HALF)
            return wslot[s][:, HALF * k:HALF * (k + 1)]

        def fill_out(eng, copy, g):
            eng.wait_ge(s_z, g + 1)
            copy(z_at(g), ps[:, 7, 0:HALF]).then_inc(s_zo[g % 2], 1)

        CHUNKS = 5

        r_n = [0]

        def r(shape, dt=F32):
            n = int(np.prod(shape))
            at = r_n[0]
            r_n[0] += n
            assert r_n[0] <= 2 * D - D + 64
            v = rbuf[:, at:at + n]
            if dt != F32:
                v = v.bitcast(dt)
            names = "abc"[:len(shape)]
            if len(shape) == 1:
                return v
            return v.rearrange("p (" + " ".join(names) + ") -> p " + " ".join(names),
                               **{k: n_ for k, n_ in zip(names[1:], shape[1:])})

        r_lg = r((TILES, GROUPS + EXPERTS))
        r_gm, r_f, r_sum, r_pg, r_v1, r_v2, r_d, r_den = (r((TILES,)) for _ in range(8))
        r_dg, r_eq, r_og = (r((TILES, GROUPS)) for _ in range(3))
        r_sel = r((TILES, EXPERTS))
        r_ein, r_e2, r_w = (r((TILES, PER)) for _ in range(3))
        r_o = [r((TILES, PER)) for _ in range(2)]
        r_g = [r((TILES,)) for _ in range(2)]
        r_rank, r_at, r_hf, r_slot = (r((TILES,)) for _ in range(4))
        r_ri = r((TILES,), I32)
        r_cm, r_ci = r((2,)), r((2,), I32)
        ent = sb("ent", [P, 2, TILES, 4], U32)
        slot_at = sb("slot_at", [P, 2, TILES], U32)
        Mb = sb("Mb", [P, TILES, EXPERTS], BF16)

        work_M = work[:, 1056:1056 + 2 * TILES * EXPERTS].rearrange("p (a t n) -> p a t n", a=2, t=TILES)
        work_R = work[:, 1376:1376 + 2 * TILES * EXPERTS].rearrange("p (a t n) -> p a t n", a=2, t=TILES)

        def layer(l):
            def L(a):
                return a[bass.ds(l, 1)]

            ORDER = ((w_exp_gate, 0, 3), (w_exp_gate, 1, 0), (w_exp_up, 0, 4), (w_exp_up, 1, 1),
                     (w_exp_down, 0, 5), (w_exp_down, 1, 2))

            def load_expert(sp, w, e, s):
                src = w[bass.ds(l, 1), e]
                if w is w_exp_down:
                    sp.dma_start(wslot[s][:, :].rearrange("p (c n) -> p c n", c=FC),
                                 src.rearrange("a b (c p) n -> p (a b c) n", p=P)).then_inc(loaded[s], 16)
                else:
                    sp.dma_start(wslot[s][:, :], src.rearrange("a b (p c) n -> p (a b c n)", p=P)).then_inc(loaded[s], 16)

            def experts_sync(sp):
                with sp.Fori(1, PAIRS) as i:
                    for w, par, s in ORDER:
                        sp.wait_ge(freed[s], i)
                        load_expert(sp, w, bass.ds(2 * i + par, 1), s)

            def experts_pool(pool):
                token_bound = pool.to_reg(POS - 1)
                row_bound = pool.to_reg(YROWS - 1)

                def stage(idx, col, k):
                    pool.tensor_copy(idx[:, :], tabs[:, col, k:k + 1]).then_inc(e_idx, 1)
                    pool.wait_ge(e_idx, 1)
                    pool.sem_clear(e_idx)

                def gather(col):
                    stage(idx_g, col, 0)
                    pool.indirect_dma_start(out=xg, out_offset=None, in_=t_dram,
                                            in_offset=bass.IndirectOffsetOnAxis(ap=idx_g[:, 0:1], axis=0),
                                            bounds_check=token_bound, oob_is_err=False).then_inc(e_gath, 16)

                def scatter(i, first):
                    if not first:
                        pool.wait_ge(e_scat, 16 * i)
                    pool.tensor_copy(gcol[:, :], tabs[:, slice(0, 1) if first else bass.ds(i, 1), 2:3].bitcast(F32)).then_inc(e_st, 1)
                    pool.wait_ge(e_y, 2 * (i + 1))
                    stage(idx_s, slice(0, 1) if first else bass.ds(i, 1), 1)
                    pool.indirect_dma_start(out=y_dram, out_offset=bass.IndirectOffsetOnAxis(ap=idx_s[:, 0:1], axis=0),
                                            in_=ysb, in_offset=None, bounds_check=row_bound,
                                            oob_is_err=False).then_inc(e_scat, 16)

                def next_gather(i):
                    pool.wait_ge(e_gath, 16 * (i + 1))
                    pool.wait_ge(e_xgT, i + 1)
                    gather(slice(1, 2) if isinstance(i, int) else bass.ds(i + 1, 1))

                pool.memset(xg, 0.0).then_inc(e_blank, 1)
                pool.wait_ge(e_blank, 1)
                gather(slice(0, 1))
                next_gather(0)
                scatter(0, True)
                with pool.Fori(1, PAIRS) as i:
                    next_gather(i)
                    scatter(i, False)
                pool.wait_ge(e_gath, 16 * (PAIRS + 1))
                pool.wait_ge(e_scat, 16 * PAIRS)

            def experts_tensor(pe):
                def turn_tokens():
                    for c in range(KC):
                        last = pe.transpose(ps[:, 6 + c // 4, (c % 4) * P:(c % 4 + 1) * P], xg[:, c::KC], ident)
                    last.then_inc(e_xgT, 1)

                pe.wait_ge(e_gath, 16)
                turn_tokens()
                with pe.Fori(0, PAIRS) as i:
                    pe.wait_ge(e_xT, 2 * (i + 1))
                    for bank, pair in ((0, (3, 0)), (1, (4, 1))):
                        wa, wb = (wslot[s][:, :].rearrange("p (c n) -> p c n", c=KC) for s in pair)
                        for s in pair:
                            pe.wait_ge(loaded[s], 16 * (i + 1))
                        for c in range(KC):
                            for par, w in ((0, wa), (1, wb)):
                                last = pe.matmul(ps[CAP * par:CAP * (par + 1), bank, :],
                                                 xgT[:, c, CAP * par:CAP * (par + 1)], w[:, c, :],
                                                 start=(c == 0), stop=(c == KC - 1))
                                if c == KC - 1:
                                    last.then_inc(freed[pair[par]], 1)
                    pe.wait_ge(e_h, i + 1)
                    for c in range(FC):
                        last = pe.transpose(ps[:, 4, c * P:(c + 1) * P], hh[:, c * P:(c + 1) * P], ident)
                    last.then_inc(e_hT, 1)
                    pe.wait_ge(e_hTe, i + 1)
                    pe.wait_ge(e_st, i + 1)
                    for s in (5, 2):
                        pe.wait_ge(loaded[s], 16 * (i + 1))
                    for half in range(2):
                        for c in range(FC):
                            for par, s in ((0, 5), (1, 2)):
                                w = wslot[s][:, :].rearrange("p (c n) -> p c n", c=FC)
                                last = pe.matmul(ps[CAP * par:CAP * (par + 1), 2 + half, :],
                                                 hT[:, c, CAP * par:CAP * (par + 1)],
                                                 w[:, c, half * 512:(half + 1) * 512],
                                                 start=(c == 0), stop=(c == FC - 1))
                                if half == 1 and c == FC - 1:
                                    last.then_inc(freed[s], 1)
                    pe.wait_ge(e_gath, 16 * (i + 2))
                    turn_tokens()

            def experts_scalar(act):
                def tokens_out(i):
                    act.wait_ge(e_xgT, i)
                    for k in range(2):
                        act.copy(xgT[:, 4 * k:4 * k + 4, :].rearrange("p c n -> p (c n)"), ps[:, 6 + k, :]).then_inc(e_xT, 1)

                tokens_out(1)
                with act.Fori(0, PAIRS) as i:
                    act.wait_ge(freed[0], i + 1)
                    act.activation(sg, ps[:, 0, :], ACT.Silu).then_inc(e_sg, 1)
                    act.wait_ge(freed[1], i + 1)
                    tokens_out(i + 2)

            def experts_vector(dve):
                with dve.Fori(0, PAIRS) as i:
                    dve.wait_ge(e_sg, i + 1)
                    dve.wait_ge(freed[1], i + 1)
                    dve.tensor_tensor(hh, sg, ps[:, 1, :], ALU.mult).then_inc(e_h, 1)
                    dve.wait_ge(e_hT, i + 1)
                    dve.tensor_copy(hT.rearrange("p c n -> p (c n)"), ps[:, 4, :]).then_inc(e_hTe, 1)
                    dve.wait_ge(freed[2], i + 1)
                    dve.wait_ge(e_st, i + 1)
                    for half in range(2):
                        dve.tensor_scalar(ysb[:, half * 512:(half + 1) * 512], ps[:, 2 + half, :], gcol[:, 0:1], None,
                                          ALU.mult).then_inc(e_y, 1)

            def load_table(pool, rows):
                pool.dma_start(tabs[:, 0:PAIRS, :].rearrange("p m c -> p (m c)"), rows).then_inc(s_tabl, 16)
                pool.wait_ge(s_tabl, 16)

            with nc.Block() as block:
                @block.sync
                def _(sp):
                    w3 = w_in[bass.ds(l, 1)].rearrange("a (p c) n -> p (a c) n", p=P)
                    wo_a = L(w_o_swa).rearrange("a (c p) n -> p (a c) n", p=P)
                    wo_b = L(w_o_fox).rearrange("a (c p) n -> p (a c) n", p=P)
                    wo = L(w_out).rearrange("a (c p) n -> p (a c) n", p=P)

                    def view(s, c):
                        return wslot[s][:, :].rearrange("p (c n) -> p c n", c=c)

                    def load_y(i):
                        for a in range(2):
                            at = (a * TILES + i) * P
                            sp.dma_start(y_tile(i, a), y_dram[at:at + ROWS[i], :]).then_inc(y_in[i], 16)

                    with sp.If(l > 0):
                        load_y(0)
                    sp.dma_start(gainb[:, :], L(norm1_g).broadcast_to((P, D))).then_inc(s_g1, 16)
                    kvf = wslot[0][:, 0:KC * 264].rearrange("p (c n) -> p c n", c=KC)
                    with sp.If(l > 0):
                        for i in range(1, TILES):
                            load_y(i)
                    sp.dma_start(kvf[:, :, 0:256], w3[:, :, W_KV:W_QB]).then_inc(w_qkv[0], 16)
                    sp.dma_start(kvf[:, :, 256:264], w3[:, :, W_F:W_G]).then_inc(w_f, 16)
                    for c, at in ((1, 0), (2, W_QB), (3, W_KB), (4, W_VB)):
                        if c == 4:
                            sp.wait_ge(s_h, TILES)
                        sp.dma_start(view(c, KC), w3[:, :, at:at + 512]).then_inc(w_qkv[c], 16)
                    sp.dma_start(view(5, 4), wo_a).then_inc(w_oa, 16)
                    sp.wait_ge(s_xn, TILES)
                    sp.dma_start(gainb[:, :], L(norm2_g).broadcast_to((P, D))).then_inc(s_g2, 16)
                    for n in range(4):
                        s = n + 1
                        sp.wait_ge(s_prj, TILES * (s + 1))
                        for br in range(2):
                            dst = wslot[s][:, :].rearrange("p (c b n) -> p c b n", c=KC, b=2)
                            at = W_G + br * D + n * 256
                            sp.dma_start(dst[:, :, br, :], w3[:, :, at:at + 256]).then_inc(w_gates[n][br], 16)
                    sp.wait_ge(s_z, 16)
                    sp.dma_start(view(2, 4), wo_b).then_inc(w_ob, 16)
                    sp.wait_ge(s_z, 24)
                    sp.dma_start(view(3, 4), wo[:, 0:4, :]).then_inc(w_o[0], 16)
                    sp.wait_ge(s_sig, 16)
                    sp.dma_start(view(0, 4), wo[:, 4:8, :]).then_inc(w_o[1], 16)
                    free = {1: (s_sig, EARLY), 4: (s_gate, 4 * KC - EARLY), 5: (s_y, 2 * KC), 2: (s_y, 2 * KC),
                            3: (s_wo, 2 * TILES), 0: (s_wo, 2 * TILES)}
                    for s in (1, 4, 5, 2, None, 3, 0):
                        if s is None:
                            for k in range(TILES):
                                sp.wait_ge(s_xn, TILES + k + 1)
                                sp.dma_start(t_dram[P * k:P * k + ROWS[k], :], xn[k][0:ROWS[k], :]).then_inc(s_tst, 16)
                            continue
                        w, par, _ = next(o for o in ORDER if o[2] == s)
                        sp.wait_ge(*free[s])
                        load_expert(sp, w, slice(par, par + 1), s)
                    experts_sync(sp)

                @block.gpsimd
                def _(pool):
                    own = Own(pool, p_own)
                    with nc.allow_non_contiguous_dma("small parameters"):
                        pool.dma_start(hgain[:, :, :].rearrange("p k n -> p (k n)"),
                                       L(qk_gain).rearrange("a k n -> a (k n)").broadcast_to((P, 4 * HD))).then_inc(s_par, 16)
                        pool.dma_start(sinks[:, :], L(attn_sinks).broadcast_to((P, HEADS))).then_inc(s_par, 16)
                        pool.dma_start(fbias[:, :], L(b_forget).broadcast_to((P, HEADS))).then_inc(s_par, 16)
                        pool.dma_start(gbias_rows[:, :], L(b_merge).rearrange("a (k p) -> (a k) p", p=P)).then_inc(s_par, 16)
                        pool.dma_start(rbias[:, 0:GROUPS], L(b_router_group).broadcast_to((P, GROUPS))).then_inc(s_par, 16)
                        pool.dma_start(rbias[:, GROUPS:], L(b_router_expert).broadcast_to((P, EXPERTS))).then_inc(s_par, 16)
                        pool.dma_start(wr[:, :, 0:GROUPS],
                                       L(w_router_group).rearrange("a (p c) n -> p (a c) n", p=P)).then_inc(s_par, 16)
                        pool.dma_start(wr[:, :, GROUPS:],
                                       L(w_router_expert).rearrange("a (p c) n -> p (a c) n", p=P)).then_inc(s_par, 16)

                    def rsqrt_of_mean(dst, src, n):
                        own.link(pool.tensor_scalar(dst, src, 1.0 / n, EPS, ALU.mult, ALU.add))
                        return pool.tensor_tensor(dst, dst, halfneg[0:dst.shape[0], 0:dst.shape[1]], ALU.pow)

                    def norms(q):
                        for k in range(TILES):
                            r = ROWS[k]
                            pool.wait_ge(s_ss, TILES * q + k + 1)
                            rsqrt_of_mean(rstd[0:r, k:k + 1], ss[0:r, k:k + 1], D).then_inc(s_rstd, 1)

                    pool.memset(blank, NOWHERE).then_inc(s_tab0, 1)
                    pool.wait_ge(s_tab0, 1)
                    pool.dma_start(tab_dram.rearrange("(p r) c -> p (r c)", p=P), blank).then_inc(s_blank, 16)

                    norms(0)
                    pool.wait_ge(s_blank, 16)
                    for u in range(4 * TILES):
                        c, i = divmod(u, TILES)
                        n = KV if c == 0 else HEADS
                        pool.wait_ge(s_hss, u + 1)
                        rsqrt_of_mean(hr[0:ROWS[i], 0:n], hss[0:ROWS[i], 0:n], HD).then_inc(s_hr, 1)
                    norms(1)
                    pool.wait_ge(s_ent, 1)
                    for a in range(2):
                        for i in range(TILES):
                            r = ROWS[i]
                            pool.indirect_dma_start(
                                out=tab_dram, out_offset=bass.IndirectOffsetOnAxis(ap=slot_at[0:r, a, i:i + 1], axis=0),
                                in_=ent[0:r, a, i, :], in_offset=None, bounds_check=TAB - 1,
                                oob_is_err=False).then_inc(s_scat, 16)
                    pool.wait_ge(s_scat, 16 * 2 * TILES)
                    load_table(pool, tab_dram[0:P * PAIRS].rearrange("(p m) c -> p (m c)", p=P))
                    pool.wait_ge(s_tst, 16 * TILES)
                    experts_pool(pool)

                @block.scalar
                def _(act):
                    def square(q, k):
                        r = ROWS[k]
                        if q == 0:
                            act.wait_ge(s_h, k + 1)
                        else:
                            act.wait_ge(s_res, 2 * (k + 1))
                        if k:
                            act.wait_ge(s_ss, TILES * q + k)
                        act.activation(xsq[0:r, :], h[0:r, k, :], ACT.Square, accum_out=ss[0:r, k:k + 1]).then_inc(s_ss, 1)

                    def turned_out(q):
                        for k in range(TILES):
                            r = ROWS[k]
                            if k == 0:
                                square(q, 0)
                            if k + 1 < TILES:
                                square(q, k + 1)
                            for half in range(2):
                                act.wait_ge(s_tp, 2 * (TILES * q + k) + half + 1)
                                src = ps[:, 2 * q + half, :].rearrange("p (c n) -> p c n", c=4)[:, :, 0:r]
                                act.copy(xT[:, 4 * half:4 * half + 4, COL[k]:COL[k] + r], src).then_inc(s_xT, 1)

                    turned_out(0)

                    def head_out(u):
                        c, i = divmod(u, TILES)
                        r = ROWS[i]
                        dst = (kaT, qaT, qbT, kbT)[c]
                        n = KV if c == 0 else 4
                        act.wait_ge(s_qT, u + 1)
                        src = ps[:, u % 2, :].rearrange("p (c n) -> p c n", c=4)[:, 0:n, 0:r]
                        act.copy(dst[:, 0:n, COL[i]:COL[i] + r], src).then_inc(s_qTe, 1)

                    for u in range(4 * TILES):
                        c, i = divmod(u, TILES)
                        r, n = ROWS[i], (P if c == 0 else 512)
                        act.wait_ge(s_prj, u + 1)
                        if u >= 1:
                            act.wait_ge(s_hss, u)
                        act.activation(sq[0:r, 0:n], ps[0:r, 2 + u % 3, 0:n], ACT.Square).then_inc(s_sq, 1)
                        if u == TILES:
                            act.wait_ge(s_fz, 1)
                            act.activation(frg[:, 2], frg[:, 1], ACT.Exp, scale=-1.0).then_inc(s_fe, 1)
                            act.wait_ge(s_fe, 1)
                            act.activation(frg[:, 3], frg[:, 2], ACT.Ln, bias=1.0).then_inc(s_fe, 1)
                        if u >= 2:
                            head_out(u - 2)
                    head_out(4 * TILES - 2)
                    head_out(4 * TILES - 1)
                    act.wait_ge(s_gb, 1)
                    act.copy(gbias[:, :], ps[:, 7, 0:2 * KC]).then_inc(s_gbe, 1)

                    def turn_out(n):
                        t = turns[n]
                        b = n % 2
                        act.wait_ge(s_T, n + 1)
                        evacuate(act, act.copy, n).then_inc(s_Te[b], 1)

                    for v, st in enumerate(steps):
                        if st["score"] is not None:
                            j, br, hd = units[v]
                            r = ROWS[j]
                            act.wait_ge(s_nm, v + 1)
                            if hd >= 2:
                                act.wait_ge(s_T, last_turn[v - 2] + 1)
                            elif v >= 16:
                                act.wait_ge(s_T, last_turn[v - 16 + 6] + 1)
                            act.activation(prob_out(v), score_in(v), ACT.Exp, bias=nm[0:r, v:v + 1],
                                           accum_out=rs[0:r, v:v + 1]).then_inc(s_P, 1)
                        if st["norm"] is not None and units[st["norm"]][1] == 0:
                            n = block_of(st["norm"]) // 2
                            j = units[st["norm"]][0]
                            act.wait_ge(s_skin, n + 1)
                            act.activation(esk[0:ROWS[j], :], den[0:ROWS[j], :], ACT.Exp).then_inc(s_esk, 1)
                        for n in st["turn"] + ([st["oturn"]] if st["oturn"] is not None else []):
                            if n % 2:
                                turn_out(n)
                        if st["fill_out"] is not None and st["fill_out"] % 2 == 0:
                            fill_out(act, act.copy, st["fill_out"])

                    for w in range(2 * KC):
                        n = w // 2
                        if 2 * w < EARLY:
                            for k in range(2):
                                act.wait_ge(s_zo[k], w + 1)
                        else:
                            act.wait_ge(s_gate, 2 * (w + 1) - EARLY)
                        if w >= 2:
                            act.wait_ge(s_mrg, w - 1)
                        for br in range(2):
                            z = z_at(2 * w + br) if 2 * w < EARLY else ps[:, 4 * (w % 2) + br, 0:HALF]
                            act.activation(sig2(w, br), z, ACT.Sigmoid,
                                           bias=gbias[:, br * KC + n:br * KC + n + 1]).then_inc(s_sig, 1)
                    turned_out(1)
                    act.wait_ge(s_exl, 1)
                    act.activation(r_dg, r_dg, ACT.Exp).then_inc(s_exd, 1)
                    act.wait_ge(s_exl, 2)
                    act.activation(r_d, r_d, ACT.Exp).then_inc(s_exd, 1)
                    experts_scalar(act)

                @block.tensor
                def _(pe):
                    def turn_norm(q, k):
                        r = ROWS[k]
                        pe.wait_ge(s_xn, TILES * q + k + 1)
                        for half in range(2):
                            n = 2 * k + half
                            if n >= 2:
                                pe.wait_ge(s_xT, 2 * TILES * q + n - 1)
                            for c in range(4):
                                last = pe.transpose(ps[:, 2 * q + half, c * P:c * P + r],
                                                    xn[k][0:r, 4 * half + c::KC], ident[0:r, 0:r])
                            last.then_inc(s_tp, 1)

                    for k in range(TILES):
                        turn_norm(0, k)

                    def turn_heads(u):
                        c, i = divmod(u, TILES)
                        r = ROWS[i]
                        pe.wait_ge(s_qn, u + 1)
                        if u >= 2:
                            pe.wait_ge(s_qTe, u - 1)
                        for k in range(KV if c == 0 else 4):
                            last = pe.transpose(ps[:, u % 2, k * P:k * P + r], qnb[0:r, u % 2, k * P:(k + 1) * P],
                                                ident[0:r, 0:r])
                        last.then_inc(s_qT, 1)

                    for c in range(CHUNKS):
                        n = 264 if c == 0 else 512
                        s = c
                        w = wslot[s][:, 0:KC * n].rearrange("p (c n) -> p c n", c=KC)
                        pe.wait_ge(w_qkv[c], 16)
                        if c == 0:
                            pe.wait_ge(w_f, 16)
                        for i in range(TILES):
                            u = c * TILES + i
                            r = ROWS[i]
                            pe.wait_ge(s_xT, 2 * TILES if c else 2 * (i + 1))
                            if u >= 3:
                                pe.wait_ge(s_prjfree, u - 2)
                            for k in range(KC):
                                last = pe.matmul(ps[0:r, 2 + u % 3, 0:n], xT[:, k, COL[i]:COL[i] + r], w[:, k, :],
                                                 start=(k == 0), stop=(k == KC - 1))
                            last.then_inc(s_prj, 1)
                            if u >= 2 and u - 2 < 4 * TILES:
                                turn_heads(u - 2)
                    pe.wait_ge(s_lf, 1)
                    lf = frg[:, 0]
                    cps = ps[:, 5, 0:TILES * HEADS].rearrange("p (t n) -> p t n", t=TILES)
                    pe.matmul(cps[0:META, NT, :], upto[0:META, 0:META], lf[0:META, NT, :], start=True, stop=True)
                    for j in range(NT):
                        pe.matmul(cps[:, j, :], ones[0:META, :], lf[0:META, NT, :], start=True, stop=False)
                        for i in range(j):
                            pe.matmul(cps[:, j, :], ones, lf[:, i, :], start=False, stop=False)
                        last = pe.matmul(cps[:, j, :], upto, lf[:, j, :], start=False, stop=True)
                    last.then_inc(s_c, 1)
                    pe.wait_ge(s_par, 16 * 8)
                    pe.transpose(ps[:, 7, 0:2 * KC], gbias_rows[:, :], ident[0:2 * KC, 0:2 * KC]).then_inc(s_gb, 1)
                    pe.wait_ge(s_ce, 1)
                    cp24 = cpart[:, :, :, :].rearrange("p t k n -> p t (k n)")
                    for j in range(NT):
                        pe.transpose(ps[0:3 * HEADS, 6, j * P:(j + 1) * P], cp24[:, j, :], ident)
                    pe.transpose(ps[0:3 * HEADS, 5, 64:64 + META], cp24[0:META, NT, :], ident[0:META, 0:META]).then_inc(s_c, 1)
                    pe.wait_ge(s_ce, 2)
                    pe.wait_ge(s_qTe, 4 * TILES)
                    pe.wait_ge(s_prjfree, CHUNKS * TILES)
                    pe.wait_ge(s_gbe, 1)

                    def score(v):
                        j, br, hd = units[v]
                        r = ROWS[j]
                        if v >= 2:
                            pe.wait_ge(s_P, v - 1)
                        part = slice(HD * (hd % 2), HD * (hd % 2) + HD)
                        b = 2 + 2 * (v % 2)
                        if br == 0:
                            q = qaT[part, hd // 2, COL[j]:COL[j] + r]
                            g = hd // (HEADS // KV)
                            if j == NT:
                                return pe.matmul(ps[0:r, b, 0:META], q, kaT[part, g, 0:META], start=True, stop=True)
                            lo_ = COL[j] - CHUNK if j else 0
                            n = COL[j] + P - lo_
                            pe.matmul(ps[:, b, 0:n], q, kaT[part, g, lo_:lo_ + n], start=True, stop=False)
                            return pe.matmul(ps[:, b, 0:n], identb[:, :], windowb[:, CHUNK + P - n:], start=False, stop=True)
                        q = qbT[part, hd // 2, COL[j]:COL[j] + r]
                        k = kbT[part, hd // 2, :]
                        pk = pickb[:, hd:hd + 1].broadcast_to((3 * HEADS, r))
                        own_ = META if j == NT else P
                        pe.matmul(ps[0:r, b, 512 - META:512], q, k[:, 0:META], start=True, stop=False)
                        last = pe.matmul(ps[0:r, b, 512 - META:512], pk, nc3[:, 0:META], start=False, stop=(j != NT))
                        if j == NT:
                            return pe.matmul(ps[0:r, b, 512 - META:512], identb[0:META, 0:META], causalb[0:META, 0:META],
                                             start=False, stop=True)
                        n = (j + 1) * P
                        pe.matmul(ps[:, b + 1, 0:n], q, k[:, META:META + n], start=True, stop=False)
                        pe.matmul(ps[:, b + 1, n - P:n], identb[:, :], causalb[:, :], start=False, stop=False,
                                  skip_group_check=True)
                        return pe.matmul(ps[:, b + 1, 0:n], pk, nc3[:, META:META + n], start=False, stop=True)

                    def turn(n):
                        t = turns[n]
                        b = n % 2
                        if n >= 2:
                            pe.wait_ge(s_Te[b], n // 2)
                        if t["o"] is not None:
                            r = ROWS[units[t["o"]][0]]
                            pe.wait_ge(s_on, block_of(t["o"]) + 1)
                            for c in range(4):
                                last = pe.transpose(ps[:, b, c * P:c * P + r], osb[0:r, c * P:(c + 1) * P], ident[0:r, 0:r])
                            last.then_inc(s_T, 1)
                            return
                        v = t["unit"]
                        r = ROWS[units[v][0]]
                        pe.wait_ge(s_P, v + 1)
                        src = prob(v)
                        for k, (at, n_k, _) in enumerate(t["blocks"]):
                            last = pe.transpose(ps[0:n_k, b, k * P:k * P + r], src[0:r, at:at + n_k], ident[0:r, 0:r])
                        last.then_inc(s_T, 1)

                    def times_v(n):
                        t = turns[n]
                        b = n % 2
                        j, br, hd = units[t["unit"]]
                        r = ROWS[j]
                        pe.wait_ge(s_Te[b], n // 2 + 1)
                        if hd == 0 and t["first"] and block_of(t["unit"]):
                            pe.wait_ge(s_on, block_of(t["unit"]))
                        for k, (_, n_k, tile) in enumerate(t["blocks"]):
                            vv = va[0:n_k, tile, HD * (hd // 4):HD * (hd // 4) + HD] if br == 0 else \
                                vb[0:n_k, tile, HD * hd:HD * (hd + 1)]
                            last = pe.matmul(ps[0:r, 6, HD * hd:HD * (hd + 1)], PT[0:n_k, b, k * P:k * P + r], vv,
                                             start=(t["first"] and k == 0),
                                             stop=(t["last"] and k == len(t["blocks"]) - 1))
                        last.then_inc(s_PV, 1)

                    def gate(g, k, out):
                        n, half, br = g // 4, g // 2 % 2, g % 2
                        s = 1 + n // 2
                        if k == 0 and g % 8 < 2:
                            pe.wait_ge(w_gates[s - 1][br], 16)
                        wg = wslot[s][:, :].rearrange("p (c b n) -> p c b n", c=KC, b=2)
                        return pe.matmul(out, wg[:, k, br, P * (n % 2):P * (n % 2) + P],
                                         xT[:, k, HALF * half:HALF * (half + 1)], start=(k == 0), stop=(k == KC - 1))

                    def fill(todo):
                        for g, k in todo:
                            if k == 0 and g:
                                pe.wait_ge(s_zo[(g - 1) % 2], (g - 1) // 2 + 1)
                            ins = gate(g, k, ps[:, 7, 0:HALF])
                            if k == KC - 1:
                                ins.then_inc(s_z, 1)

                    for v, st in enumerate(steps):
                        if st["score"] is not None:
                            score(v).then_inc(s_S, 1)
                        fill(st["fill"][0])
                        for n in st["turn"]:
                            turn(n)
                        fill(st["fill"][1])
                        for n in st["pv"]:
                            times_v(n)
                        if st["oturn"] is not None:
                            turn(st["oturn"])

                    for b in range(2):
                        pe.wait_ge(s_Te[b], (len(turns) + 1 - b) // 2)
                        pe.wait_ge(s_zo[b], EARLY // 2)
                    pe.wait_ge(w_oa, 16)
                    pe.wait_ge(w_ob, 16)
                    woA = wslot[5][:, :].rearrange("p (c n) -> p c n", c=4)
                    woB = wslot[2][:, :].rearrange("p (c n) -> p c n", c=4)
                    for w in range(2 * KC):
                        n, half = divmod(w, 2)
                        cols = slice(HALF * half, HALF * (half + 1))
                        bank = 4 * (w % 2)
                        if w >= 2:
                            pe.wait_ge(s_mrg, w - 1)
                        for br in range(2 if 2 * w >= EARLY else 0):
                            for k in range(KC):
                                last = gate(2 * w + br, k, ps[:, bank + br, 0:HALF])
                            last.then_inc(s_gate, 1)
                        for br, (wo_, oT) in enumerate(((woA, qaT), (woB, qbT))):
                            for k in range(4):
                                last = pe.matmul(ps[:, bank + 2 + br, 0:HALF], wo_[:, k, n * P:(n + 1) * P],
                                                 oT[:, k, cols], start=(k == 0), stop=(k == 3))
                        last.then_inc(s_y, 1)
                    def normed_and_routed(k):
                        r = ROWS[k]
                        turn_norm(1, k)
                        pe.wait_ge(s_xT, 2 * (TILES + k + 1))
                        for c in range(KC):
                            last = pe.matmul(ps[0:r, 4, 36 * k:36 * (k + 1)], xT[:, c, COL[k]:COL[k] + r], wr[:, c, :],
                                             start=(c == 0), stop=(c == KC - 1))
                        last.then_inc(s_lg, 1)

                    pe.wait_ge(s_mrg, 2 * KC)
                    for n in range(2):
                        pe.wait_ge(w_o[n], 16)
                    for i in range(TILES):
                        r = ROWS[i]
                        for half in range(2):
                            xu = 2 * i + half
                            if xu >= 2:
                                pe.wait_ge(s_res, xu - 1)
                            for k in range(KC):
                                w = wslot[(3, 0)[k // 4]][:, :].rearrange("p (c n) -> p c n", c=4)
                                last = pe.matmul(ps[0:r, half, :], mrgT[:, k, COL[i]:COL[i] + r],
                                                 w[:, k % 4, 512 * half:512 * (half + 1)], start=(k == 0),
                                                 stop=(k == KC - 1))
                            last.then_inc(s_wo, 1)
                        if i:
                            normed_and_routed(i - 1)
                    normed_and_routed(TILES - 1)
                    pe.wait_ge(s_M, 1)
                    for i in range(TILES):
                        r = ROWS[i]
                        for k in range(i):
                            pe.matmul(ps[0:r, 5, 32 * i:32 * (i + 1)], onesb[:, 0:r], Mb[:, k, :], start=(k == 0), stop=False)
                        pe.matmul(ps[0:r, 5, 32 * i:32 * (i + 1)], beforeb[0:r, 0:r], Mb[0:r, i, :], start=(i == 0), stop=True)
                    for i in range(TILES):
                        r = ROWS[i]
                        last = pe.matmul(ps[:, 5, 160:192], onesb[0:r, :], Mb[0:r, i, :], start=(i == 0), stop=(i == NT))
                    last.then_inc(s_rank, 1)
                    experts_tensor(pe)

                @block.vector
                def _(dve):
                    own = Own(dve, d_own)
                    link = own.link

                    def norm(q, k):
                        r = ROWS[k]
                        dve.wait_ge(s_rstd, TILES * q + k + 1)
                        dve.scalar_tensor_tensor(out=xn[k][0:r, :], in0=h[0:r, k, :], scalar=rstd[0:r, k:k + 1],
                                                 in1=gainb[0:r, :], op0=ALU.mult, op1=ALU.mult).then_inc(s_xn, 1)

                    for k in range(TILES):
                        with dve.If(l > 0):
                            dve.wait_ge(y_in[k], 32)
                            for a in range(2):
                                dve.tensor_tensor(h[0:ROWS[k], k, :], h[0:ROWS[k], k, :], y_tile(k, a),
                                                  ALU.add).then_inc(y_add, 1)
                                dve.wait_ge(y_add, 2 * k + a + 1)
                        dve.sem_inc(s_h, 1)
                        if k == 0:
                            dve.wait_ge(s_g1, 16)
                        if k:
                            norm(0, k - 1)
                    norm(0, TILES - 1)
                    dve.wait_ge(s_par, 16 * 8)
                    for k in (0, 2):
                        link(dve.tensor_scalar(hgain[:, k, :], hgain[:, k, :], HD ** -0.5, None, ALU.mult))
                    link(dve.memset(frg[:, :, :, :], 0.0))
                    for u in range(CHUNKS * TILES):
                        c, i = divmod(u, TILES)
                        r = ROWS[i]
                        bank = ps[0:r, 2 + u % 3, :]
                        if c == CHUNKS - 1:
                            dve.wait_ge(s_prj, u + 1)
                            dve.tensor_copy(vb[0:r, i, :], bank).then_inc(s_prjfree, 1)
                            continue
                        nh = KV if c == 0 else HEADS
                        n = nh * HD
                        dve.wait_ge(s_sq, u + 1)
                        dve.tensor_reduce(hss[0:r, 0:nh], sq[0:r, 0:n].rearrange("p (h d) -> p h d", d=HD), AX,
                                          ALU.add).then_inc(s_hss, 1)
                        if c == 0:
                            dve.tensor_copy(va[0:r, i, :], bank[:, P:2 * P])
                            link(dve.tensor_copy(frg[0:r, 0, i, :], bank[:, 2 * P:2 * P + HEADS]))
                        dve.wait_ge(s_hr, u + 1)
                        y1 = qn1[0:r, 0:n].rearrange("p (h d) -> p h d", d=HD)
                        y2 = qn2[0:r, 0:n].rearrange("p (h d) -> p h d", d=HD)
                        dve.tensor_tensor(y1, bank[:, 0:n].rearrange("p (h d) -> p h d", d=HD),
                                          hr[0:r, 0:nh].unsqueeze(2).broadcast_to((r, nh, HD)), ALU.mult).then_inc(s_prjfree, 1)
                        dve.wait_ge(s_prjfree, u + 1)
                        if u >= 2:
                            dve.wait_ge(s_qT, u - 1)
                        gk = (1, 0, 2, 3)[c]
                        gb = hgain[0:r, gk, :].unsqueeze(1).broadcast_to((r, nh, HD))
                        dst = qnb[0:r, u % 2, :]
                        if c >= 2:
                            dve.tensor_tensor(dst.rearrange("p (h d) -> p h d", d=HD), y1, gb, ALU.mult).then_inc(s_qn, 1)
                            continue
                        link(dve.tensor_tensor(y2, y1, gb, ALU.mult))
                        link(dve.tensor_tensor(y1, y2, cosv[0:r, i, :].unsqueeze(1).broadcast_to((r, nh, HD)), ALU.mult))
                        sc = rot[0:r, 0:n].rearrange("p (h d) -> p h d", d=HD)
                        for a, b in ((0, 32), (32, 0)):
                            ins = dve.tensor_tensor(sc[:, :, a:a + 32], y2[:, :, b:b + 32],
                                                    sinv[0:r, i, a:a + 32].unsqueeze(1).broadcast_to((r, nh, 32)), ALU.mult)
                            link(ins)
                        if c == 0:
                            d4 = dst[:, 0:256].rearrange("p (h t d) -> p h t d", t=2, d=HD)
                            dve.tensor_tensor(d4, y1.unsqueeze(2).broadcast_to((r, nh, 2, HD)),
                                              sc.unsqueeze(2).broadcast_to((r, nh, 2, HD)), ALU.add).then_inc(s_qn, 1)
                        else:
                            dve.tensor_tensor(dst.rearrange("p (h d) -> p h d", d=HD), y1, sc, ALU.add).then_inc(s_qn, 1)
                        if u == TILES - 1:
                            z, az = frg[:, 0], frg[:, 1]
                            link(dve.tensor_tensor(z, z, fbias[:, :].unsqueeze(1).broadcast_to((P, TILES, HEADS)), ALU.add))
                            link(dve.tensor_scalar(az, z, -1.0, None, ALU.mult))
                            dve.tensor_tensor(az, z, az, ALU.max).then_inc(s_fz, 1)
                            dve.wait_ge(s_fz, 1)
                            link(dve.tensor_scalar(z, z, 0.0, None, ALU.min))
                        if u == TILES:
                            dve.wait_ge(s_fe, 2)
                            dve.tensor_tensor(frg[:, 0], frg[:, 0], frg[:, 3], ALU.subtract).then_inc(s_lf, 1)
                    dve.wait_ge(s_c, 1)
                    cps = ps[:, 5, 0:TILES * HEADS].rearrange("p (t n) -> p t n", t=TILES)
                    link(dve.memset(cso[:, :, :], 0.0))
                    link(dve.tensor_copy(cso[:, 0:NT, :], cps[:, 0:NT, :]))
                    link(dve.tensor_copy(cso[0:META, NT, :], cps[0:META, NT, :]))
                    rest = cso
                    for k in range(3):
                        link(dve.tensor_copy(cpartb[:, :, :], rest[:, :, :]))
                        part = dve.tensor_copy(cpart[:, :, k, :], cpartb[:, :, :])
                        if k == 2:
                            part.then_inc(s_ce, 1)
                            break
                        link(part)
                        link(dve.tensor_tensor(cres[:, :, :], rest[:, :, :], cpart[:, :, k, :], ALU.subtract))
                        rest = cres
                    dve.wait_ge(s_c, 2)
                    dve.tensor_scalar(nc3[:, META:POS], ps[0:3 * HEADS, 6, :], -1.0, None, ALU.mult)
                    dve.tensor_scalar(nc3[:, 0:META], ps[0:3 * HEADS, 5, 64:64 + META], -1.0, None, ALU.mult).then_inc(s_ce, 1)
                    dve.wait_ge(s_qT, 4 * TILES)
                    link(dve.memset(PA[:, :, 0:CHUNK], 0.0))

                    for v, st in enumerate(steps):
                        if st["score"] is not None:
                            j, br, hd = units[v]
                            r = ROWS[j]
                            dve.wait_ge(s_S, v + 1)
                            link(dve.tensor_reduce(mx[0:r, v:v + 1], score_in(v), AX, ALU.max))
                            floor = sinks[0:r, hd:hd + 1] if br == 0 else LOWEST
                            dve.tensor_scalar(nm[0:r, v:v + 1], mx[0:r, v:v + 1], floor, -1.0, ALU.max,
                                              ALU.mult).then_inc(s_nm, 1)
                        if st["norm"] is not None:
                            u = st["norm"]
                            j, br, _ = units[u]
                            r = ROWS[j]
                            v0 = u - HEADS + 1
                            blk = block_of(u)
                            dve.wait_ge(s_nm, u + 1)
                            dve.wait_ge(s_PV, pv_upto(u))
                            if br == 0:
                                dve.tensor_tensor(den[0:r, :], sinks[0:r, :], nm[0:r, v0:v0 + HEADS], ALU.add).then_inc(s_skin, 1)
                                dve.wait_ge(s_esk, blk // 2 + 1)
                                link(dve.tensor_tensor(den[0:r, :], esk[0:r, :], rs[0:r, v0:v0 + HEADS], ALU.add))
                                link(dve.reciprocal(rden[0:r, :], den[0:r, :]))
                            else:
                                link(dve.reciprocal(rden[0:r, :], rs[0:r, v0:v0 + HEADS]))
                            if blk >= 1:
                                dve.wait_ge(s_T, oturn_of[blk - 1] + 1)
                            dve.tensor_tensor(osb[0:r, :].rearrange("p (h d) -> p h d", d=HD),
                                              ps[0:r, 6, :].rearrange("p (h d) -> p h d", d=HD),
                                              rden[0:r, :].unsqueeze(2).broadcast_to((r, HEADS, HD)),
                                              ALU.mult).then_inc(s_on, 1)
                        for n in st["turn"] + ([st["oturn"]] if st["oturn"] is not None else []):
                            if n % 2 == 0:
                                dve.wait_ge(s_T, n + 1)
                                evacuate(dve, dve.tensor_copy, n).then_inc(s_Te[0], 1)
                        if st["fill_out"] is not None and st["fill_out"] % 2:
                            fill_out(dve, dve.tensor_copy, st["fill_out"])

                    for w in range(2 * KC):
                        n, half = divmod(w, 2)
                        bank = 4 * (w % 2)
                        dve.wait_ge(s_y, w + 1)
                        dve.wait_ge(s_sig, 2 * w + 2)
                        for br in range(2):
                            ins = dve.tensor_tensor(sig2(w, br), sig2(w, br), ps[:, bank + 2 + br, 0:HALF], ALU.mult)
                            link(ins)
                        dve.tensor_tensor(mrgT[:, n, HALF * half:HALF * (half + 1)], sig2(w, 0), sig2(w, 1),
                                          ALU.add).then_inc(s_mrg, 1)
                    for i in range(TILES):
                        r = ROWS[i]
                        for half in range(2):
                            xu = 2 * i + half
                            hv = h[0:r, i, 512 * half:512 * (half + 1)]
                            dve.wait_ge(s_wo, xu + 1)
                            dve.tensor_tensor(hv, hv, ps[0:r, half, :], ALU.add).then_inc(s_res, 1)
                        if i == 0:
                            dve.wait_ge(s_g2, 16)
                        norm(1, i)
                    def b3(a, n):
                        return a.unsqueeze(2).broadcast_to((P, TILES, n))

                    def first_max(src, top, eq, onehot, n):
                        down = C("down")[:, 0:n].unsqueeze(1).broadcast_to((P, TILES, n))
                        link(dve.tensor_reduce(top, src, AX, ALU.max))
                        link(dve.tensor_tensor(eq, src, b3(top, n), ALU.is_equal))
                        link(dve.tensor_tensor(eq, eq, down, ALU.mult))
                        link(dve.tensor_reduce(r_f, eq, AX, ALU.max))
                        link(dve.tensor_tensor(onehot, eq, b3(r_f, n), ALU.is_equal))

                    link(dve.memset(r_lg, 0.0))
                    dve.wait_ge(s_lg, TILES)
                    lgp = ps[:, 4, 0:36 * TILES].rearrange("p (t n) -> p t n", t=TILES)
                    link(dve.tensor_tensor(r_lg[:, 0:NT, :], lgp[:, 0:NT, :],
                                           rbias[:, :].unsqueeze(1).broadcast_to((P, NT, 36)), ALU.add))
                    link(dve.tensor_tensor(r_lg[0:META, NT, :], lgp[0:META, NT, :], rbias[0:META, :], ALU.add))
                    first_max(r_lg[:, :, 0:GROUPS], r_gm, r_eq, r_og, GROUPS)
                    dve.tensor_tensor(r_dg, r_lg[:, :, 0:GROUPS], b3(r_gm, GROUPS), ALU.subtract).then_inc(s_exl, 1)
                    og4 = r_og.unsqueeze(3).broadcast_to((P, TILES, GROUPS, PER))
                    sel4 = r_sel.rearrange("p t (g e) -> p t g e", g=GROUPS)
                    link(dve.tensor_tensor(sel4, r_lg[:, :, GROUPS:].rearrange("p t (g e) -> p t g e", g=GROUPS), og4,
                                           ALU.mult))
                    link(dve.tensor_reduce(r_ein, r_sel.rearrange("p t (g e) -> p t e g", g=GROUPS), AX, ALU.add))
                    first_max(r_ein, r_v1, r_w, r_o[0], PER)
                    link(dve.scalar_tensor_tensor(out=r_e2, in0=r_o[0], scalar=LOWEST, in1=r_ein, op0=ALU.mult, op1=ALU.add))
                    first_max(r_e2, r_v2, r_w, r_o[1], PER)
                    dve.tensor_tensor(r_d, r_v2, r_v1, ALU.subtract).then_inc(s_exl, 1)
                    for a in range(2):
                        link(dve.tensor_tensor(work_M[:, a].rearrange("p t (g e) -> p t g e", g=GROUPS), og4,
                                               r_o[a].unsqueeze(2).broadcast_to((P, TILES, GROUPS, PER)), ALU.mult))
                    dve.tensor_tensor(Mb[:, :, :], work_M[:, 0], work_M[:, 1], ALU.add).then_inc(s_M, 1)
                    dve.wait_ge(s_exd, 2)
                    link(dve.tensor_reduce(r_sum, r_dg, AX, ALU.add))
                    link(dve.reciprocal(r_pg, r_sum))
                    link(dve.tensor_scalar(r_den, r_d, 1.0, None, ALU.add))
                    link(dve.reciprocal(r_den, r_den))
                    link(dve.tensor_tensor(r_g[0], r_den, r_pg, ALU.mult))
                    link(dve.tensor_tensor(r_g[1], r_g[0], r_d, ALU.mult))
                    link(dve.memset(work_R[:, 0], 0.0))
                    dve.wait_ge(s_rank, 1)
                    rkp = ps[:, 5, 0:32 * TILES].rearrange("p (t n) -> p t n", t=TILES)
                    dve.tensor_copy(work_R[:, 0, 0:NT, :], rkp[:, 0:NT, :])
                    link(dve.tensor_copy(work_R[0:META, 0, NT, :], rkp[0:META, NT, :]))
                    ebase = C("ebase").unsqueeze(1).broadcast_to((P, TILES, EXPERTS))
                    for a in range(2):
                        link(dve.tensor_tensor(work_R[:, 1], work_M[:, a], work_R[:, 0], ALU.mult))
                        link(dve.tensor_reduce(r_rank, work_R[:, 1], AX, ALU.add))
                        link(dve.tensor_tensor(work_R[:, 1], work_M[:, a], ebase, ALU.mult))
                        link(dve.tensor_reduce(r_at, work_R[:, 1], AX, ALU.add))
                        link(dve.tensor_copy(r_ri, r_rank))
                        link(dve.tensor_scalar(r_ri, r_ri, 6, None, ALU.arith_shift_right))
                        link(dve.tensor_copy(r_hf, r_ri))
                        link(dve.scalar_tensor_tensor(out=r_slot, in0=r_rank, scalar=float(PAIRS), in1=r_at, op0=ALU.mult,
                                                      op1=ALU.add))
                        link(dve.scalar_tensor_tensor(out=slot_at[:, a, :], in0=r_hf, scalar=float(CAP * PAIRS), in1=r_slot,
                                                      op0=ALU.mult, op1=ALU.add))
                        link(dve.tensor_copy(ent[:, a, :, 0], C("row")))
                        link(dve.tensor_scalar(ent[:, a, :, 1], C("row"), float(a * TILES * P), None, ALU.add))
                        link(dve.tensor_copy(ent[:, a, :, 2].bitcast(F32), r_g[a]))
                        link(dve.tensor_copy(ent[:, a, :, 3], C("row")))
                    link(dve.tensor_reduce(r_cm[0:1, 0:1], ps[0:1, 5, 160:192], AX, ALU.max))
                    link(dve.tensor_scalar(r_ci[0:1, 0:1], r_cm[0:1, 0:1], CAP - 1.0, None, ALU.add))
                    dve.tensor_scalar(cnt[0:1, 0:1], r_ci[0:1, 0:1], 6, None, ALU.arith_shift_right).then_inc(s_ent, 1)
                    experts_vector(dve)

            clear_all()

            rounds = nc.values_load(cnt[0:1, 0:1], min_val=1, max_val=ROUNDS)
            with nc.If(rounds > 1):
                with nc.Fori(1, rounds) as rnd:
                    with nc.Block() as block:
                        @block.sync
                        def _(sp):
                            for w, par, s in ORDER:
                                load_expert(sp, w, slice(par, par + 1), s)
                            experts_sync(sp)

                        @block.gpsimd
                        def _(pool):
                            load_table(pool, tab_dram.rearrange("(r p m) c -> r p (m c)", p=P, m=PAIRS)[
                                bass.ds(rnd, 1)].rearrange("r p n -> (r p) n"))
                            experts_pool(pool)

                        @block.scalar
                        def _(act):
                            experts_scalar(act)

                        @block.tensor
                        def _(pe):
                            experts_tensor(pe)

                        @block.vector
                        def _(dve):
                            experts_vector(dve)
                    clear_all()

        with nc.Fori(0, DEPTH) as l:
            layer(l)

        with nc.Block() as block:
            @block.sync
            def _(sp):
                for i in range(NT):
                    for a in range(2):
                        at = (a * TILES + i) * P
                        sp.dma_start(y_tile(i, a), y_dram[at:at + P, :]).then_inc(y_in[i], 16)
                for i in range(NT):
                    sp.wait_ge(y_add, 2 * (i + 1))
                    sp.dma_start(out[0, i * P:(i + 1) * P, :], h[:, i, :]).then_inc(s_out, 16)
                sp.wait_ge(s_out, 16 * NT)

            @block.vector
            def _(dve):
                for i in range(NT):
                    dve.wait_ge(y_in[i], 32)
                    for a in range(2):
                        dve.tensor_tensor(h[:, i, :], h[:, i, :], y_tile(i, a), ALU.add).then_inc(y_add, 1)
                        dve.wait_ge(y_add, 2 * i + a + 1)


INPUTS = ["x", "meta_tokens", "norm1_g", "w_in", "qk_gain", "attn_sinks", "b_forget", "b_merge", "w_o_swa", "w_o_fox",
          "w_out", "norm2_g", "w_router_group", "b_router_group", "w_router_expert", "b_router_expert", "w_exp_gate",
          "w_exp_up", "w_exp_down"]


def kernel(**inputs):
    import concourse.bacc as bacc
    from concourse.bass_utils import run_bass_kernel_spmd

    nc = bacc.Bacc("TRN2", target_bir_lowering=False, num_devices=1)
    arrays = {f"in_{name}": np.ascontiguousarray(inputs[name]) for name in INPUTS}
    arrays["in_constants"] = constants()
    args = [nc.dram_tensor(name, a.shape, F32, kind="ExternalInput").ap() for name, a in arrays.items()]
    out = nc.dram_tensor("out_0", (1, SEQ, D), F32, kind="ExternalOutput").ap()
    trunk_kernel(nc, *args, out)
    result = run_bass_kernel_spmd(nc, [arrays], core_ids=[0])
    return result.results[0]["out_0"]
```

```python
from contextlib import ExitStack

import concourse.bass as bass
import numpy as np
from concourse import mybir

F32 = mybir.dt.float32
BF16 = mybir.dt.bfloat16
I32 = mybir.dt.int32
U32 = mybir.dt.uint32
ALU = mybir.AluOpType
ACT = mybir.ActivationFunctionType
AX = mybir.AxisListType.X

P = 128
D = 1024
SEQ = 512
META = 16
POS = SEQ + META
DEPTH = 2
HD = 64
HEADS = 8
KV = 2
CHUNK = 64
NT = SEQ // P
TILES = NT + 1
KC = D // P
EPS = 1e-6
NEG = -1e30
LOWEST = -3.0e38
THETA = 10000.0

W_KV = HEADS * HD
W_QB = W_KV + 2 * KV * HD
W_KB = W_QB + 512
W_VB = W_KB + 512
W_F = W_VB + 512
W_G = W_F + HEADS

GROUPS = 4
PER = 8
EXPERTS = GROUPS * PER
FF = 512
FC = FF // P
PAIRS = EXPERTS // 2
CAP = 64
ROUNDS = -(-POS // CAP)
TAB = ROUNDS * P * PAIRS
NOWHERE = 1 << 20
YROWS = 2 * TILES * P

PACK = 32
QUARTERS = P // PACK

ROWS = [P] * NT + [META]
COL = [META + P * i for i in range(NT)] + [0]

EARLY = 30
FILL = (2, 2, 2, 2)
HALF = POS // 2

CONST = {}


def constants():
    cols = []

    def put(name, a):
        a = np.asarray(a, np.float32)
        full = np.zeros((P, a.shape[1]), np.float32)
        full[:a.shape[0]] = a
        at = sum(c.shape[1] for c in cols)
        CONST[name] = (at, a.shape[1])
        cols.append(full)

    k = np.arange(P)
    put("ident", np.eye(P))
    put("upto", k[:, None] <= k[None, :])
    put("before", k[:, None] < k[None, :])
    put("ones", np.ones((P, P)))
    put("causal", np.where(k[None, :] > k[:, None], NEG, 0.0))
    key = np.arange(CHUNK + P)
    masked = np.where(k[:, None] < CHUNK, key[None, :] >= 2 * CHUNK, key[None, :] < CHUNK)
    put("window", np.where(masked, NEG, 0.0))
    inv = np.power(np.float32(THETA), -np.arange(0, HD, 2, dtype=np.float32) / np.float32(HD)).astype(np.float32)
    cos, sin = np.zeros((P, TILES, HD), np.float32), np.zeros((P, TILES, HD), np.float32)
    for i in range(TILES):
        at = k if i < NT else k % PACK
        ang = (COL[i] + at).astype(np.float32)[:, None] * inv[None, :]
        cos[:, i] = np.concatenate([np.cos(ang), np.cos(ang)], 1)
        sin[:, i] = np.concatenate([-np.sin(ang), np.sin(ang)], 1)
    put("cos", cos.reshape(P, -1))
    put("sin", sin.reshape(P, -1))
    put("down", np.tile(PER - np.arange(PER), (P, 1)))
    e = np.arange(EXPERTS)
    put("ebase", np.tile((e % 2) * CAP * PAIRS + e // 2, (P, 1)))
    put("pick", np.arange(3 * HEADS)[:, None] % HEADS == np.arange(HEADS)[None, :])
    row = np.arange(TILES)[None, :] * P + k[:, None]
    put("row", row)
    put("value", np.concatenate([row, row, row, row + TILES * P], 1) - NOWHERE)
    put("slots", np.tile(np.arange(CAP), (P, 1)))
    return np.concatenate(cols, 1)


NCONST = constants().shape[1]


def packed(c, i):
    return c > 0 and i == NT


def proj_shape(c, i):
    if packed(c, i):
        return P, HEADS // QUARTERS
    return ROWS[i], (KV if c == 0 else HEADS)


def res_upto(k):
    return 2 * (k + 1) if k < NT else 2 * NT + QUARTERS


def attention_plan():
    units = [(j, br, h) for j in [NT] + list(range(NT)) for br in (0, 1) for h in range(HEADS)]
    steps, turns, pvs = [], [], 0
    for v in range(len(units) + 6):
        st = {"score": v if v < len(units) else None, "turn": [], "pv": []}
        for name, lag in (("sinks", 2), ("sums", 3), ("norm", 4), ("oturn", 5)):
            done = 0 <= v - lag < len(units) and units[v - lag][2] == HEADS - 1
            st[name] = v - lag if done else None
        if 0 <= v - 2 < len(units):
            j, br, h = units[v - 2]
            if br == 0:
                if j == NT:
                    sets = [[(P - META, META, NT)]]
                elif j == 0:
                    sets = [[(P, P, 0)], [(P - META, META, NT)]]
                else:
                    sets = [[(0, P, j - 1), (P, P, j)]]
            elif j == NT:
                sets = [[(0, META, NT)]]
            else:
                sets = [[(COL[i], P, i) for i in range(j + 1)], [(0, META, NT)]]
            for n, s in enumerate(sets):
                st["turn"].append(len(turns))
                turns.append({"unit": v - 2, "blocks": s, "first": n == 0, "last": n == len(sets) - 1, "o": None})
        if 0 <= v - 3 < len(units):
            st["pv"] = [n for n, t in enumerate(turns) if t["unit"] == v - 3]
        if st["oturn"] is not None:
            st["oturn"] = len(turns)
            turns.append({"unit": None, "blocks": None, "o": v - 5})
        steps.append(st)
    for st in steps:
        st["fill"], st["fill_out"] = [[], []], None
    for g in range(EARLY):
        place, k = 2 * len(units) * g // EARLY, 0
        for m in FILL:
            steps[place // 2]["fill"][place % 2] = [(g, k + a) for a in range(m)]
            k += m
            place += 1
        steps[(place - 1) // 2]["fill_out"] = g
    for st in steps:
        for n in st["pv"]:
            pvs += 1
            turns[n]["pv_count"] = pvs
    return units, steps, turns


def trunk_kernel(nc, x, meta_tokens, norm1_g, w_in, qk_gain, attn_sinks, b_forget, b_merge, w_o_swa, w_o_fox, w_out,
                 norm2_g, w_router_group, b_router_group, w_router_expert, b_router_expert,
                 w_exp_gate, w_exp_up, w_exp_down, const, out):
    ctx = ExitStack()
    with ctx:
        def sb(name, shape, dt=F32):
            return ctx.enter_context(nc.sbuf_tensor(name, shape, dt))

        def sem(name):
            s = ctx.enter_context(nc.semaphore(name))
            sems.append(s)
            return s

        sems = []
        t_dram = nc.dram_tensor("t_rows", (POS, D), F32, kind="Internal").ap()
        y_dram = nc.dram_tensor("y_rows", (YROWS, D), F32, kind="Internal").ap()
        tab_dram = nc.dram_tensor("slot_table", (TAB, 4), U32, kind="Internal").ap()

        cst = sb("cst", [P, NCONST])

        def C(name):
            at, n = CONST[name]
            return cst[:, at:at + n]

        ident, upto, ones = C("ident"), C("upto"), C("ones")
        cosv = C("cos").rearrange("p (t d) -> p t d", d=HD)
        sinv = C("sin").rearrange("p (t d) -> p t d", d=HD)
        identb = sb("identb", [P, P], BF16)
        causalb = sb("causalb", [P, P], BF16)
        windowb = sb("windowb", [P, CHUNK + P], BF16)
        beforeb = sb("beforeb", [P, P], BF16)
        onesb = sb("onesb", [P, P], BF16)
        SLOT = 4096
        wslot = [sb(f"wslot{s}", [P, SLOT]) for s in range(6)]
        h = sb("h", [P, TILES, D])
        xT = sb("xT", [P, KC, POS])
        gainb = sb("gainb", [P, D])
        wr = sb("wr", [P, KC, GROUPS + EXPERTS])
        rbias = sb("rbias", [P, GROUPS + EXPERTS])
        hgain = sb("hgain", [P, 4, HD])
        sinks = sb("sinks", [P, HEADS])
        fbias = sb("fbias", [P, HEADS])
        gbias = sb("gbias", [P, 2 * KC])
        halfneg = sb("halfneg", [P, HEADS])
        small = sb("small", [P, 56])
        qaT = sb("qaT", [P, 4, POS])
        qbT = sb("qbT", [P, 4, POS])
        arena = sb("arena", [P, 4 * POS + TILES * 512])
        kbT = arena[:, 0:4 * POS].rearrange("p (c n) -> p c n", c=4)
        vb = arena[:, 4 * POS:4 * POS + TILES * 512].rearrange("p (t n) -> p t n", t=TILES)
        vbf = arena[:, 4 * POS:4 * POS + TILES * 512]
        mrgT = arena[:, 0:KC * POS].rearrange("p (c n) -> p c n", c=KC)
        kaT = sb("kaT", [P, KV, POS])
        va = sb("va", [P, TILES, KV * HD])
        work = sb("work", [P, 3888])
        tabs = sb("tabs", [P, PAIRS + 1, 4], U32)
        cnt = sb("cnt", [1, 2], I32)
        idx_g = sb("idx_g", [P, 1], U32)
        idx_s = sb("idx_s", [P, 1], U32)
        gcol = sb("gcol", [P, 1])

        qaf, qbf = (t[:, :, :].rearrange("p c n -> p (c n)") for t in (qaT, qbT))
        kaf = kaT[:, :, :].rearrange("p c n -> p (c n)")
        xn = [qaf[:, 0:D], qaf[:, D:2 * D], kaf[:, 0:D], work[:, 0:D], work[:, 1700:1700 + D]]
        xsq = qbf[:, 0:D]
        sq, qn1, qn2, rot = (work[:, 512 * k:512 * (k + 1)] for k in range(4))
        qnb = work[:, 2048:3072].rearrange("p (b n) -> p b n", b=2)
        PA = work[:, 0:3 * 2 * P].rearrange("p (b n) -> p b n", b=3)
        PF = work[:, 768:768 + 3 * POS].rearrange("p (b n) -> p b n", b=3)
        PT = work[:, 2352:3376].rearrange("p (b n) -> p b n", b=2)
        osb = work[:, 3376:3888]
        gbias_rows = work[0:2 * KC, 3376:3376 + P]
        sig = work[:, 0:4 * HALF].rearrange("p (k n) -> p k n", k=4)
        rbuf = qbf[:, D:2 * D + 64]
        xg = arena[:, 0:D]
        xgT = arena[:, D:2 * D].rearrange("p (c n) -> p c n", c=KC)
        sg = arena[:, 2048:2560]
        hh = arena[:, 2560:3072]
        hT = arena[:, 3072:3584].rearrange("p (c n) -> p c n", c=FC)
        ysb = arena[:, 3584:4608]

        ss, rstd = small[:, 0:8], small[:, 8:16]
        hss, hr = small[:, 16:24], small[:, 24:32]
        stat = sb("stat", [P, 3, 80])
        mx, nm, rs = stat[:, 0, :], stat[:, 1, :], stat[:, 2, :]
        esk, den, rden = small[:, 32:40], small[:, 40:48], small[:, 48:56]
        frg = sb("frg", [P, 4, TILES, HEADS])
        cso = sb("cso", [P, TILES, HEADS])
        cres = sb("cres", [P, TILES, HEADS])
        cpart = sb("cpart", [P, TILES, 3, HEADS])
        cpartb = sb("cpartb", [P, TILES, HEADS], BF16)
        nc3 = sb("nc3", [3 * HEADS, POS], BF16)
        pickb = sb("pickb", [3 * HEADS, HEADS], BF16)

        ps = ctx.enter_context(nc.psum_tensor("ps", [P, 8, 512], F32))

        s_in = sem("s_in")
        s_tab0 = sem("s_tab0")
        loaded = [sem(f"loaded{s}") for s in range(6)]
        w_qkv = [sem(f"w_qkv{k}") for k in range(5)]
        w_f = sem("w_f")
        w_gates = [[sem(f"w_gates{k}_{br}") for br in range(2)] for k in range(4)]
        w_oa, w_ob = sem("w_oa"), sem("w_ob")
        w_o = [sem(f"w_o{k}") for k in range(2)]
        freed = [sem(f"freed{s}") for s in range(6)]
        s_par = sem("s_par")
        s_rpar = sem("s_rpar")
        s_g1 = sem("s_g1")
        s_g2 = sem("s_g2")
        s_ss = sem("s_ss")
        s_rstd = sem("s_rstd")
        s_xn = sem("s_xn")
        s_tp = sem("s_tp")
        s_xT = sem("s_xT")
        s_tst = sem("s_tst")
        s_h = sem("s_h")
        s_gb = sem("s_gb")
        s_gbe = sem("s_gbe")
        s_prj = sem("s_prj")
        s_prjfree = sem("s_prjfree")
        s_sq = sem("s_sq")
        s_hss = sem("s_hss")
        s_hr = sem("s_hr")
        s_qn = sem("s_qn")
        s_qT = sem("s_qT")
        s_qTe = sem("s_qTe")
        s_fz = sem("s_fz")
        s_fe = sem("s_fe")
        s_lf = sem("s_lf")
        s_c = sem("s_c")
        s_ce = sem("s_ce")
        s_S = sem("s_S")
        s_nm = sem("s_nm")
        s_P = sem("s_P")
        s_T = sem("s_T")
        s_Te = [sem(f"s_Te{b}") for b in range(2)]
        s_PV = sem("s_PV")
        s_skin = sem("s_skin")
        s_esk = sem("s_esk")
        s_on = sem("s_on")
        s_z = sem("s_z")
        s_zo = [sem(f"s_zo{k}") for k in range(2)]
        s_gate = sem("s_gate")
        s_y = sem("s_y")
        s_sig = sem("s_sig")
        s_mrg = sem("s_mrg")
        s_wo = sem("s_wo")
        s_res = sem("s_res")
        s_lg = sem("s_lg")
        s_M = sem("s_M")
        s_rank = sem("s_rank")
        s_exl = sem("s_exl")
        s_exd = sem("s_exd")
        s_ent = sem("s_ent")
        s_scat = sem("s_scat")
        s_tabl = sem("s_tabl")
        s_put = sem("s_put")
        e_blank = sem("e_blank")
        e_st = sem("e_st")
        e_idx = sem("e_idx")
        e_gath = sem("e_gath")
        e_xgT = sem("e_xgT")
        e_xT = sem("e_xT")
        e_sg = sem("e_sg")
        e_h = sem("e_h")
        e_hT = sem("e_hT")
        e_hTe = sem("e_hTe")
        e_y = sem("e_y")
        e_scat = sem("e_scat")
        y_in = [sem(f"y_in{i}") for i in range(TILES)]
        y_add = sem("y_add")
        s_blank = sem("s_blank")
        s_out = sem("s_out")
        d_own = sem("d_own")
        p_own = sem("p_own")
        lo, hi = min(s.num for s in sems), max(s.num for s in sems)
        assert hi - lo + 1 == len(sems)

        blank = vbf[:, 0:TAB * 4 // P].bitcast(U32)

        def y_tile(i, a):
            if i == NT:
                return arena[0:META, a * D:(a + 1) * D]
            return wslot[4 + i // 2][:, (2 * (i % 2) + a) * D:(2 * (i % 2) + a + 1) * D]

        def clear_all():
            nc.all_engine_barrier()
            with nc.Block() as block:
                @block.gpsimd
                def _(pool):
                    pool.dma_reset(range(lo, hi + 1))
                    pool.sem_clear(range(lo, hi + 1))
            nc.all_engine_barrier()

        class Own:

            def __init__(self, eng, s):
                self.eng, self.s, self.n = eng, s, 0

            def link(self, ins):
                self.n += 1
                ins.then_inc(self.s, 1)
                self.eng.wait_ge(self.s, self.n)

        with nc.Block() as block:
            @block.sync
            def _(sp):
                sp.dma_start(cst[:, :], const).then_inc(s_in, 16)
                for i in range(NT):
                    sp.dma_start(h[:, i, :], x[0, i * P:(i + 1) * P, :]).then_inc(s_in, 16)
                sp.dma_start(h[0:META, NT, :], meta_tokens).then_inc(s_in, 16)
                sp.wait_ge(s_in, 16 * (TILES + 1))

            @block.gpsimd
            def _(pool):
                pool.memset(halfneg[:, :], -0.5)
                pool.memset(tabs[:, :, :], NOWHERE)

            @block.vector
            def _(dve):
                dve.wait_ge(s_in, 16 * (TILES + 1))
                for dst, name in ((identb, "ident"), (causalb, "causal"), (windowb, "window"), (beforeb, "before"),
                                  (onesb, "ones")):
                    dve.tensor_copy(dst[:, :], C(name))
                dve.tensor_copy(pickb[:, :], C("pick")[0:3 * HEADS, :])
        clear_all()

        units, steps, turns = attention_plan()
        last_turn = {t["unit"]: n for n, t in enumerate(turns) if t["unit"] is not None}
        oturn_of = {t["o"] // HEADS: n for n, t in enumerate(turns) if t["o"] is not None}

        def block_of(v):
            return v // HEADS

        def pv_upto(v):
            return turns[last_turn[v]]["pv_count"]

        psf = ps[:, :, :].rearrange("p b n -> p (b n)")

        def keys_of(v):
            j, br, _ = units[v]
            if j == NT:
                return META
            return (COL[j] + P if br else (CHUNK if j else META) + P)

        def score_in(v):
            j, br, _ = units[v]
            at = 512 * (2 + 2 * (v % 2)) + (512 - META if br else 0)
            return psf[0:ROWS[j], at:at + keys_of(v)]

        def prob(v):
            return (PF if units[v][1] else PA)[:, v % 3, :]

        def prob_before(v):
            return next((u for u in range(v - 3, -1, -3) if units[u][1] == units[v][1]), None)

        def prob_out(v):
            j, br, _ = units[v]
            n = keys_of(v)
            at = 0 if br else (P - META if j == NT else 2 * P - n)
            return prob(v)[0:ROWS[j], at:at + n]

        def evacuate(eng, copy, n):
            t, b = turns[n], n % 2
            src = ps[:, b, :].rearrange("p (c n) -> p c n", c=4)
            if t["o"] is not None:
                j, br, _ = units[t["o"]]
                return copy((qaT, qbT)[br][:, :, COL[j]:COL[j] + ROWS[j]], src[:, :, 0:ROWS[j]])
            r, nk, nb = ROWS[units[t["unit"]][0]], t["blocks"][0][1], len(t["blocks"])
            before = [m for m in range(n % 2, n, 2) if turns[m]["o"] is None]
            if before:
                eng.wait_ge(s_PV, turns[before[-1]]["pv_count"])
            return copy(PT[0:nk, b, :].rearrange("p (c n) -> p c n", c=4)[:, 0:nb, 0:r], src[0:nk, 0:nb, 0:r])

        def sig2(w, br):
            return sig[:, 2 * (w % 2) + br, :]

        def z_at(g):
            s, k = divmod(g, wslot[0].shape[1] // HALF)
            return wslot[s][:, HALF * k:HALF * (k + 1)]

        def fill_out(eng, copy, g):
            eng.wait_ge(s_z, g + 1)
            copy(z_at(g), ps[:, 7, 0:HALF]).then_inc(s_zo[g % 2], 1)

        CHUNKS = 5

        r_n = [0]

        def r(shape, dt=F32):
            n = int(np.prod(shape))
            at = r_n[0]
            r_n[0] += n
            assert r_n[0] <= 2 * D - D + 64
            v = rbuf[:, at:at + n]
            if dt != F32:
                v = v.bitcast(dt)
            names = "abc"[:len(shape)]
            if len(shape) == 1:
                return v
            return v.rearrange("p (" + " ".join(names) + ") -> p " + " ".join(names),
                               **{k: n_ for k, n_ in zip(names[1:], shape[1:])})

        r_lg = r((TILES, GROUPS + EXPERTS))
        r_gm, r_f, r_sum, r_pg, r_v1, r_v2, r_d, r_den = (r((TILES,)) for _ in range(8))
        r_dg, r_eq, r_og = (r((TILES, GROUPS)) for _ in range(3))
        r_sel = r((TILES, EXPERTS))
        r_ein, r_e2, r_w = (r((TILES, PER)) for _ in range(3))
        r_o = [r((TILES, PER)) for _ in range(2)]
        BOTH = 2 * TILES
        r_g = r((BOTH,))
        r_rank, r_at, r_hf, r_slot = (r((BOTH,)) for _ in range(4))
        r_ri = r((BOTH,), I32)
        r_cm, r_ci = r((2,)), r((2,), I32)
        ent = sb("ent", [P, 2 * TILES, 4], U32)
        slot_at = sb("slot_at", [P, 2 * TILES], U32)
        Mb = sb("Mb", [P, TILES, EXPERTS], BF16)

        work_M = work[:, 1056:1056 + BOTH * EXPERTS].rearrange("p (b n) -> p b n", n=EXPERTS)
        work_R = work[:, 1376:1376 + BOTH * EXPERTS].rearrange("p (b n) -> p b n", n=EXPERTS)
        in_slot = va[:, :, :].rearrange("p t n -> p (t n)").rearrange("p (b n) -> p b n", n=CAP)
        put_at = work[:, 2724:2724 + BOTH * 3 * EXPERTS].rearrange("p (b q v m) -> p b q v m", b=BOTH, q=2, v=3)

        def layer(l):
            def L(a):
                return a[bass.ds(l, 1)]

            ORDER = ((w_exp_gate, 0, 3), (w_exp_gate, 1, 0), (w_exp_up, 0, 4), (w_exp_up, 1, 1),
                     (w_exp_down, 0, 5), (w_exp_down, 1, 2))

            def load_expert(sp, w, e, s):
                src = w[bass.ds(l, 1), e]
                if w is w_exp_down:
                    sp.dma_start(wslot[s][:, :].rearrange("p (c n) -> p c n", c=FC),
                                 src.rearrange("a b (c p) n -> p (a b c) n", p=P)).then_inc(loaded[s], 16)
                else:
                    sp.dma_start(wslot[s][:, :], src.rearrange("a b (p c) n -> p (a b c n)", p=P)).then_inc(loaded[s], 16)

            def experts_sync(sp):
                with sp.Fori(1, PAIRS) as i:
                    for w, par, s in ORDER:
                        sp.wait_ge(freed[s], i)
                        load_expert(sp, w, bass.ds(2 * i + par, 1), s)

            def experts_pool(pool, meanwhile=None):
                token_bound = pool.to_reg(POS - 1)
                row_bound = pool.to_reg(YROWS - 1)

                def stage(idx, col, k):
                    pool.tensor_copy(idx[:, :], tabs[:, col, k:k + 1]).then_inc(e_idx, 1)
                    pool.wait_ge(e_idx, 1)
                    pool.sem_clear(e_idx)

                def gather(col):
                    stage(idx_g, col, 0)
                    pool.indirect_dma_start(out=xg, out_offset=None, in_=t_dram,
                                            in_offset=bass.IndirectOffsetOnAxis(ap=idx_g[:, 0:1], axis=0),
                                            bounds_check=token_bound, oob_is_err=False).then_inc(e_gath, 16)

                def scatter(i, first):
                    if not first:
                        pool.wait_ge(e_scat, 16 * i)
                    pool.tensor_copy(gcol[:, :], tabs[:, slice(0, 1) if first else bass.ds(i, 1), 2:3].bitcast(F32)).then_inc(e_st, 1)
                    pool.wait_ge(e_y, 2 * (i + 1))
                    stage(idx_s, slice(0, 1) if first else bass.ds(i, 1), 1)
                    pool.indirect_dma_start(out=y_dram, out_offset=bass.IndirectOffsetOnAxis(ap=idx_s[:, 0:1], axis=0),
                                            in_=ysb, in_offset=None, bounds_check=row_bound,
                                            oob_is_err=False).then_inc(e_scat, 16)

                def next_gather(i):
                    pool.wait_ge(e_gath, 16 * (i + 1))
                    pool.wait_ge(e_xgT, i + 1)
                    gather(slice(1, 2) if isinstance(i, int) else bass.ds(i + 1, 1))

                gather(slice(0, 1))
                if meanwhile:
                    meanwhile()
                next_gather(0)
                scatter(0, True)
                with pool.Fori(1, PAIRS) as i:
                    next_gather(i)
                    scatter(i, False)
                pool.wait_ge(e_gath, 16 * (PAIRS + 1))
                pool.wait_ge(e_scat, 16 * PAIRS)

            def experts_tensor(pe):
                def turn_tokens():
                    for c in range(KC):
                        last = pe.transpose(ps[:, 6 + c // 4, (c % 4) * P:(c % 4 + 1) * P], xg[:, c::KC], ident)
                    last.then_inc(e_xgT, 1)

                pe.wait_ge(e_gath, 16)
                turn_tokens()
                with pe.Fori(0, PAIRS) as i:
                    pe.wait_ge(e_xT, 2 * (i + 1))
                    for bank, pair in ((0, (3, 0)), (1, (4, 1))):
                        wa, wb = (wslot[s][:, :].rearrange("p (c n) -> p c n", c=KC) for s in pair)
                        for s in pair:
                            pe.wait_ge(loaded[s], 16 * (i + 1))
                        for c in range(KC):
                            for par, w in ((0, wa), (1, wb)):
                                last = pe.matmul(ps[CAP * par:CAP * (par + 1), bank, :],
                                                 xgT[:, c, CAP * par:CAP * (par + 1)], w[:, c, :],
                                                 start=(c == 0), stop=(c == KC - 1))
                                if c == KC - 1:
                                    last.then_inc(freed[pair[par]], 1)
                    pe.wait_ge(e_h, i + 1)
                    for c in range(FC):
                        last = pe.transpose(ps[:, 4, c * P:(c + 1) * P], hh[:, c * P:(c + 1) * P], ident)
                    last.then_inc(e_hT, 1)
                    pe.wait_ge(e_hTe, i + 1)
                    pe.wait_ge(e_st, i + 1)
                    for s in (5, 2):
                        pe.wait_ge(loaded[s], 16 * (i + 1))
                    for half in range(2):
                        for c in range(FC):
                            for par, s in ((0, 5), (1, 2)):
                                w = wslot[s][:, :].rearrange("p (c n) -> p c n", c=FC)
                                last = pe.matmul(ps[CAP * par:CAP * (par + 1), 2 + half, :],
                                                 hT[:, c, CAP * par:CAP * (par + 1)],
                                                 w[:, c, half * 512:(half + 1) * 512],
                                                 start=(c == 0), stop=(c == FC - 1))
                                if half == 1 and c == FC - 1:
                                    last.then_inc(freed[s], 1)
                    pe.wait_ge(e_gath, 16 * (i + 2))
                    turn_tokens()

            def experts_scalar(act):
                def tokens_out(i):
                    act.wait_ge(e_xgT, i)
                    for k in range(2):
                        act.copy(xgT[:, 4 * k:4 * k + 4, :].rearrange("p c n -> p (c n)"), ps[:, 6 + k, :]).then_inc(e_xT, 1)

                tokens_out(1)
                with act.Fori(0, PAIRS) as i:
                    act.wait_ge(freed[0], i + 1)
                    act.activation(sg, ps[:, 0, :], ACT.Silu).then_inc(e_sg, 1)
                    act.wait_ge(freed[1], i + 1)
                    tokens_out(i + 2)

            def experts_vector(dve):
                with dve.Fori(0, PAIRS) as i:
                    dve.wait_ge(e_sg, i + 1)
                    dve.wait_ge(freed[1], i + 1)
                    dve.tensor_tensor(hh, sg, ps[:, 1, :], ALU.mult).then_inc(e_h, 1)
                    dve.wait_ge(e_hT, i + 1)
                    dve.tensor_copy(hT.rearrange("p c n -> p (c n)"), ps[:, 4, :]).then_inc(e_hTe, 1)
                    dve.wait_ge(freed[2], i + 1)
                    dve.wait_ge(e_st, i + 1)
                    for half in range(2):
                        dve.tensor_scalar(ysb[:, half * 512:(half + 1) * 512], ps[:, 2 + half, :], gcol[:, 0:1], None,
                                          ALU.mult).then_inc(e_y, 1)

            def blank_tokens(pool):
                pool.memset(xg, 0.0).then_inc(e_blank, 1)
                pool.wait_ge(e_blank, 1)

            def load_table(pool, rows):
                pool.dma_start(tabs[:, 0:PAIRS, :].rearrange("p m c -> p (m c)"), rows).then_inc(s_tabl, 16)
                pool.wait_ge(s_tabl, 16)

            with nc.Block() as block:
                @block.sync
                def _(sp):
                    w3 = w_in[bass.ds(l, 1)].rearrange("a (p c) n -> p (a c) n", p=P)
                    wo_a = L(w_o_swa).rearrange("a (c p) n -> p (a c) n", p=P)
                    wo_b = L(w_o_fox).rearrange("a (c p) n -> p (a c) n", p=P)
                    wo = L(w_out).rearrange("a (c p) n -> p (a c) n", p=P)

                    def view(s, c):
                        return wslot[s][:, :].rearrange("p (c n) -> p c n", c=c)

                    def load_y(i):
                        for a in range(2):
                            at = (a * TILES + i) * P
                            sp.dma_start(y_tile(i, a), y_dram[at:at + ROWS[i], :]).then_inc(y_in[i], 16)

                    with sp.If(l > 0):
                        load_y(0)
                    sp.dma_start(gainb[:, :], L(norm1_g).broadcast_to((P, D))).then_inc(s_g1, 16)
                    kvf = wslot[0][:, 0:KC * 264].rearrange("p (c n) -> p c n", c=KC)
                    with sp.If(l > 0):
                        load_y(1)
                        load_y(2)
                    sp.dma_start(kvf[:, :, 0:256], w3[:, :, W_KV:W_QB]).then_inc(w_qkv[0], 16)
                    sp.dma_start(kvf[:, :, 256:264], w3[:, :, W_F:W_G]).then_inc(w_f, 16)
                    with sp.If(l > 0):
                        for i in range(3, TILES):
                            load_y(i)
                    for c, at in ((1, 0), (2, W_QB), (3, W_KB), (4, W_VB)):
                        if c == 4:
                            sp.wait_ge(s_h, TILES)
                        sp.dma_start(view(c, KC), w3[:, :, at:at + 512]).then_inc(w_qkv[c], 16)
                    sp.dma_start(view(5, 4), wo_a).then_inc(w_oa, 16)
                    sp.wait_ge(s_xn, TILES)
                    sp.dma_start(gainb[:, :], L(norm2_g).broadcast_to((P, D))).then_inc(s_g2, 16)
                    for n in range(4):
                        s = n + 1
                        sp.wait_ge(s_prj, TILES * (s + 1))
                        for br in range(2):
                            dst = wslot[s][:, :].rearrange("p (c b n) -> p c b n", c=KC, b=2)
                            at = W_G + br * D + n * 256
                            sp.dma_start(dst[:, :, br, :], w3[:, :, at:at + 256]).then_inc(w_gates[n][br], 16)
                    sp.wait_ge(s_z, 16)
                    sp.dma_start(view(2, 4), wo_b).then_inc(w_ob, 16)
                    sp.wait_ge(s_z, 24)
                    sp.dma_start(view(3, 4), wo[:, 0:4, :]).then_inc(w_o[0], 16)
                    sp.wait_ge(s_sig, 16)
                    sp.dma_start(view(0, 4), wo[:, 4:8, :]).then_inc(w_o[1], 16)
                    free = {1: (s_sig, EARLY), 4: (s_gate, 4 * KC - EARLY), 5: (s_y, 2 * KC), 2: (s_y, 2 * KC),
                            3: (s_wo, 2 * NT + 1), 0: (s_wo, 2 * NT + 1)}
                    for s in (1, 4, 5, 2, None, 3, 0):
                        if s is None:
                            for k in range(TILES):
                                sp.wait_ge(s_xn, TILES + k + 1)
                                sp.dma_start(t_dram[P * k:P * k + ROWS[k], :], xn[k][0:ROWS[k], :]).then_inc(s_tst, 16)
                            continue
                        w, par, _ = next(o for o in ORDER if o[2] == s)
                        sp.wait_ge(*free[s])
                        load_expert(sp, w, slice(par, par + 1), s)
                    experts_sync(sp)

                @block.gpsimd
                def _(pool):
                    own = Own(pool, p_own)
                    with nc.allow_non_contiguous_dma("small parameters"):
                        pool.dma_start(hgain[:, :, :].rearrange("p k n -> p (k n)"),
                                       L(qk_gain).rearrange("a k n -> a (k n)").broadcast_to((P, 4 * HD))).then_inc(s_par, 16)
                        pool.dma_start(sinks[:, :], L(attn_sinks).broadcast_to((P, HEADS))).then_inc(s_par, 16)
                        pool.dma_start(fbias[:, :], L(b_forget).broadcast_to((P, HEADS))).then_inc(s_par, 16)
                        pool.dma_start(gbias_rows[:, :], L(b_merge).rearrange("a (k p) -> (a k) p", p=P)).then_inc(s_par, 16)

                    def router_parameters():
                        with nc.allow_non_contiguous_dma("small parameters"):
                            pool.dma_start(rbias[:, 0:GROUPS], L(b_router_group).broadcast_to((P, GROUPS))).then_inc(s_rpar, 16)
                            pool.dma_start(rbias[:, GROUPS:], L(b_router_expert).broadcast_to((P, EXPERTS))).then_inc(s_rpar, 16)
                            pool.dma_start(wr[:, :, 0:GROUPS],
                                           L(w_router_group).rearrange("a (p c) n -> p (a c) n", p=P)).then_inc(s_rpar, 16)
                            pool.dma_start(wr[:, :, GROUPS:],
                                           L(w_router_expert).rearrange("a (p c) n -> p (a c) n", p=P)).then_inc(s_rpar, 16)

                    def blank_table():
                        pool.memset(blank, NOWHERE).then_inc(s_tab0, 1)
                        pool.wait_ge(s_tab0, 1)
                        pool.dma_start(tab_dram.rearrange("(p r) c -> p (r c)", p=P), blank).then_inc(s_blank, 16)

                    def rsqrt_of_mean(dst, src, n):
                        own.link(pool.tensor_scalar(dst, src, 1.0 / n, EPS, ALU.mult, ALU.add))
                        return pool.tensor_tensor(dst, dst, halfneg[0:dst.shape[0], 0:dst.shape[1]], ALU.pow)

                    def norms(q):
                        for k in range(TILES):
                            r = ROWS[k]
                            pool.wait_ge(s_ss, TILES * q + k + 1)
                            rsqrt_of_mean(rstd[0:r, k:k + 1], ss[0:r, k:k + 1], D).then_inc(s_rstd, 1)

                    norms(0)
                    for u in range(4 * TILES):
                        c, i = divmod(u, TILES)
                        r, n = proj_shape(c, i)
                        if u == TILES:
                            router_parameters()
                        if u == 2 * TILES:
                            blank_table()
                        if u == 3 * TILES:
                            pool.wait_ge(s_blank, 16)
                        pool.wait_ge(s_hss, u + 1)
                        rsqrt_of_mean(hr[0:r, 0:n], hss[0:r, 0:n], HD).then_inc(s_hr, 1)
                    norms(1)
                    pool.wait_ge(s_wo, 2 * NT + 1)
                    blank_tokens(pool)

                    def fill_table():
                        pool.wait_ge(s_ent, 1)
                        for b in range(BOTH):
                            r = ROWS[b % TILES]
                            pool.indirect_dma_start(
                                out=tab_dram, out_offset=bass.IndirectOffsetOnAxis(ap=slot_at[0:r, b:b + 1], axis=0),
                                in_=ent[0:r, b, :], in_offset=None, bounds_check=TAB - 1,
                                oob_is_err=False).then_inc(s_scat, 16)
                        pool.wait_ge(s_scat, 16 * BOTH)

                    pool.wait_ge(s_tabl, 3)
                    pool.wait_ge(s_tst, 16 * TILES)
                    experts_pool(pool, fill_table)

                @block.scalar
                def _(act):
                    def square(q, k):
                        r = ROWS[k]
                        if q == 0:
                            act.wait_ge(s_h, k + 1)
                        else:
                            act.wait_ge(s_res, res_upto(k))
                        if k:
                            act.wait_ge(s_ss, TILES * q + k)
                        act.activation(xsq[0:r, :], h[0:r, k, :], ACT.Square, accum_out=ss[0:r, k:k + 1]).then_inc(s_ss, 1)

                    def turned_out(q):
                        for k in range(TILES):
                            r = ROWS[k]
                            if k == 0 or q == 1:
                                square(q, k)
                            if k + 1 < TILES and q == 0:
                                square(q, k + 1)
                            for half in range(2):
                                act.wait_ge(s_tp, 2 * (TILES * q + k) + half + 1)
                                src = ps[:, 2 * q + half, :].rearrange("p (c n) -> p c n", c=4)[:, :, 0:r]
                                act.copy(xT[:, 4 * half:4 * half + 4, COL[k]:COL[k] + r], src).then_inc(s_xT, 1)

                    turned_out(0)

                    def head_out(u):
                        c, i = divmod(u, TILES)
                        r = ROWS[i]
                        dst = (kaT, qaT, qbT, kbT)[c]
                        n = KV if c == 0 else 4
                        act.wait_ge(s_qT, u + 1)
                        width = 4 * PACK if packed(c, i) else 512
                        src = ps[:, u % 2, 0:width].rearrange("p (c n) -> p c n", c=4)[:, 0:n, 0:r]
                        act.copy(dst[:, 0:n, COL[i]:COL[i] + r], src).then_inc(s_qTe, 1)

                    for u in range(4 * TILES):
                        c, i = divmod(u, TILES)
                        r, nh = proj_shape(c, i)
                        n = nh * HD
                        act.wait_ge(s_prj, u + 1)
                        if u >= 1:
                            act.wait_ge(s_hss, u)
                        act.activation(sq[0:r, 0:n], ps[0:r, 2 + u % 3, 0:n], ACT.Square).then_inc(s_sq, 1)
                        if u == TILES:
                            act.wait_ge(s_fz, 1)
                            act.activation(frg[:, 2], frg[:, 1], ACT.Exp, scale=-1.0).then_inc(s_fe, 1)
                            act.wait_ge(s_fe, 1)
                            act.activation(frg[:, 3], frg[:, 2], ACT.Ln, bias=1.0).then_inc(s_fe, 1)
                        if u >= 2:
                            head_out(u - 2)
                    head_out(4 * TILES - 2)
                    head_out(4 * TILES - 1)
                    act.wait_ge(s_gb, 1)
                    act.copy(gbias[:, :], ps[:, 7, 0:2 * KC]).then_inc(s_gbe, 1)

                    def turn_out(n):
                        t = turns[n]
                        b = n % 2
                        act.wait_ge(s_T, n + 1)
                        evacuate(act, act.copy, n).then_inc(s_Te[b], 1)

                    for v, st in enumerate(steps):
                        if st["sinks"] is not None and units[st["sinks"]][1] == 0:
                            n = block_of(st["sinks"]) // 2
                            j = units[st["sinks"]][0]
                            act.wait_ge(s_skin, n + 1)
                            act.activation(esk[0:ROWS[j], :], den[0:ROWS[j], :], ACT.Exp).then_inc(s_esk, 1)
                        if st["score"] is not None:
                            j, br, hd = units[v]
                            r = ROWS[j]
                            act.wait_ge(s_nm, v + 1)
                            if prob_before(v) is not None:
                                act.wait_ge(s_T, last_turn[prob_before(v)] + 1)
                            act.activation(prob_out(v), score_in(v), ACT.Exp, bias=nm[0:r, v:v + 1],
                                           accum_out=rs[0:r, v:v + 1]).then_inc(s_P, 1)
                        for n in st["turn"] + ([st["oturn"]] if st["oturn"] is not None else []):
                            if n % 2:
                                turn_out(n)
                        if st["fill_out"] is not None and st["fill_out"] % 2 == 0:
                            fill_out(act, act.copy, st["fill_out"])

                    for w in range(2 * KC):
                        n = w // 2
                        if 2 * w < EARLY:
                            for k in range(2):
                                act.wait_ge(s_zo[k], w + 1)
                        else:
                            act.wait_ge(s_gate, 2 * (w + 1) - EARLY)
                        if w >= 2:
                            act.wait_ge(s_mrg, w - 1)
                        for br in range(2):
                            z = z_at(2 * w + br) if 2 * w < EARLY else ps[:, 4 * (w % 2) + br, 0:HALF]
                            act.activation(sig2(w, br), z, ACT.Sigmoid,
                                           bias=gbias[:, br * KC + n:br * KC + n + 1]).then_inc(s_sig, 1)
                    turned_out(1)
                    act.wait_ge(s_exl, 1)
                    act.activation(r_dg, r_dg, ACT.Exp).then_inc(s_exd, 1)
                    act.wait_ge(s_exl, 2)
                    act.activation(r_d, r_d, ACT.Exp).then_inc(s_exd, 1)
                    experts_scalar(act)

                @block.tensor
                def _(pe):
                    def turn_norm(q, k):
                        r = ROWS[k]
                        pe.wait_ge(s_xn, TILES * q + k + 1)
                        for half in range(2):
                            n = 2 * k + half
                            if n >= 2:
                                pe.wait_ge(s_xT, 2 * TILES * q + n - 1)
                            for c in range(4):
                                last = pe.transpose(ps[:, 2 * q + half, c * P:c * P + r],
                                                    xn[k][0:r, 4 * half + c::KC], ident[0:r, 0:r])
                            last.then_inc(s_tp, 1)

                    def turn_heads(u):
                        c, i = divmod(u, TILES)
                        r = ROWS[i]
                        pe.wait_ge(s_qn, u + 1)
                        if u >= 2:
                            pe.wait_ge(s_qTe, u - 1)
                        if packed(c, i):
                            pe.transpose(ps[:, u % 2, 0:P], qnb[:, u % 2, 0:P], ident).then_inc(s_qT, 1)
                            return
                        for k in range(KV if c == 0 else 4):
                            last = pe.transpose(ps[:, u % 2, k * P:k * P + r], qnb[0:r, u % 2, k * P:(k + 1) * P],
                                                ident[0:r, 0:r])
                        last.then_inc(s_qT, 1)

                    def quarters(dst, tokens, w, k):
                        n = w.shape[-1] // QUARTERS
                        for g in range(QUARTERS):
                            last = pe.matmul(dst[PACK * g:PACK * (g + 1), :], tokens, w[:, n * g:n * (g + 1)],
                                             start=(k == 0), stop=(k == KC - 1))
                        return last

                    def project(c, i):
                        u = c * TILES + i
                        r, n = ROWS[i], (264 if c == 0 else 512)
                        w = wslot[c][:, 0:KC * n].rearrange("p (c n) -> p c n", c=KC)
                        if i == 0:
                            pe.wait_ge(w_qkv[c], 16)
                            if c == 0:
                                pe.wait_ge(w_f, 16)
                        pe.wait_ge(s_xT, 2 * TILES if c else 2 * (i + 1))
                        if u >= 3:
                            pe.wait_ge(s_prjfree, u - 2)
                        for k in range(KC):
                            if packed(c, i):
                                last = quarters(ps[:, 2 + u % 3, 0:P], xT[:, k, 0:PACK], w[:, k, :], k)
                            else:
                                last = pe.matmul(ps[0:r, 2 + u % 3, 0:n], xT[:, k, COL[i]:COL[i] + r], w[:, k, :],
                                                 start=(k == 0), stop=(k == KC - 1))
                        last.then_inc(s_prj, 1)

                    turn_norm(0, 0)
                    for k in range(1, TILES):
                        turn_norm(0, k)
                        if k - 1 < 3:
                            project(0, k - 1)
                    for u in range(3, CHUNKS * TILES):
                        project(u // TILES, u % TILES)
                        if u - 3 < 4 * TILES:
                            turn_heads(u - 3)
                    pe.wait_ge(s_lf, 1)
                    lf = frg[:, 0]
                    cps = ps[:, 5, 0:TILES * HEADS].rearrange("p (t n) -> p t n", t=TILES)
                    pe.matmul(cps[0:META, NT, :], upto[0:META, 0:META], lf[0:META, NT, :], start=True, stop=True)
                    for j in range(NT):
                        pe.matmul(cps[:, j, :], ones[0:META, :], lf[0:META, NT, :], start=True, stop=False)
                        for i in range(j):
                            pe.matmul(cps[:, j, :], ones, lf[:, i, :], start=False, stop=False)
                        last = pe.matmul(cps[:, j, :], upto, lf[:, j, :], start=False, stop=True)
                    last.then_inc(s_c, 1)
                    pe.wait_ge(s_par, 16 * 4)
                    pe.transpose(ps[:, 7, 0:2 * KC], gbias_rows[:, :], ident[0:2 * KC, 0:2 * KC]).then_inc(s_gb, 1)
                    pe.wait_ge(s_ce, 1)
                    cp24 = cpart[:, :, :, :].rearrange("p t k n -> p t (k n)")
                    for j in range(NT):
                        pe.transpose(ps[0:3 * HEADS, 6, j * P:(j + 1) * P], cp24[:, j, :], ident)
                    pe.transpose(ps[0:3 * HEADS, 5, 64:64 + META], cp24[0:META, NT, :], ident[0:META, 0:META]).then_inc(s_c, 1)
                    pe.wait_ge(s_ce, 2)
                    pe.wait_ge(s_qTe, 4 * TILES)
                    pe.wait_ge(s_prjfree, CHUNKS * TILES)
                    pe.wait_ge(s_gbe, 1)

                    def score(v):
                        j, br, hd = units[v]
                        r = ROWS[j]
                        if v >= 2:
                            pe.wait_ge(s_P, v - 1)
                        part = slice(HD * (hd % 2), HD * (hd % 2) + HD)
                        b = 2 + 2 * (v % 2)
                        if br == 0:
                            q = qaT[part, hd // 2, COL[j]:COL[j] + r]
                            g = hd // (HEADS // KV)
                            if j == NT:
                                return pe.matmul(ps[0:r, b, 0:META], q, kaT[part, g, 0:META], start=True, stop=True)
                            lo_ = COL[j] - CHUNK if j else 0
                            n = COL[j] + P - lo_
                            pe.matmul(ps[:, b, 0:n], q, kaT[part, g, lo_:lo_ + n], start=True, stop=False)
                            return pe.matmul(ps[:, b, 0:n], identb[:, :], windowb[:, CHUNK + P - n:], start=False, stop=True)
                        q = qbT[part, hd // 2, COL[j]:COL[j] + r]
                        k = kbT[part, hd // 2, :]
                        pk = pickb[:, hd:hd + 1].broadcast_to((3 * HEADS, r))
                        pe.matmul(ps[0:r, b, 512 - META:512], q, k[:, 0:META], start=True, stop=False)
                        last = pe.matmul(ps[0:r, b, 512 - META:512], pk, nc3[:, 0:META], start=False, stop=(j != NT))
                        if j == NT:
                            return pe.matmul(ps[0:r, b, 512 - META:512], identb[0:META, 0:META], causalb[0:META, 0:META],
                                             start=False, stop=True)
                        n = (j + 1) * P
                        pe.matmul(ps[:, b + 1, 0:n], q, k[:, META:META + n], start=True, stop=False)
                        pe.matmul(ps[:, b + 1, n - P:n], identb[:, :], causalb[:, :], start=False, stop=False,
                                  skip_group_check=True)
                        return pe.matmul(ps[:, b + 1, 0:n], pk, nc3[:, META:META + n], start=False, stop=True)

                    def turn(n):
                        t = turns[n]
                        b = n % 2
                        if n >= 2:
                            pe.wait_ge(s_Te[b], n // 2)
                        if t["o"] is not None:
                            r = ROWS[units[t["o"]][0]]
                            pe.wait_ge(s_on, block_of(t["o"]) + 1)
                            for c in range(4):
                                last = pe.transpose(ps[:, b, c * P:c * P + r], osb[0:r, c * P:(c + 1) * P], ident[0:r, 0:r])
                            last.then_inc(s_T, 1)
                            return
                        v = t["unit"]
                        r = ROWS[units[v][0]]
                        pe.wait_ge(s_P, v + 1)
                        src = prob(v)
                        for k, (at, n_k, _) in enumerate(t["blocks"]):
                            last = pe.transpose(ps[0:n_k, b, k * P:k * P + r], src[0:r, at:at + n_k], ident[0:r, 0:r])
                        last.then_inc(s_T, 1)

                    def times_v(n):
                        t = turns[n]
                        b = n % 2
                        j, br, hd = units[t["unit"]]
                        r = ROWS[j]
                        pe.wait_ge(s_Te[b], n // 2 + 1)
                        if hd == 0 and t["first"] and block_of(t["unit"]):
                            pe.wait_ge(s_on, block_of(t["unit"]))
                        for k, (_, n_k, tile) in enumerate(t["blocks"]):
                            vv = va[0:n_k, tile, HD * (hd // 4):HD * (hd // 4) + HD] if br == 0 else \
                                vb[0:n_k, tile, HD * hd:HD * (hd + 1)]
                            last = pe.matmul(ps[0:r, 6, HD * hd:HD * (hd + 1)], PT[0:n_k, b, k * P:k * P + r], vv,
                                             start=(t["first"] and k == 0),
                                             stop=(t["last"] and k == len(t["blocks"]) - 1))
                        last.then_inc(s_PV, 1)

                    def gate(g, k, out):
                        n, half, br = g // 4, g // 2 % 2, g % 2
                        s = 1 + n // 2
                        if k == 0 and g % 8 < 2:
                            pe.wait_ge(w_gates[s - 1][br], 16)
                        wg = wslot[s][:, :].rearrange("p (c b n) -> p c b n", c=KC, b=2)
                        return pe.matmul(out, wg[:, k, br, P * (n % 2):P * (n % 2) + P],
                                         xT[:, k, HALF * half:HALF * (half + 1)], start=(k == 0), stop=(k == KC - 1))

                    def fill(todo):
                        for g, k in todo:
                            if k == 0 and g:
                                pe.wait_ge(s_zo[(g - 1) % 2], (g - 1) // 2 + 1)
                            ins = gate(g, k, ps[:, 7, 0:HALF])
                            if k == KC - 1:
                                ins.then_inc(s_z, 1)

                    for v, st in enumerate(steps):
                        if st["score"] is not None:
                            score(v).then_inc(s_S, 1)
                        fill(st["fill"][0])
                        for n in st["pv"]:
                            times_v(n)
                        for n in st["turn"]:
                            turn(n)
                        fill(st["fill"][1])
                        if st["oturn"] is not None:
                            turn(st["oturn"])

                    for b in range(2):
                        pe.wait_ge(s_Te[b], (len(turns) + 1 - b) // 2)
                        pe.wait_ge(s_zo[b], EARLY // 2)
                    pe.wait_ge(w_oa, 16)
                    pe.wait_ge(w_ob, 16)
                    woA = wslot[5][:, :].rearrange("p (c n) -> p c n", c=4)
                    woB = wslot[2][:, :].rearrange("p (c n) -> p c n", c=4)
                    for w in range(2 * KC):
                        n, half = divmod(w, 2)
                        cols = slice(HALF * half, HALF * (half + 1))
                        bank = 4 * (w % 2)
                        if w >= 2:
                            pe.wait_ge(s_mrg, w - 1)
                        for br in range(2 if 2 * w >= EARLY else 0):
                            for k in range(KC):
                                last = gate(2 * w + br, k, ps[:, bank + br, 0:HALF])
                            last.then_inc(s_gate, 1)
                        for br, (wo_, oT) in enumerate(((woA, qaT), (woB, qbT))):
                            for k in range(4):
                                last = pe.matmul(ps[:, bank + 2 + br, 0:HALF], wo_[:, k, n * P:(n + 1) * P],
                                                 oT[:, k, cols], start=(k == 0), stop=(k == 3))
                        last.then_inc(s_y, 1)
                    def routed(k):
                        r = ROWS[k]
                        pe.wait_ge(s_xT, 2 * (TILES + k + 1))
                        for c in range(KC):
                            last = pe.matmul(ps[0:r, 4, 36 * k:36 * (k + 1)], xT[:, c, COL[k]:COL[k] + r], wr[:, c, :],
                                             start=(c == 0), stop=(c == KC - 1))
                        last.then_inc(s_lg, 1)

                    pe.wait_ge(s_rpar, 16 * 4)
                    pe.wait_ge(s_mrg, 2 * KC)
                    for n in range(2):
                        pe.wait_ge(w_o[n], 16)
                    for i in range(TILES):
                        r = ROWS[i]
                        for half in range(1 if i == NT else 2):
                            xu = 2 * i + half
                            if xu >= 2:
                                pe.wait_ge(s_res, xu - 1)
                            for k in range(KC):
                                w = wslot[(3, 0)[k // 4]][:, :].rearrange("p (c n) -> p c n", c=4)[:, k % 4, :]
                                if i == NT:
                                    last = quarters(ps[:, 0, 0:D // QUARTERS], mrgT[:, k, 0:PACK], w, k)
                                else:
                                    last = pe.matmul(ps[0:r, half, :], mrgT[:, k, COL[i]:COL[i] + r],
                                                     w[:, 512 * half:512 * (half + 1)], start=(k == 0),
                                                     stop=(k == KC - 1))
                                if k == KC - 1:
                                    last.then_inc(s_wo, 1)
                                if i and half == 0 and k == (KC // 2 if i == NT else KC - 1):
                                    turn_norm(1, i - 1)
                        if i:
                            routed(i - 1)
                    turn_norm(1, NT)
                    routed(NT)
                    pe.wait_ge(s_M, 1)
                    for i in range(TILES):
                        r = ROWS[i]
                        for k in range(i):
                            pe.matmul(ps[:, 5, 32 * i:32 * (i + 1)], onesb[:, :], Mb[:, k, :], start=(k == 0), stop=False)
                        pe.matmul(ps[:, 5, 32 * i:32 * (i + 1)], beforeb[0:r, :], Mb[0:r, i, :], start=(i == 0), stop=True)
                    for i in range(TILES):
                        r = ROWS[i]
                        last = pe.matmul(ps[:, 5, 160:192], onesb[0:r, :], Mb[0:r, i, :], start=(i == 0), stop=(i == NT))
                    last.then_inc(s_rank, 1)
                    pe.wait_ge(s_put, 2)
                    for q in range(2):
                        for b in range(BOTH):
                            r = ROWS[b % TILES]
                            last = pe.matmul(ps[CAP * q:CAP * (q + 1), 4, 0:3 * PAIRS], in_slot[0:r, b, :],
                                             put_at[0:r, b, q, :, :].rearrange("p v m -> p (v m)"),
                                             start=(b == 0), stop=(b == BOTH - 1))
                    last.then_inc(s_put, 1)
                    experts_tensor(pe)

                @block.vector
                def _(dve):
                    own = Own(dve, d_own)
                    link = own.link

                    def norm(q, k):
                        r = ROWS[k]
                        dve.wait_ge(s_rstd, TILES * q + k + 1)
                        dve.scalar_tensor_tensor(out=xn[k][0:r, :], in0=h[0:r, k, :], scalar=rstd[0:r, k:k + 1],
                                                 in1=gainb[0:r, :], op0=ALU.mult, op1=ALU.mult).then_inc(s_xn, 1)

                    for k in range(TILES):
                        with dve.If(l > 0):
                            dve.wait_ge(y_in[k], 32)
                            for a in range(2):
                                dve.tensor_tensor(h[0:ROWS[k], k, :], h[0:ROWS[k], k, :], y_tile(k, a),
                                                  ALU.add).then_inc(y_add, 1)
                                dve.wait_ge(y_add, 2 * k + a + 1)
                        dve.sem_inc(s_h, 1)
                        if k == 0:
                            dve.wait_ge(s_g1, 16)
                        if k:
                            norm(0, k - 1)
                    norm(0, TILES - 1)
                    dve.wait_ge(s_par, 16 * 4)
                    for k in (0, 2):
                        link(dve.tensor_scalar(hgain[:, k, :], hgain[:, k, :], HD ** -0.5, None, ALU.mult))
                    link(dve.memset(frg[:, :, :, :], 0.0))
                    for u in range(CHUNKS * TILES):
                        c, i = divmod(u, TILES)
                        r, nh = proj_shape(c, i)
                        bank = ps[0:r, 2 + u % 3, :]
                        if c == CHUNKS - 1:
                            dve.wait_ge(s_prj, u + 1)
                            if packed(c, i):
                                for g in range(QUARTERS):
                                    last = dve.tensor_copy(vb[0:META, i, P * g:P * (g + 1)],
                                                           ps[PACK * g:PACK * g + META, 2 + u % 3, 0:P])
                                last.then_inc(s_prjfree, 1)
                                continue
                            dve.tensor_copy(vb[0:r, i, :], bank).then_inc(s_prjfree, 1)
                            continue
                        n = nh * HD
                        dve.wait_ge(s_sq, u + 1)
                        dve.tensor_reduce(hss[0:r, 0:nh], sq[0:r, 0:n].rearrange("p (h d) -> p h d", d=HD), AX,
                                          ALU.add).then_inc(s_hss, 1)
                        if c == 0:
                            dve.tensor_copy(va[0:r, i, :], bank[:, P:2 * P])
                            link(dve.tensor_copy(frg[0:r, 0, i, :], bank[:, 2 * P:2 * P + HEADS]))
                        dve.wait_ge(s_hr, u + 1)
                        y1 = qn1[0:r, 0:n].rearrange("p (h d) -> p h d", d=HD)
                        y2 = qn2[0:r, 0:n].rearrange("p (h d) -> p h d", d=HD)
                        dve.tensor_tensor(y1, bank[:, 0:n].rearrange("p (h d) -> p h d", d=HD),
                                          hr[0:r, 0:nh].unsqueeze(2).broadcast_to((r, nh, HD)), ALU.mult).then_inc(s_prjfree, 1)
                        dve.wait_ge(s_prjfree, u + 1)
                        if u >= 2:
                            dve.wait_ge(s_qT, u - 1)
                        gk = (1, 0, 2, 3)[c]
                        gb = hgain[0:r, gk, :].unsqueeze(1).broadcast_to((r, nh, HD))
                        dst = qnb[0:r, u % 2, 0:max(n, 2 * P)] if c == 0 else qnb[0:r, u % 2, 0:n]
                        if c >= 2:
                            dve.tensor_tensor(dst.rearrange("p (h d) -> p h d", d=HD), y1, gb, ALU.mult).then_inc(s_qn, 1)
                            continue
                        link(dve.tensor_tensor(y2, y1, gb, ALU.mult))
                        link(dve.tensor_tensor(y1, y2, cosv[0:r, i, :].unsqueeze(1).broadcast_to((r, nh, HD)), ALU.mult))
                        sc = rot[0:r, 0:n].rearrange("p (h d) -> p h d", d=HD)
                        for a, b in ((0, 32), (32, 0)):
                            ins = dve.tensor_tensor(sc[:, :, a:a + 32], y2[:, :, b:b + 32],
                                                    sinv[0:r, i, a:a + 32].unsqueeze(1).broadcast_to((r, nh, 32)), ALU.mult)
                            link(ins)
                        if c == 0:
                            d4 = dst[:, 0:256].rearrange("p (h t d) -> p h t d", t=2, d=HD)
                            dve.tensor_tensor(d4, y1.unsqueeze(2).broadcast_to((r, nh, 2, HD)),
                                              sc.unsqueeze(2).broadcast_to((r, nh, 2, HD)), ALU.add).then_inc(s_qn, 1)
                        else:
                            dve.tensor_tensor(dst.rearrange("p (h d) -> p h d", d=HD), y1, sc, ALU.add).then_inc(s_qn, 1)
                        if u == TILES - 1:
                            z, az = frg[:, 0], frg[:, 1]
                            link(dve.tensor_tensor(z, z, fbias[:, :].unsqueeze(1).broadcast_to((P, TILES, HEADS)), ALU.add))
                            link(dve.tensor_scalar(az, z, -1.0, None, ALU.mult))
                            dve.tensor_tensor(az, z, az, ALU.max).then_inc(s_fz, 1)
                            dve.wait_ge(s_fz, 1)
                            link(dve.tensor_scalar(z, z, 0.0, None, ALU.min))
                        if u == TILES:
                            dve.wait_ge(s_fe, 2)
                            dve.tensor_tensor(frg[:, 0], frg[:, 0], frg[:, 3], ALU.subtract).then_inc(s_lf, 1)
                    dve.wait_ge(s_c, 1)
                    cps = ps[:, 5, 0:TILES * HEADS].rearrange("p (t n) -> p t n", t=TILES)
                    link(dve.memset(cso[:, :, :], 0.0))
                    link(dve.tensor_copy(cso[:, 0:NT, :], cps[:, 0:NT, :]))
                    link(dve.tensor_copy(cso[0:META, NT, :], cps[0:META, NT, :]))
                    rest = cso
                    for k in range(3):
                        link(dve.tensor_copy(cpartb[:, :, :], rest[:, :, :]))
                        part = dve.tensor_copy(cpart[:, :, k, :], cpartb[:, :, :])
                        if k == 2:
                            part.then_inc(s_ce, 1)
                            break
                        link(part)
                        link(dve.tensor_tensor(cres[:, :, :], rest[:, :, :], cpart[:, :, k, :], ALU.subtract))
                        rest = cres
                    dve.wait_ge(s_c, 2)
                    dve.tensor_scalar(nc3[:, META:POS], ps[0:3 * HEADS, 6, :], -1.0, None, ALU.mult)
                    dve.tensor_scalar(nc3[:, 0:META], ps[0:3 * HEADS, 5, 64:64 + META], -1.0, None, ALU.mult).then_inc(s_ce, 1)
                    dve.wait_ge(s_qT, 4 * TILES)
                    link(dve.memset(PA[:, :, 0:CHUNK], 0.0))

                    for v, st in enumerate(steps):
                        if st["sinks"] is not None and units[st["sinks"]][1] == 0:
                            u = st["sinks"]
                            r = ROWS[units[u][0]]
                            dve.wait_ge(s_nm, u + 1)
                            dve.tensor_tensor(den[0:r, :], sinks[0:r, :], nm[0:r, u - HEADS + 1:u + 1],
                                              ALU.add).then_inc(s_skin, 1)
                        if st["sums"] is not None:
                            u = st["sums"]
                            r = ROWS[units[u][0]]
                            sums = rs[0:r, u - HEADS + 1:u + 1]
                            dve.wait_ge(s_P, u + 1)
                            if units[u][1] == 0:
                                dve.wait_ge(s_esk, block_of(u) // 2 + 1)
                                link(dve.tensor_tensor(den[0:r, :], esk[0:r, :], sums, ALU.add))
                                sums = den[0:r, :]
                            link(dve.reciprocal(rden[0:r, :], sums))
                        if st["score"] is not None:
                            j, br, hd = units[v]
                            r = ROWS[j]
                            dve.wait_ge(s_S, v + 1)
                            link(dve.tensor_reduce(mx[0:r, v:v + 1], score_in(v), AX, ALU.max))
                            floor = sinks[0:r, hd:hd + 1] if br == 0 else LOWEST
                            dve.tensor_scalar(nm[0:r, v:v + 1], mx[0:r, v:v + 1], floor, -1.0, ALU.max,
                                              ALU.mult).then_inc(s_nm, 1)
                        if st["norm"] is not None:
                            u = st["norm"]
                            j, br, _ = units[u]
                            r = ROWS[j]
                            blk = block_of(u)
                            dve.wait_ge(s_PV, pv_upto(u))
                            if blk >= 1:
                                dve.wait_ge(s_T, oturn_of[blk - 1] + 1)
                            dve.tensor_tensor(osb[0:r, :].rearrange("p (h d) -> p h d", d=HD),
                                              ps[0:r, 6, :].rearrange("p (h d) -> p h d", d=HD),
                                              rden[0:r, :].unsqueeze(2).broadcast_to((r, HEADS, HD)),
                                              ALU.mult).then_inc(s_on, 1)
                        for n in st["turn"] + ([st["oturn"]] if st["oturn"] is not None else []):
                            if n % 2 == 0:
                                dve.wait_ge(s_T, n + 1)
                                evacuate(dve, dve.tensor_copy, n).then_inc(s_Te[0], 1)
                        if st["fill_out"] is not None and st["fill_out"] % 2:
                            fill_out(dve, dve.tensor_copy, st["fill_out"])

                    for w in range(2 * KC):
                        n, half = divmod(w, 2)
                        bank = 4 * (w % 2)
                        dve.wait_ge(s_y, w + 1)
                        dve.wait_ge(s_sig, 2 * w + 2)
                        for br in range(2):
                            ins = dve.tensor_tensor(sig2(w, br), sig2(w, br), ps[:, bank + 2 + br, 0:HALF], ALU.mult)
                            link(ins)
                        dve.tensor_tensor(mrgT[:, n, HALF * half:HALF * (half + 1)], sig2(w, 0), sig2(w, 1),
                                          ALU.add).then_inc(s_mrg, 1)
                    for i in range(TILES):
                        r = ROWS[i]
                        if i == NT:
                            dve.wait_ge(s_wo, 2 * NT + 1)
                            for g in range(QUARTERS):
                                hv = h[0:META, i, D // QUARTERS * g:D // QUARTERS * (g + 1)]
                                dve.tensor_tensor(hv, hv, ps[PACK * g:PACK * g + META, 0, 0:D // QUARTERS],
                                                  ALU.add).then_inc(s_res, 1)
                        for half in range(0 if i == NT else 2):
                            xu = 2 * i + half
                            hv = h[0:r, i, 512 * half:512 * (half + 1)]
                            dve.wait_ge(s_wo, xu + 1)
                            dve.tensor_tensor(hv, hv, ps[0:r, half, :], ALU.add).then_inc(s_res, 1)
                        if i == 0:
                            dve.wait_ge(s_g2, 16)
                        norm(1, i)
                    def b3(a, n):
                        return a.unsqueeze(2).broadcast_to((P, TILES, n))

                    def first_max(src, top, eq, onehot, n):
                        down = C("down")[:, 0:n].unsqueeze(1).broadcast_to((P, TILES, n))
                        link(dve.tensor_reduce(top, src, AX, ALU.max))
                        link(dve.tensor_tensor(eq, src, b3(top, n), ALU.is_equal))
                        link(dve.tensor_tensor(eq, eq, down, ALU.mult))
                        link(dve.tensor_reduce(r_f, eq, AX, ALU.max))
                        link(dve.tensor_tensor(onehot, eq, b3(r_f, n), ALU.is_equal))

                    link(dve.memset(r_lg, 0.0))
                    dve.wait_ge(s_rpar, 16 * 4)
                    dve.wait_ge(s_lg, TILES)
                    lgp = ps[:, 4, 0:36 * TILES].rearrange("p (t n) -> p t n", t=TILES)
                    link(dve.tensor_tensor(r_lg[:, 0:NT, :], lgp[:, 0:NT, :],
                                           rbias[:, :].unsqueeze(1).broadcast_to((P, NT, 36)), ALU.add))
                    link(dve.tensor_tensor(r_lg[0:META, NT, :], lgp[0:META, NT, :], rbias[0:META, :], ALU.add))
                    first_max(r_lg[:, :, 0:GROUPS], r_gm, r_eq, r_og, GROUPS)
                    dve.tensor_tensor(r_dg, r_lg[:, :, 0:GROUPS], b3(r_gm, GROUPS), ALU.subtract).then_inc(s_exl, 1)
                    og4 = r_og.unsqueeze(3).broadcast_to((P, TILES, GROUPS, PER))
                    sel4 = r_sel.rearrange("p t (g e) -> p t g e", g=GROUPS)
                    link(dve.tensor_tensor(sel4, r_lg[:, :, GROUPS:].rearrange("p t (g e) -> p t g e", g=GROUPS), og4,
                                           ALU.mult))
                    link(dve.tensor_reduce(r_ein, r_sel.rearrange("p t (g e) -> p t e g", g=GROUPS), AX, ALU.add))
                    first_max(r_ein, r_v1, r_w, r_o[0], PER)
                    link(dve.scalar_tensor_tensor(out=r_e2, in0=r_o[0], scalar=LOWEST, in1=r_ein, op0=ALU.mult, op1=ALU.add))
                    first_max(r_e2, r_v2, r_w, r_o[1], PER)
                    dve.tensor_tensor(r_d, r_v2, r_v1, ALU.subtract).then_inc(s_exl, 1)
                    for a in range(2):
                        link(dve.tensor_tensor(
                            work_M[:, TILES * a:TILES * (a + 1)].rearrange("p t (g e) -> p t g e", g=GROUPS), og4,
                            r_o[a].unsqueeze(2).broadcast_to((P, TILES, GROUPS, PER)), ALU.mult))
                    dve.tensor_tensor(Mb[:, :, :], work_M[:, 0:TILES], work_M[:, TILES:BOTH], ALU.add).then_inc(s_M, 1)

                    def put(v, value):
                        return dve.tensor_tensor(put_at[:, :, :, v, :],
                                                 work_M[:, :, :].rearrange("p b (m q) -> p b q m", q=2),
                                                 value.unsqueeze(2).unsqueeze(3).broadcast_to((P, BOTH, 2, PAIRS)), ALU.mult)

                    put(0, C("value")[:, 0:BOTH])
                    put(1, C("value")[:, BOTH:2 * BOTH])
                    dve.wait_ge(s_exd, 2)
                    link(dve.tensor_reduce(r_sum, r_dg, AX, ALU.add))
                    link(dve.reciprocal(r_pg, r_sum))
                    link(dve.tensor_scalar(r_den, r_d, 1.0, None, ALU.add))
                    link(dve.reciprocal(r_den, r_den))
                    link(dve.tensor_tensor(r_g[:, 0:TILES], r_den, r_pg, ALU.mult))
                    link(dve.tensor_tensor(r_g[:, TILES:BOTH], r_g[:, 0:TILES], r_d, ALU.mult))
                    put(2, r_g).then_inc(s_put, 1)
                    dve.wait_ge(s_rank, 1)
                    rkp = ps[:, 5, 0:32 * TILES].rearrange("p (t n) -> p t n", t=TILES)
                    for a in range(2):
                        link(dve.tensor_tensor(work_R[:, TILES * a:TILES * (a + 1)], work_M[:, TILES * a:TILES * (a + 1)],
                                               rkp, ALU.mult))
                    link(dve.tensor_reduce(r_rank, work_R, AX, ALU.add))
                    dve.tensor_tensor(in_slot, r_rank.unsqueeze(2).broadcast_to((P, BOTH, CAP)),
                                      C("slots").unsqueeze(1).broadcast_to((P, BOTH, CAP)), ALU.is_equal).then_inc(s_put, 1)
                    link(dve.tensor_tensor(work_R, work_M, C("ebase").unsqueeze(1).broadcast_to((P, BOTH, EXPERTS)),
                                           ALU.mult))
                    link(dve.tensor_reduce(r_at, work_R, AX, ALU.add))
                    dve.wait_ge(s_put, 3)
                    tabp = ps[:, 4, 0:3 * PAIRS].rearrange("p (v m) -> p v m", v=3)
                    for v in range(2):
                        dve.tensor_scalar(tabs[:, 0:PAIRS, v], tabp[:, v, :], float(NOWHERE), None, ALU.add).then_inc(s_tabl, 1)
                    dve.tensor_copy(tabs[:, 0:PAIRS, 2].bitcast(F32), tabp[:, 2, :]).then_inc(s_tabl, 1)
                    link(dve.tensor_copy(r_ri, r_rank))
                    link(dve.tensor_scalar(r_ri, r_ri, 6, None, ALU.arith_shift_right))
                    link(dve.tensor_copy(r_hf, r_ri))
                    link(dve.scalar_tensor_tensor(out=r_slot, in0=r_rank, scalar=float(PAIRS), in1=r_at, op0=ALU.mult,
                                                  op1=ALU.add))
                    link(dve.scalar_tensor_tensor(out=slot_at[:, :], in0=r_hf, scalar=float(CAP * PAIRS), in1=r_slot,
                                                  op0=ALU.mult, op1=ALU.add))
                    for a in range(2):
                        half = slice(TILES * a, TILES * (a + 1))
                        link(dve.tensor_copy(ent[:, half, 0], C("row")))
                        link(dve.tensor_scalar(ent[:, half, 1], C("row"), float(a * TILES * P), None, ALU.add))
                        link(dve.tensor_copy(ent[:, half, 3], C("row")))
                    link(dve.tensor_copy(ent[:, :, 2].bitcast(F32), r_g))
                    link(dve.tensor_reduce(r_cm[0:1, 0:1], ps[0:1, 5, 160:192], AX, ALU.max))
                    link(dve.tensor_scalar(r_ci[0:1, 0:1], r_cm[0:1, 0:1], CAP - 1.0, None, ALU.add))
                    dve.tensor_scalar(cnt[0:1, 0:1], r_ci[0:1, 0:1], 6, None, ALU.arith_shift_right).then_inc(s_ent, 1)
                    experts_vector(dve)

            clear_all()

            rounds = nc.values_load(cnt[0:1, 0:1], min_val=1, max_val=ROUNDS)
            with nc.If(rounds > 1):
                with nc.Fori(1, rounds) as rnd:
                    with nc.Block() as block:
                        @block.sync
                        def _(sp):
                            for w, par, s in ORDER:
                                load_expert(sp, w, slice(par, par + 1), s)
                            experts_sync(sp)

                        @block.gpsimd
                        def _(pool):
                            blank_tokens(pool)
                            load_table(pool, tab_dram.rearrange("(r p m) c -> r p (m c)", p=P, m=PAIRS)[
                                bass.ds(rnd, 1)].rearrange("r p n -> (r p) n"))
                            experts_pool(pool)

                        @block.scalar
                        def _(act):
                            experts_scalar(act)

                        @block.tensor
                        def _(pe):
                            experts_tensor(pe)

                        @block.vector
                        def _(dve):
                            experts_vector(dve)
                    clear_all()

        with nc.Fori(0, DEPTH) as l:
            layer(l)

        with nc.Block() as block:
            @block.sync
            def _(sp):
                for i in range(NT):
                    for a in range(2):
                        at = (a * TILES + i) * P
                        sp.dma_start(y_tile(i, a), y_dram[at:at + P, :]).then_inc(y_in[i], 16)
                for i in range(NT):
                    sp.wait_ge(y_add, 2 * (i + 1))
                    sp.dma_start(out[0, i * P:(i + 1) * P, :], h[:, i, :]).then_inc(s_out, 16)
                sp.wait_ge(s_out, 16 * NT)

            @block.vector
            def _(dve):
                for i in range(NT):
                    dve.wait_ge(y_in[i], 32)
                    for a in range(2):
                        dve.tensor_tensor(h[:, i, :], h[:, i, :], y_tile(i, a), ALU.add).then_inc(y_add, 1)
                        dve.wait_ge(y_add, 2 * i + a + 1)


INPUTS = ["x", "meta_tokens", "norm1_g", "w_in", "qk_gain", "attn_sinks", "b_forget", "b_merge", "w_o_swa", "w_o_fox",
          "w_out", "norm2_g", "w_router_group", "b_router_group", "w_router_expert", "b_router_expert", "w_exp_gate",
          "w_exp_up", "w_exp_down"]


def kernel(**inputs):
    import concourse.bacc as bacc
    from concourse.bass_utils import run_bass_kernel_spmd

    nc = bacc.Bacc("TRN2", target_bir_lowering=False, num_devices=1)
    arrays = {f"in_{name}": np.ascontiguousarray(inputs[name]) for name in INPUTS}
    arrays["in_constants"] = constants()
    args = [nc.dram_tensor(name, a.shape, F32, kind="ExternalInput").ap() for name, a in arrays.items()]
    out = nc.dram_tensor("out_0", (1, SEQ, D), F32, kind="ExternalOutput").ap()
    trunk_kernel(nc, *args, out)
    result = run_bass_kernel_spmd(nc, [arrays], core_ids=[0])
    return result.results[0]["out_0"]
```
